# Optimizing a Trainium2 kernel written in Bass

```python
import math, functools
import jax, jax.numpy as jnp
from jax import lax
import numpy as np

D_MODEL = 1024
BATCH = 1
SEQ = 512
DEPTH = 1
DEC_BATCH = 8
DEC_SEQ = 4
PAST_LEN = 256
PAGE_SIZE = 128

D_RNN = D_MODEL
RNN_BLOCKS = 16
RNN_BLOCK_W = D_RNN // RNN_BLOCKS
CONV_W = 4
LRU_C = 8.0
N_HEADS = 8
HEAD_DIM = 64
ATT_W = N_HEADS * HEAD_DIM
IDX_HEADS = 8
IDX_DIM = 64
TOPK_MAX = 256
QBLOCK = 128
N_BUCKETS = 32
MAX_DISTANCE = 128
D_FF = ((-(-8 * D_MODEL // 3) + 255) // 256) * 256
P_DIM = 256
EPS = 1e-6
IN_WIDTHS = (D_RNN, D_RNN, ATT_W, ATT_W, ATT_W, IDX_HEADS * IDX_DIM, IDX_DIM, IDX_HEADS, D_MODEL, D_MODEL)
D_IN = sum(IN_WIDTHS)

kernel_name = 'hybrid_rglru_dsa_decoder_step'

def _split_points():
    return np.cumsum(np.array(IN_WIDTHS))[:-1].tolist()

def _rmsnorm(x, g):
    xf = x.astype(jnp.float32)
    y = xf * lax.rsqrt(jnp.mean(xf * xf, axis=-1, keepdims=True) + EPS)
    return (y * g.astype(jnp.float32)).astype(x.dtype)

def _causal_conv(x, buf, w, b):
    T = x.shape[1]
    xx = jnp.concatenate([buf.astype(x.dtype), x], axis=1)
    y = b + sum(xx[:, j:j + T] * w[j] for j in range(CONV_W))
    return y, xx[:, T:]

def _rg_lru(x, h0, w_a, b_a, w_x, b_x, lam):
    B, T, _ = x.shape
    xf = x.astype(jnp.float32)
    xb = xf.reshape(B, T, RNN_BLOCKS, RNN_BLOCK_W)
    r = jax.nn.sigmoid(jnp.einsum('btnc,ncd->btnd', xb, w_a.astype(jnp.float32)).reshape(B, T, D_RNN) + b_a.astype(jnp.float32))
    i = jax.nn.sigmoid(jnp.einsum('btnc,ncd->btnd', xb, w_x.astype(jnp.float32)).reshape(B, T, D_RNN) + b_x.astype(jnp.float32))
    log_a = LRU_C * r * jax.nn.log_sigmoid(lam.astype(jnp.float32))
    a = jnp.exp(log_a)
    u = jnp.sqrt(-jnp.expm1(2.0 * log_a)) * (i * xf)

    def step(h, au):
        h = au[0] * h + au[1]
        return h, h

    h_last, hs = lax.scan(step, h0.astype(jnp.float32), (a.swapaxes(0, 1), u.swapaxes(0, 1)))
    return hs.swapaxes(0, 1).astype(x.dtype), h_last

def _rel_bucket(n):
    max_exact = N_BUCKETS // 2
    nf = jnp.maximum(n, 1).astype(jnp.float32)
    large = max_exact + (jnp.log(nf / max_exact) / math.log(MAX_DISTANCE / max_exact) * (N_BUCKETS - max_exact)).astype(jnp.int32)
    large = jnp.minimum(large, N_BUCKETS - 1)
    return jnp.where(n < max_exact, n, large)

def _index_select(iq, iw, ik, q_pos, k_top):
    dots = jnp.einsum('bthd,bsd->bths', iq, ik).astype(jnp.float32) * IDX_DIM ** -0.5
    score = jnp.einsum('bths,bth->bts', jax.nn.relu(dots), iw.astype(jnp.float32))
    L = ik.shape[1]
    causal = jnp.arange(L, dtype=jnp.int32)[None, :] <= q_pos[:, None]
    score = jnp.where(causal[None], score, -jnp.inf)
    _, sel = lax.top_k(score, k_top)
    valid = sel <= q_pos[None, :, None]
    return sel, valid

def _sparse_attend(q, k_sel, v_sel, sel, valid, q_pos, rel_bias):
    logits = jnp.einsum('bthd,btkhd->bthk', q, k_sel).astype(jnp.float32) * HEAD_DIM ** -0.5
    bucket = _rel_bucket(jnp.maximum(q_pos[None, :, None] - sel, 0))
    bias = rel_bias.astype(jnp.float32)[bucket]
    logits = logits + bias.transpose(0, 1, 3, 2)
    logits = jnp.where(valid[:, :, None, :], logits, -jnp.inf)
    p = jax.nn.softmax(logits, axis=-1)
    return jnp.einsum('bthk,btkhd->bthd', p.astype(v_sel.dtype), v_sel)

def _take_rows(rows, idx):
    return jax.vmap(lambda r, i: r[i])(rows, idx)

def _attend_prompt(q, k, v, iq, ik, iw, *, rel_bias):
    B, T = q.shape[:2]
    k_top = min(TOPK_MAX, T // 4)
    nb = T // QBLOCK

    def to_blocks(a):
        return a.reshape((B, nb, QBLOCK) + a.shape[2:]).swapaxes(0, 1)

    def blk(args):
        qb, iqb, iwb, pos = args
        sel, valid = _index_select(iqb, iwb, ik, pos, k_top)
        return _sparse_attend(qb, _take_rows(k, sel), _take_rows(v, sel), sel, valid, pos, rel_bias)

    pos = jnp.arange(T, dtype=jnp.int32).reshape(nb, QBLOCK)
    out = lax.map(blk, (to_blocks(q), to_blocks(iq), to_blocks(iw), pos))
    return out.swapaxes(0, 1).reshape(q.shape)

def _gather_paged(pool, page_table, sel, new_rows):
    B = sel.shape[0]
    past_len = page_table.shape[1] * PAGE_SIZE
    is_past = sel < past_len
    sp = jnp.minimum(sel, past_len - 1)
    phys = jnp.take_along_axis(page_table, (sp // PAGE_SIZE).reshape(B, -1), axis=1).reshape(sel.shape)
    from_pool = pool[phys, sp % PAGE_SIZE].astype(new_rows.dtype)
    from_new = _take_rows(new_rows, jnp.clip(sel - past_len, 0, new_rows.shape[1] - 1))
    mask = is_past.reshape(is_past.shape + (1,) * (from_pool.ndim - 3))
    return jnp.where(mask, from_pool, from_new)

def _attend_sample(q, k, v, iq, ik, iw, *, rel_bias, k_pool, v_pool, ik_pool, page_table):
    B, T = q.shape[:2]
    past_len = page_table.shape[1] * PAGE_SIZE
    k_top = min(TOPK_MAX, (past_len + T) // 4)
    ik_past = ik_pool[page_table].reshape(B, past_len, IDX_DIM).astype(ik.dtype)
    ik_all = jnp.concatenate([ik_past, ik], axis=1)
    pos = past_len + jnp.arange(T, dtype=jnp.int32)
    sel, valid = _index_select(iq, iw, ik_all, pos, k_top)
    k_sel = _gather_paged(k_pool, page_table, sel, k)
    v_sel = _gather_paged(v_pool, page_table, sel, v)
    return _sparse_attend(q, k_sel, v_sel, sel, valid, pos, rel_bias)

def _layer(x, p_l, conv_buf, h0, attend, lw):
    (norm_mix, w_in, conv_w, conv_b, w_rg_a, b_rg_a, w_rg_x, b_rg_x, lam,
     w_rnn_out, w_att_out, w_o, norm_ffn, w_ffn_gate, w_ffn_up, w_ffn_down,
     norm_ple, w_ple_gate, w_ple_proj) = lw
    B, T, _ = x.shape
    h = _rmsnorm(x, norm_mix)
    z = h @ w_in
    xr, gr, q, k, v, iq, ik, iw, ga, gb = jnp.split(z, _split_points(), axis=-1)
    xc, new_buf = _causal_conv(xr, conv_buf, conv_w, conv_b)
    yr, h_last = _rg_lru(xc, h0, w_rg_a, b_rg_a, w_rg_x, b_rg_x, lam)
    branch_a = (yr * jax.nn.gelu(gr)) @ w_rnn_out
    q = q.reshape(B, T, N_HEADS, HEAD_DIM)
    k = k.reshape(B, T, N_HEADS, HEAD_DIM)
    v = v.reshape(B, T, N_HEADS, HEAD_DIM)
    iq = iq.reshape(B, T, IDX_HEADS, IDX_DIM)
    iw = iw * IDX_HEADS ** -0.5
    o = attend(q, k, v, iq, ik, iw)
    branch_b = o.reshape(B, T, ATT_W) @ w_att_out
    x = x + (jax.nn.sigmoid(ga) * branch_a + jax.nn.sigmoid(gb) * branch_b) @ w_o
    h2 = _rmsnorm(x, norm_ffn)
    x = x + (jax.nn.silu(h2 @ w_ffn_gate) * (h2 @ w_ffn_up)) @ w_ffn_down
    h3 = _rmsnorm(x, norm_ple)
    x = x + jax.nn.sigmoid(h3 @ w_ple_gate) * (p_l @ w_ple_proj)
    return x, (k, v, ik, h_last, new_buf)

def setup_inputs(seed: int = 0) -> dict:
    key = jax.random.key(seed)
    ks = jax.random.split(key, 32)

    def nrm(i, shape, scale):
        return scale * jax.random.normal(ks[i], shape, jnp.float32)

    n_pages = PAST_LEN // PAGE_SIZE
    n_used = DEC_BATCH * n_pages
    n_pool = (5 * n_used + 3) // 4
    perm = jax.random.permutation(ks[9], n_pool)
    page_table = perm[:n_used].reshape(DEC_BATCH, n_pages).astype(jnp.int32)
    a_pow = jax.random.uniform(ks[19], (DEPTH, D_RNN), jnp.float32, 0.9, 0.999)
    a_base = a_pow ** (1.0 / LRU_C)
    lru_lambda = jnp.log(a_base) - jnp.log1p(-a_base)
    return {
        'x_prompt': nrm(0, (BATCH, SEQ, D_MODEL), 1.0),
        'x_sample': nrm(1, (DEC_BATCH, DEC_SEQ, D_MODEL), 1.0),
        'p_prompt': nrm(2, (DEPTH, BATCH, SEQ, P_DIM), 1.0),
        'p_sample': nrm(3, (DEPTH, DEC_BATCH, DEC_SEQ, P_DIM), 1.0),
        'cache_k': nrm(4, (DEPTH, n_pool, PAGE_SIZE, N_HEADS, HEAD_DIM), 1.0),
        'cache_v': nrm(5, (DEPTH, n_pool, PAGE_SIZE, N_HEADS, HEAD_DIM), 1.0),
        'cache_idx_k': nrm(6, (DEPTH, n_pool, PAGE_SIZE, IDX_DIM), 1.0),
        'state_rglru_h': nrm(7, (DEPTH, DEC_BATCH, D_RNN), 0.5),
        'state_conv': nrm(8, (DEPTH, DEC_BATCH, CONV_W - 1, D_RNN), 1.0),
        'page_table': page_table,
        'rel_bias': nrm(10, (N_BUCKETS, N_HEADS), 0.5),
        'norm_mix': 1.0 + nrm(11, (DEPTH, D_MODEL), 0.05),
        'w_in': nrm(12, (DEPTH, D_MODEL, D_IN), D_MODEL ** -0.5),
        'conv_w': nrm(13, (DEPTH, CONV_W, D_RNN), CONV_W ** -0.5),
        'conv_b': nrm(14, (DEPTH, D_RNN), 0.01),
        'w_rg_a': nrm(15, (DEPTH, RNN_BLOCKS, RNN_BLOCK_W, RNN_BLOCK_W), RNN_BLOCK_W ** -0.5),
        'b_rg_a': nrm(16, (DEPTH, D_RNN), 0.01),
        'w_rg_x': nrm(17, (DEPTH, RNN_BLOCKS, RNN_BLOCK_W, RNN_BLOCK_W), RNN_BLOCK_W ** -0.5),
        'b_rg_x': nrm(18, (DEPTH, D_RNN), 0.01),
        'lru_lambda': lru_lambda,
        'w_rnn_out': nrm(20, (DEPTH, D_RNN, D_MODEL), D_RNN ** -0.5),
        'w_att_out': nrm(21, (DEPTH, ATT_W, D_MODEL), ATT_W ** -0.5),
        'w_o': nrm(22, (DEPTH, D_MODEL, D_MODEL), D_MODEL ** -0.5),
        'norm_ffn': 1.0 + nrm(23, (DEPTH, D_MODEL), 0.05),
        'w_ffn_gate': nrm(24, (DEPTH, D_MODEL, D_FF), D_MODEL ** -0.5),
        'w_ffn_up': nrm(25, (DEPTH, D_MODEL, D_FF), D_MODEL ** -0.5),
        'w_ffn_down': nrm(26, (DEPTH, D_FF, D_MODEL), D_FF ** -0.5),
        'norm_ple': 1.0 + nrm(27, (DEPTH, D_MODEL), 0.05),
        'w_ple_gate': nrm(28, (DEPTH, D_MODEL, D_MODEL), D_MODEL ** -0.5),
        'w_ple_proj': nrm(29, (DEPTH, P_DIM, D_MODEL), P_DIM ** -0.5),
        'norm_final': 1.0 + nrm(30, (D_MODEL,), 0.05),
    }

def reference(x_prompt, x_sample, p_prompt, p_sample, cache_k, cache_v, cache_idx_k,
              state_rglru_h, state_conv, page_table, rel_bias, norm_mix, w_in, conv_w, conv_b,
              w_rg_a, b_rg_a, w_rg_x, b_rg_x, lru_lambda, w_rnn_out, w_att_out, w_o,
              norm_ffn, w_ffn_gate, w_ffn_up, w_ffn_down, norm_ple, w_ple_gate, w_ple_proj,
              norm_final):
    xp, xs = x_prompt, x_sample
    bp = xp.shape[0]
    attend_p = functools.partial(_attend_prompt, rel_bias=rel_bias)
    new_p, new_s = [], []
    for l in range(DEPTH):
        lw = (norm_mix[l], w_in[l], conv_w[l], conv_b[l], w_rg_a[l], b_rg_a[l], w_rg_x[l],
              b_rg_x[l], lru_lambda[l], w_rnn_out[l], w_att_out[l], w_o[l], norm_ffn[l],
              w_ffn_gate[l], w_ffn_up[l], w_ffn_down[l], norm_ple[l], w_ple_gate[l], w_ple_proj[l])
        zero_buf = jnp.zeros((bp, CONV_W - 1, D_RNN), xp.dtype)
        zero_h = jnp.zeros((bp, D_RNN), jnp.float32)
        xp, sp = _layer(xp, p_prompt[l], zero_buf, zero_h, attend_p, lw)
        attend_s = functools.partial(_attend_sample, rel_bias=rel_bias, k_pool=cache_k[l],
                                     v_pool=cache_v[l], ik_pool=cache_idx_k[l], page_table=page_table)
        xs, ss = _layer(xs, p_sample[l], state_conv[l], state_rglru_h[l], attend_s, lw)
        new_p.append(sp)
        new_s.append(ss)
    y_prompt = _rmsnorm(xp, norm_final)
    y_sample = _rmsnorm(xs, norm_final)
    k_prompt = jnp.stack([s[0] for s in new_p])
    v_prompt = jnp.stack([s[1] for s in new_p])
    idx_k_prompt = jnp.stack([s[2] for s in new_p])
    h_prompt = jnp.stack([s[3] for s in new_p])
    conv_prompt = jnp.stack([s[4] for s in new_p])
    k_sample = jnp.stack([s[0] for s in new_s])
    v_sample = jnp.stack([s[1] for s in new_s])
    idx_k_sample = jnp.stack([s[2] for s in new_s])
    h_sample = jnp.stack([s[3] for s in new_s])
    conv_sample = jnp.stack([s[4] for s in new_s])
    return (y_prompt, y_sample, k_prompt, v_prompt, idx_k_prompt, h_prompt, conv_prompt,
            k_sample, v_sample, idx_k_sample, h_sample, conv_sample)


_drawn_inputs = setup_inputs


def setup_inputs(seed=0):
    import zlib

    import numpy as np

    out = dict(_drawn_inputs(seed))
    spreads = {}
    factors = {'b_rg_a': 24.417, 'b_rg_x': 8.0, 'norm_ple': 7.714}
    for name, (base, spread) in spreads.items():
        noise = np.random.default_rng([zlib.crc32(name.encode()), seed]).standard_normal(out[name].shape)
        drawn = base * np.exp(spread * noise) if base else spread * noise
        out[name] = __import__('jax').numpy.asarray(drawn.astype(out[name].dtype))
    for name, factor in factors.items():
        out[name] = (out[name] * factor).astype(out[name].dtype)
    return out
```

```python
from contextlib import ExitStack

import numpy as np

import concourse.bass as bass
from concourse import mybir

F32 = mybir.dt.float32
F32R = mybir.dt.float32r
I32 = mybir.dt.int32
ALU = mybir.AluOpType
ACT = mybir.ActivationFunctionType

P = 128
D = 1024
DC = D // P
SEQ = 512
NB = 8
NJ = 4
NS = NB * NJ
T = SEQ + NS
HT = T // 2
TT = SEQ // P
NH = 8
HD = 64
ATT = NH * HD
HP = NH // 2
PG = 128
NPG = 2
PAST = NPG * PG
SK = PAST + NS
DFF = 2816
FC = DFF // P
PD = 256
EPS = 1e-6
TOPK_P = SEQ // 4
TOPK_S = (PAST + NJ) // 4
NBUCK = 32
LW = 640
LMAX = 511
MASKED = -3.0e38
TAKEN = -3.4e38
TAKEN_BELOW = -3.3e38
PAD = -3.2e38
OFF = -1.0e30
RING = 4
UC = 8
CW = 4
EXT = CW - 1 + SEQ + NB * (CW - 1 + NJ)
EO = EXT - (CW - 1)
EH = EO // 2
S0 = SEQ + CW - 1
ST = CW - 1 + NJ
FA = 12
FFN_HALVES = ((0, FA), (FA, FC - FA))

R_MIX, R_FFN, R_PLE, R_FIN, R_CW, R_CB, R_BA, R_BX, R_LAM, R_SC, R_SH = 0, 1, 2, 3, 4, 8, 9, 10, 11, 12, 36
NR = 44
C_CP, C_CS, C_HP, C_HS, NC = 0, 3, 27, 28, 36

W_AT = dict(xr=0, gr=D, q=2 * D, k=2 * D + ATT, v=2 * D + 2 * ATT, iq=2 * D + 3 * ATT,
            ik=2 * D + 4 * ATT, ga=2 * D + 4 * ATT + HD + NH, gb=3 * D + 4 * ATT + HD + NH)


def plan_tiles():
    def w_in(kind, j, cols=P):
        return (kind, j, [("w_in", 0, DC, W_AT[kind] + P * j, cols, "h", 0)])

    def square(kind, j, weight, operand, chunks=DC):
        return (kind, j, [(weight, 0, chunks, P * j, P, operand, 0)])

    tiles = [w_in("iq", j) for j in range(HP)] + [w_in("ik", 0, HD + NH)]
    for kind in ("q", "k", "v"):
        tiles += [w_in(kind, j) for j in range(HP)]
    for c in range(DC):
        tiles += [w_in("xr", c), w_in("gr", c)]
    for j in range(DC):
        tiles += [w_in("ga", j), square("rnn", j, "w_rnn_out", "y")]
    for j in range(DC):
        tiles += [w_in("gb", j), square("att", j, "w_att_out", "o", HP)]
    tiles += [square("wo", j, "w_o", "m") for j in range(DC)]
    tiles += [square("pp", j, "w_ple_proj", "p", PD // P) for j in range(DC)]
    for f0, fn in FFN_HALVES:
        for f in range(f0, f0 + fn):
            tiles += [square("gate", f, "w_ffn_gate", "h"), square("up", f, "w_ffn_up", "h")]
        half = fn // 2
        for j in range(DC):
            tiles.append(("down", j, [("w_ffn_down", f0 + half * k, half, P * j, P, "f", half * k)
                                      for k in range(2)]))
    tiles += [square("pg", j, "w_ple_gate", "h") for j in range(DC)]
    return tiles


TILES = plan_tiles()
UNITS = [(t, k, u) for t, (_, _, us) in enumerate(TILES) for k, u in enumerate(us)]
FIRST = {}
for _n, (_t, _k, _u) in enumerate(UNITS):
    FIRST.setdefault(TILES[_t][:2] if TILES[_t][0] != "down" else ("down", TILES[_t][1], UNITS[_n][2][1] >= FA), _n)
FIRST_TILE = {}
for _t, (_k, _j, _u) in enumerate(TILES):
    FIRST_TILE.setdefault(_k, _t)
NTH = {}
for _t, (_k, _j, _u) in enumerate(TILES):
    NTH[(_k, _j, _k == "down" and _u[0][1] >= FA)] = _t
LAST_UNIT = {t: n for n, (t, _, _) in enumerate(UNITS)}
STEPS = NH * TT


def plan_aux():
    jobs = ["prm", "xs"] + [("x", c) for c in range(4)] + ["rstd_a", "rstd_b"] + [("x", c) for c in range(4, DC)]
    jobs += [("iks", n) for n in range(4)] + ["lines_a", "lines_b", "selT"]
    jobs += ["ik"] + [("idx", s) for s in range(NH * (TT - 1))] + ["iwcol", "sidx"]
    jobs += [("kout", t) for t in range(TT + 1)]
    for b in range(NB):
        jobs += [("kts", b, 0), ("kts", b, 1)]
    jobs += [("vout", t) for t in range(TT + 1)] + [("smask", 0), ("smask", 1)]
    for c in range(DC):
        jobs += [("gate", c, 0, 0), ("gate", c, 0, 1), ("gate", c, 1, 0), ("gate", c, 1, 1)]
        if c == 0:
            jobs += ["spt", "spn"]
    jobs += ["st_a", "st_b"]
    jobs += [("qk", s) for s in range(STEPS)]
    jobs += [("p", t) for t in range(TT + 1)]
    jobs += ["ss1a", "ss1b", "ss2a", "ss2b", "ss3"]
    for t in range(TT + 1):
        jobs += [("y", t, 0), ("y", t, 1)]
    return jobs


AUX = {name: n for n, name in enumerate(plan_aux())}


def bias_onehot():
    n = np.maximum(LMAX - np.arange(LW), 0)
    exact = NBUCK // 2
    nf = np.maximum(n, 1).astype(np.float32)
    large = exact + (np.log(nf / np.float32(exact)) / np.float32(np.log(128 / exact))
                     * np.float32(NBUCK - exact)).astype(np.int32)
    bucket = np.where(n < exact, n, np.minimum(large, NBUCK - 1))
    return (np.arange(NBUCK)[:, None] == bucket[None, :]).astype(np.float32)


def hybrid_decoder_step(nc, a, o):
    n_pool = a["cache_k"].shape[1]
    free = [16512]
    spot = {}

    def place(name, shape, dt=F32, over=None, plus=0):
        size = 4 * int(np.prod(shape[1:]))
        if over is None:
            spot[name] = free[0]
            free[0] += (size + 31) // 32 * 32
        else:
            spot[name] = spot[over] + plus
        assert spot[name] + size <= 229344, (name, spot[name] + size - 229344)
        return nc.alloc_sbuf_tensor_at(name, shape, dt, offset=spot[name])

    wraw = place("wraw", [P, RING, UC, P])
    whi = place("whi", [P, RING, UC, P], F32R)
    wlo = place("wlo", [P, RING, UC, P], F32R)
    h_hi = place("h_hi", [P, DC, T], F32R)
    h_lo = place("h_lo", [P, DC, T], F32R)
    act_hi = place("act_hi", [P, FA, T], F32R)
    act_lo = place("act_lo", [P, FA, T], F32R)
    x = place("x", [P, DC, T])
    qT = place("qT", [P, HP, T])
    kT = place("kT", [P, HP, T])
    vtok = place("vtok", [P, TT, ATT])
    iqT = place("iqT", [P, HP, T])
    ikw = place("ikw", [P, T])
    ik2 = place("ik2", [P, T])
    score = [None] + [place(f"score{i}", [P, P * (i + 1)]) for i in range(1, TT)]
    score_s = place("score_s", [NS, SK + 8])
    mask0 = place("mask0", [P, P])
    ident = place("ident", [P, P])
    ones = place("ones", [P, P])
    prmT = place("prmT", [P, DC, NR])
    iwtok = place("iwtok", [P, TT + 1, NH])
    vtok_s = place("vtok_s", [NS, ATT])
    lru = place("lru", [P, 8, DC])
    stat = place("stat", [P, 64])
    sstat = place("sstat", [P, 8])
    top8 = place("top8", [P, 8])
    pt = place("pt", [1, NB * NPG], I32)
    hmul = [place(f"hmul{i}", [P, T]) for i in range(2)]
    tail = place("tail", [P, 1120])
    xtok = place("xtok", [P, TT + 1, D], F32, "act_hi")
    rb0 = place("rb0", [P, T], F32, "act_hi", 20480)
    lines = place("lines", [NH, LW], F32, "act_hi", 22656)
    idxp = place("idxp", [P, NB * NPG, 2, HD], F32, "act_lo")
    iks = place("iks", [P, NB, PAST], F32, "act_lo", 8192)
    prm = place("prm", [NR, D], F32, "act_lo", 17408)
    onehot = place("onehot", [NBUCK, LW], F32, "act_lo", 21504)
    relb = place("relb", [NBUCK, NH], F32, "act_lo", 24064)
    junk = place("junk", [P, D], F32, "iqT")
    diag = place("diag", [P, TT + 1, P], F32, "iqT", 4096)
    relu = [place(f"relu{i}", [P, SEQ], F32, "act_lo", 17920 + 2048 * i) for i in range(2)]
    iqbd = place("iqbd", [P, NB, NS], F32, "act_hi")
    rs_s = place("rs_s", [P, 2, SK], F32, "act_hi", 4096)
    sel = place("sel", [NS, 2, P], F32, "act_hi", 6400)
    selT = place("selT", [P, 2, NS], F32, "act_hi", 7424)
    hm = place("hm", [P, NB // 2, NH], F32, "act_hi", 7680)
    iwsc = place("iwsc", [P, NB // 2, NH], F32, "act_hi", 7808)
    iktok = place("iktok", [P, TT + 1, HD + NH], F32, "act_hi", 7936)
    vT = place("vT", [P, HP, T], F32, "x")
    ktok = [place(f"ktok{i}", [P, ATT], F32, "act_lo", 2048 * i) for i in range(2)]
    kpg = [place(f"kpg{i}", [P, NPG, ATT], F32, "act_hi", 17408 + 4096 * i) for i in range(2)]
    kts = [place(f"kts{i}", [P, HP, PAST], F32, "act_lo", 17920 + 4096 * i) for i in range(2)]
    pts = place("pts", [P, NPG, 2, P], F32, "act_lo", 12032)
    ptn = place("ptn", [NS, 2, P], F32, "act_lo", 14080)
    ps_s = place("ps_s", [P, 2, SK], F32, "act_lo", 15104)
    qbd = place("qbd", [P, NB, HP, NS], F32, "act_hi", 13312)
    bias_s = place("bias_s", [P, SK], F32, "ikw")
    bias_n = place("bias_n", [P, NJ], F32, "ikw", 1152)
    bd = place("bd", [P, DC, 2, P], F32, "iqT")
    line = 4 * (EXT + 5)
    xe = [place(f"xe{i}", [P, EXT], F32, "x", line * i) for i in range(2)]
    xc = [place(f"xc{i}", [P, EO], F32, "x", line * (2 + i)) for i in range(2)]
    rq = place("rq", [P, EO], F32, "x", line * 4)
    ig = place("ig", [P, EO], F32, "x", line * 5)
    sq = place("sq", [P, EO], F32, "x", line * 6)
    stO = place("stO", [P, DC, NC], F32, "x", line * 7)
    hs = place("hs", [P, EO], F32, "tail")
    gel = [place(f"gel{i}", [P, T], F32, "tail" if i else "ikw", 2304 if i else 2176) for i in range(2)]
    orow = place("orow", [NC, D], F32, "iqT", 0)
    th = [place(f"th{i}", [P, SEQ], F32, "iqT", 2048 * i) for i in range(2)]
    tm = [place(f"tm{i}", [P, SEQ], F32, "iqT", 4096 + 2048 * i) for i in range(2)]
    pr = [place(f"pr{i}", [P, SEQ], F32, "ikw", 2048 * i) for i in range(2)]
    pT = [place(f"pT{i}", [P, TT, P], F32, "hmul0", 2048 * i) for i in range(2)]
    sg = [place(f"sg{i}", [P, T], F32, "tail", 2176 * i) for i in range(2)]
    p_hi = place("p_hi", [P, PD // P, T], F32R, "vtok")
    p_lo = place("p_lo", [P, PD // P, T], F32R, "ikw")
    ptok = place("ptok", [P, TT + 1, PD], F32, "qT")
    pp = place("pp", [P, DC, T], F32, "qT")
    sqacc = place("sqacc", [P, T], F32, "iqT")
    sqt = [place(f"sqt{i}", [P, T], F32, "iqT", 2176 * (1 + i)) for i in range(2)]
    rb = place("rb", [P, T], F32, "iqT", 2176 * 3)
    ytok = place("ytok", [P, TT + 1, D], F32, "h_hi")

    psD = nc.alloc_psum_tensor("psD", [P, 4, 512], F32)
    psX = [nc.alloc_psum_tensor(f"psX{i}", [P, 512], F32)[:] for i in range(4)]

    lines_d = nc.dram_tensor("bias_lines", [NH, P, LW], F32, kind="Internal").ap()
    x_d = nc.dram_tensor("x_saved", [P, DC * T], F32, kind="Internal").ap()

    ctx = ExitStack()
    with ctx:
        def sem(name):
            return ctx.enter_context(nc.semaphore(name))

        def sems(name, n):
            return [sem(f"{name}{i}") for i in range(n)]

        w_loaded = sems("w_loaded", RING)
        w_hi, w_lo, w_used = sem("w_hi"), sem("w_lo"), sem("w_used")
        tile_read = sems("tile_read", 2)
        aux_done, aux_read = sem("aux_done"), sems("aux_read", 2)
        x_in, prm_in, page_in, idxp_in = sems("x_in", TT + 1), sem("prm_in"), sem("page_in"), sem("idxp_in")
        small_in, bd_in, bias_in = sem("small_in"), sem("bd_in"), sem("bias_in")
        kpg_in, th_in, p_in, x_back = sems("kpg_in", 2), sems("th_in", 2), sem("p_in"), sem("x_back")
        ik_dup, lines_saved, x_saved = sem("ik_dup"), sem("lines_saved"), sem("x_kept")
        out_done, ktok_out = sem("out_done"), sems("ktok_out", 2)
        ident_ok, ones_ok, pool_const = sem("ident_ok"), sem("ones_ok"), sem("pool_const")
        dve_step, pool_step, act_step = sem("dve_step"), sem("pool_step"), sem("act_step")
        sq_done, rstd_v, rstd_a, diag_ok = sem("sq_done"), sem("rstd_v"), sem("rstd_a"), sem("diag_ok")
        n_t, n_hi, n_lo_v, n_lo_p = sem("n_t"), sem("n_hi"), sem("n_lo_v"), sem("n_lo_p")
        xn_ok, sq_ok, sqacc_ok, rb_v, rb_a = sem("xn_ok"), sem("sq_ok"), sem("sqacc_ok"), sem("rb_v"), sem("rb_a")
        idx_acc, iqbd_ok, iwcol_ok, sdots = sem("idx_acc"), sem("iqbd_ok"), sem("iwcol_ok"), sem("sdots")
        rs_ok, ss_copied, masked_in = sem("rs_ok"), sem("ss_copied"), sem("masked_in")
        topk_ok, mask_ok = sem("topk_ok"), sem("mask_ok")
        qbd_ok, slogit_b, sexp_ok, sp_ok = sem("qbd_ok"), sem("slogit_b"), sem("sexp_ok"), sem("sp_ok")
        spv_b, so_hi, so_lo = sem("spv_b"), sem("so_hi"), sem("so_lo")
        lru_a, lru_v, bd_zero, xe_ok, tap0 = sem("lru_a"), sem("lru_v"), sem("bd_zero"), sem("xe_ok"), sem("tap0")
        xc_ok, q_lru, sqrt_ok, u_ok, hs_ok = sem("xc_ok"), sem("q_lru"), sem("sqrt_ok"), sem("u_ok"), sem("hs_ok")
        yt_ok, y_hi, y_lo = sem("yt_ok"), sem("y_hi"), sem("y_lo")
        tm_ok, exp_ok, p_ok, tr_done = sem("tm_ok"), sem("exp_ok"), sem("p_ok"), sem("tr_done")
        pT_ok, pv_done, o_hi, o_lo = sem("pT_ok"), sem("pv_done"), sem("o_hi"), sem("o_lo")
        m_t, m_hi, m_lo, p_hi_ok = sem("m_t"), sem("m_hi"), sem("m_lo"), sem("p_hi_ok")
        f_hi, f_lo, xf_ok, fs_v, fs_a = sem("f_hi"), sem("f_lo"), sem("xf_ok"), sem("fs_v"), sem("fs_a")

        def tiles_of(kind):
            return [t for t, (k, _, _) in enumerate(TILES) if k == kind]

        def acc(t):
            s = 2 * (t % 2)
            return psD[:, s:s + 2, 0:HT]

        def two(ap):
            return ap.rearrange("p (a b) -> p a b", a=2)

        def seqs(ap):
            return ap.rearrange("p (b c) -> p b c", c=ST)

        def bank(job):
            return psX[AUX[job] % 2]

        def got_tile(eng, t):
            eng.wait_ge(w_used, LAST_UNIT[t] + 1)

        def got_job(eng, job):
            eng.wait_ge(aux_done, AUX[job] + 1)

        def read_job(ins, job):
            return ins.then_inc(aux_read[AUX[job] % 2], 1)

        def read_tile(ins, t):
            return ins.then_inc(tile_read[t % 2], 1)

        def job_read(eng, job):
            n = AUX[job]
            eng.wait_ge(aux_read[n % 2], n // 2 + 1)

        def tile_is_read(eng, kind, j, last=False):
            t = NTH[(kind, j, last)]
            eng.wait_ge(tile_read[t % 2], t // 2 + 1)

        def all_read(eng, kind, n):
            tile_is_read(eng, kind, n - 2)
            tile_is_read(eng, kind, n - 1)

        def x_is_new(eng, k, c):
            if k == 0:
                tile_is_read(eng, "wo", c)
            elif k == 1:
                tile_is_read(eng, "down", c, True)
            else:
                eng.wait_ge(xn_ok, c + 1)

        U = {k: FIRST[(k, 0)] for k in ("iq", "ik", "q", "k", "v", "xr", "ga", "gb", "wo", "pp", "pg")}
        h_last = (0, U["wo"], FIRST[("down", 0, True)])
        block = ctx.enter_context(nc.Block())

        @block.sync
        def _(sp):
            def load(n):
                if n >= len(UNITS):
                    return
                _, _, (w, r0, rc, c0, cc, _, _) = UNITS[n]
                if n >= RING:
                    sp.wait_ge(w_lo, n - RING + 1)
                src = a[w][0, P * r0:P * (r0 + rc), c0:c0 + cc].rearrange("(c p) n -> p c n", p=P)
                sp.dma_start(wraw[:, n % RING, 0:rc, 0:cc], src).then_inc(w_loaded[n % RING], 16)

            def pages(dst, pool, b, got):
                for g in range(NPG):
                    page = sp.value_load(pt[0:1, NPG * b + g:NPG * b + g + 1], min_val=0, max_val=n_pool - 1)
                    src = a[pool][0, bass.ds(page, 1)].rearrange("o s h d -> (o s) (h d)")
                    sp.dma_start(dst[:, g, :], src).then_inc(got, 16)

            for t in range(TT):
                sp.dma_start(xtok[:, t, :], a["x_prompt"][0, P * t:P * (t + 1), :]).then_inc(x_in[t], 16)
            sp.dma_start(xtok[0:NS, TT, :], a["x_sample"].rearrange("b j d -> (b j) d")).then_inc(x_in[TT], 16)
            for row, name in ((R_MIX, "norm_mix"), (R_FFN, "norm_ffn"), (R_PLE, "norm_ple"), (R_CB, "conv_b"),
                              (R_BA, "b_rg_a"), (R_BX, "b_rg_x"), (R_LAM, "lru_lambda")):
                sp.dma_start(prm[row:row + 1, :], a[name]).then_inc(prm_in, 16)
            sp.dma_start(prm[R_FIN:R_FIN + 1, :], a["norm_final"].rearrange("(o d) -> o d", o=1)).then_inc(prm_in, 16)
            sp.dma_start(prm[R_CW:R_CW + CW, :], a["conv_w"][0]).then_inc(prm_in, 16)
            sp.dma_start(prm[R_SC:R_SH, :], a["state_conv"][0].rearrange("b i d -> (b i) d")).then_inc(prm_in, 16)
            sp.dma_start(prm[R_SH:NR, :], a["state_rglru_h"][0]).then_inc(prm_in, 16)
            for n in range(RING):
                load(n)
            sp.dma_start(pt[:], a["page_table"].rearrange("(o b) g -> o (b g)", o=1)).then_inc(page_in, 16)
            sp.dma_start(onehot[:], a["bias_onehot"]).then_inc(small_in, 16)
            sp.dma_start(relb[:], a["rel_bias"]).then_inc(small_in, 16)
            sp.wait_ge(page_in, 16)
            for b in range(NB):
                for g in range(NPG):
                    page = sp.value_load(pt[0:1, NPG * b + g:NPG * b + g + 1], min_val=0, max_val=n_pool - 1)
                    src = a["cache_idx_k"][0, bass.ds(page, 1)].rearrange("o s d -> (o s) d")
                    for r in range(2):
                        sp.dma_start(idxp[:, NPG * b + g, r, :], src).then_inc(idxp_in, 16)
            job_read(sp, ("x", DC - 2))
            job_read(sp, ("x", DC - 1))
            sp.dma_start(x_d, x[:].rearrange("p c t -> p (c t)")).then_inc(x_saved, 16)
            job_read(sp, "lines_a")
            job_read(sp, "lines_b")
            sp.dma_start(lines_d, lines[:].unsqueeze(1).broadcast_to([NH, P, LW])).then_inc(lines_saved, 16)
            for n in range(RING, 8):
                load(n)
            tile_is_read(sp, "ik", 0)
            sp.dma_start(ik2[HD:P, :], ikw[0:HD, :]).then_inc(ik_dup, 16)
            load(8)
            job_read(sp, "ik")
            sp.dma_start(o["idx_k_prompt"][0, 0].rearrange("(t p) d -> p t d", p=P),
                         iktok[:, 0:TT, 0:HD]).then_inc(out_done, 16)
            sp.dma_start(o["idx_k_sample"][0].rearrange("b j d -> (b j) d"),
                         iktok[0:NS, TT, 0:HD]).then_inc(out_done, 16)
            for n in range(9, 13):
                load(n)
            sp.wait_ge(lines_saved, 16)
            sp.wait_ge(ik_dup, 16)
            for g in range(NB // 2):
                for jj in range(NJ):
                    rows = bias_s[NS * g + jj:NS * (g + 1):NJ, 0:PAST]
                    sp.dma_start(rows, lines_d[:, 0, LMAX - PAST - jj:LMAX - jj]).then_inc(bias_in, 16)
                    rows = bias_n[NS * g + jj:NS * (g + 1):NJ, :]
                    sp.dma_start(rows, lines_d[:, 0, LMAX - jj:LMAX - jj + NJ]).then_inc(bias_in, 16)
            for n in range(13, 16):
                load(n)
            for b in range(2):
                pages(kpg[b], "cache_k", b, kpg_in[b])
            sp.wait_ge(bd_zero, 1)
            for g, w in enumerate(("w_rg_a", "w_rg_x")):
                for h in range(2):
                    sp.dma_start(bd[HD * h:HD * (h + 1), :, g, HD * h:HD * (h + 1)],
                                 a[w][0].rearrange("(c h) k d -> h k c d", h=2)[h]).then_inc(bd_in, 16)
            load(16)
            for t in range(TT + 1):
                load(17 + t)
                rows = P if t < TT else NS
                job_read(sp, ("kout", t))
                dst = (o["k_prompt"][0, 0, P * t:P * (t + 1)].rearrange("s h d -> s (h d)") if t < TT
                       else o["k_sample"][0].rearrange("b j h d -> (b j) (h d)"))
                sp.dma_start(dst, ktok[t % 2][0:rows, :]).then_inc(ktok_out[t % 2], 16)
            for b in range(2, NB):
                job_read(sp, ("kts", b - 2, 1))
                pages(kpg[b % 2], "cache_k", b, kpg_in[b % 2])
                if 20 + b <= 24:
                    load(20 + b)
            for b in range(2):
                job_read(sp, ("kts", NB - 2 + b, 1))
                pages(kpg[b], "cache_v", b, kpg_in[b])
            for t in range(TT + 1):
                job_read(sp, ("vout", t))
                dst = (o["v_prompt"][0, 0, P * t:P * (t + 1)].rearrange("s h d -> s (h d)") if t < TT
                       else o["v_sample"][0].rearrange("b j h d -> (b j) (h d)"))
                sp.dma_start(dst, vtok[:, t, :] if t < TT else vtok_s[:]).then_inc(out_done, 16)
            load(25)
            load(26)
            for b in range(2, NB):
                load(25 + b)
                sp.wait_ge(spv_b, b - 1)
                pages(kpg[b % 2], "cache_v", b, kpg_in[b % 2])
            for n in range(33, 39):
                load(n)
            job_read(sp, "st_a")
            job_read(sp, "st_b")
            sp.dma_start(o["conv_prompt"][0, 0], orow[C_CP:C_CS, :]).then_inc(out_done, 16)
            sp.dma_start(o["conv_sample"][0].rearrange("b i d -> (b i) d"), orow[C_CS:C_HP, :]).then_inc(out_done, 16)
            sp.dma_start(o["h_prompt"][0], orow[C_HP:C_HS, :]).then_inc(out_done, 16)
            sp.dma_start(o["h_sample"][0], orow[C_HS:NC, :]).then_inc(out_done, 16)
            sp.wait_ge(out_done, 16 * (2 + TT + 1 + 4))
            n = 39
            for h in range(NH):
                if h >= 2:
                    sp.wait_ge(tm_ok, TT * (h - 1))
                src = bass.AP(tensor=lines_d.tensor, offset=LW * P * h + P - 1, ap=[[LW - 1, P], [1, SEQ]])
                sp.dma_start(th[h % 2][:], src).then_inc(th_in[h % 2], 16)
                if h >= 1:
                    load(n)
                    load(n + 1)
                    n += 2
            while n < U["gb"] + 4:
                load(n)
                n += 1
            sp.wait_ge(pv_done, STEPS)
            sp.dma_start(ptok[:, 0:TT, :], a["p_prompt"][0, 0].rearrange("(t p) d -> p t d", p=P)).then_inc(p_in, 16)
            sp.dma_start(ptok[0:NS, TT, :], a["p_sample"][0].rearrange("b j d -> (b j) d")).then_inc(p_in, 16)
            while n < U["wo"] + 4:
                load(n)
                n += 1
            sp.wait_ge(m_t, DC)
            sp.dma_start(x[:].rearrange("p c t -> p (c t)"), x_d).then_inc(x_back, 16)
            while n < len(UNITS):
                load(n)
                n += 1
            for t in range(TT + 1):
                rows = P if t < TT else NS
                job_read(sp, ("y", t, 0))
                job_read(sp, ("y", t, 1))
                dst = (o["y_prompt"][0, P * t:P * (t + 1), :] if t < TT
                       else o["y_sample"].rearrange("b j d -> (b j) d"))
                sp.dma_start(dst, ytok[0:rows, t, :]).then_inc(out_done, 16)
            sp.wait_ge(out_done, 16 * (2 + TT + 1 + 4 + TT + 1))
            sp.wait_ge(ktok_out[0], 16 * 3)
            sp.wait_ge(ktok_out[1], 16 * 2)
            sp.wait_ge(x_saved, 16)

        @block.scalar
        def _(act):
            sc = nc.scalar
            steps = [0]

            def link(ins):
                steps[0] += 1
                ins.then_inc(act_step, 1)
                act.wait_ge(act_step, steps[0])

            def round_weights(n):
                if n >= len(UNITS):
                    return
                _, _, (_, _, rc, _, cc, _, _) = UNITS[n]
                act.wait_ge(w_loaded[n % RING], 16 * (n // RING + 1))
                if n >= RING:
                    act.wait_ge(w_used, n - RING + 1)
                sc.copy(whi[:, n % RING, 0:rc, 0:cc], wraw[:, n % RING, 0:rc, 0:cc]).then_inc(w_hi, 1)

            def norm_hi(k, c):
                act.wait_ge(n_t, DC * k + c + 1)
                if k and c == 0:
                    act.wait_ge(w_used, h_last[k])
                sc.copy(h_hi[:, c, :], hmul[c % 2][:]).then_inc(n_hi, 1)

            def root(dst, src, signal):
                sc.activation(dst, src, ACT.Sqrt).then_inc(signal, 1)

            for t in range(TT + 1):
                rows = P if t < TT else NS
                act.wait_ge(x_in[t], 16)
                if t:
                    act.wait_ge(sq_done, t)
                else:
                    act.wait_ge(pool_const, 1)
                sc.activation(junk[0:rows, :], xtok[0:rows, t, :], ACT.Square,
                              accum_out=stat[0:rows, t:t + 1]).then_inc(sq_done, 1)
            got_job(act, "prm")
            read_job(sc.copy(prmT[:], bank("prm")[:, 0:DC * NR].rearrange("p (c r) -> p c r", r=NR)), "prm")
            got_job(act, "xs")
            read_job(sc.copy(x[:, :, SEQ:T], bank("xs")[:, 0:DC * NS].rearrange("p (c s) -> p c s", s=NS)), "xs")
            for c in range(0, DC, 2):
                got_job(act, ("x", c))
                read_job(sc.copy(x[:, c, 0:SEQ], bank(("x", c))), ("x", c))
                if c == 2:
                    act.wait_ge(rstd_v, 2)
                    root(stat[:, 16:16 + TT + 1], stat[:, 8:8 + TT + 1], rstd_a)
            job_read(act, "prm")
            link(sc.activation(lru[:, 0, :], prmT[:, :, R_LAM], ACT.Abs))
            sc.activation(lru[:, 1, :], lru[:, 0, :], ACT.Exp, scale=-1.0).then_inc(lru_a, 1)
            for c in range(DC):
                norm_hi(0, c)
                if c < RING:
                    round_weights(c)
            for n in range(4):
                got_job(act, ("iks", n))
                dst = iks[:, 2 * n:2 * n + 2, :].rearrange("p b s -> p (b s)")
                read_job(sc.copy(dst, bank(("iks", n))), ("iks", n))

            n = 0
            for t in tiles_of("iq"):
                got_tile(act, t)
                act.wait_ge(diag_ok, 2)
                read_tile(sc.copy(two(iqT[:, t, :]), acc(t)), t)
                round_weights(n + RING)
                n += 1
            t = tiles_of("ik")[0]
            got_tile(act, t)
            link(sc.copy(two(ikw[0:HD + NH, :]), acc(t)[0:HD + NH]))
            read_tile(sc.copy(two(ik2[0:HD, :]), acc(t)[0:HD]), t)
            round_weights(n + RING)
            n += 1

            def index_relu(s):
                got_job(act, ("idx", s))
                if s >= 2:
                    act.wait_ge(idx_acc, s - 1)
                w = P * (2 + s // NH)
                read_job(sc.activation(relu[s % 2][:, 0:w], bank(("idx", s))[:, 0:w], ACT.Relu, scale=HD ** -0.5),
                         ("idx", s))

            def key_rows(t):
                rows = P if t < TT else NS
                got_job(act, ("kout", t))
                if t >= 2:
                    act.wait_ge(ktok_out[t % 2], 16 * (t // 2))
                else:
                    job_read(act, ("iks", 3))
                    job_read(act, ("iks", 2))
                read_job(sc.copy(ktok[t % 2][0:rows, :], bank(("kout", t))[0:rows, :]), ("kout", t))

            def value_rows(t):
                rows = P if t < TT else NS
                got_job(act, ("vout", t))
                dst = vtok[:, t, :] if t < TT else vtok_s[:]
                read_job(sc.copy(dst, bank(("vout", t))[0:rows, :]), ("vout", t))

            def past_keys(b):
                for g in range(NPG):
                    got_job(act, ("kts", b, g))
                    if b >= 2 and g == 0:
                        act.wait_ge(slogit_b, b - 1)
                    dst = kts[b % 2][:, :, PG * g:PG * (g + 1)]
                    src = bank(("kts", b, g))[:].rearrange("p (m s) -> p m s", s=PG)
                    read_job(sc.copy(dst, src), ("kts", b, g))

            for kind, dst, scale in (("q", qT, HD ** -0.5), ("k", kT, 1.0), ("v", vT, 1.0)):
                for t in tiles_of(kind):
                    j = TILES[t][1]
                    if kind == "q":
                        for s in range(6 * j, 6 * j + 6):
                            index_relu(s)
                    got_tile(act, t)
                    if kind == "v" and j == 0:
                        act.wait_ge(x_saved, 16)
                    read_tile(sc.activation(two(dst[:, j, :]), acc(t), ACT.Copy, scale=scale), t)
                    round_weights(n + RING)
                    n += 1
                    if kind == "v":
                        if j == 0:
                            for tt in range(TT + 1):
                                key_rows(tt)
                        else:
                            for b in (2 * j - 2, 2 * j - 1):
                                past_keys(b)
            for b in (6, 7):
                past_keys(b)
            for tt in range(TT + 1):
                value_rows(tt)

            def sample_exp(g):
                job_read(act, ("smask", g))
                sc.activation(ps_s[:, g, :], ps_s[:, g, :], ACT.Exp, bias=sstat[:, g:g + 1], scale=-1.0,
                              accum_out=sstat[:, 2 + g:3 + g]).then_inc(sexp_ok, 1)

            def sample_turned():
                got_job(act, "spt")
                read_job(sc.copy(pts[:].rearrange("p a g q -> p (a g q)"), bank("spt")), "spt")
                got_job(act, "spn")
                read_job(sc.copy(ptn[:].rearrange("p g q -> p (g q)"), bank("spn")[0:NS, 0:2 * P]), "spn")

            def sample_out_hi():
                act.wait_ge(spv_b, NB)
                for h in range(2):
                    src = psX[2][HD * h:HD * (h + 1), 0:HP * 64].rearrange("p (m b h j) -> p m b h j", m=HP, b=NB, h=2)
                    for m in range(HP):
                        sc.copy(act_hi[HD * h:HD * (h + 1), 8 + m, SEQ:T].rearrange("p (b j) -> p b j", j=NJ),
                                src[:, m, :, h, :]).then_inc(so_hi, 1)

            def conv_line(c, t):
                s = c % 2
                if c >= 2:
                    act.wait_ge(xc_ok, c - 1)
                else:
                    job_read(act, ("vout", TT))
                    act.wait_ge(bd_zero, 2)
                got_tile(act, t)
                ps = acc(t)
                sc.copy(seqs(xe[s][:, S0:EXT])[:, :, 0:CW - 1],
                        prmT[:, c, R_SC:R_SH].rearrange("p (b i) -> p b i", b=NB)).then_inc(xe_ok, 1)
                sc.copy(xe[s][:, CW - 1:CW - 1 + HT], ps[:, 0, :]).then_inc(xe_ok, 1)
                sc.copy(xe[s][:, CW - 1 + HT:S0], ps[:, 1, 0:SEQ - HT]).then_inc(xe_ok, 1)
                read_tile(sc.copy(seqs(xe[s][:, S0:EXT])[:, :, CW - 1:ST],
                                  ps[:, 1, SEQ - HT:HT].rearrange("p (b j) -> p b j", j=NJ)), t)
                act.wait_ge(xe_ok, 3 * (c + 1))
                tile_is_read(act, "xr", c)
                if c >= 2:
                    act.wait_ge(u_ok, c - 1)
                sc.activation(xc[s][:], xe[s][:, 0:EO], ACT.Identity, scale=prmT[:, c, R_CW:R_CW + 1],
                              bias=prmT[:, c, R_CB:R_CB + 1]).then_inc(tap0, 1)

            def gates(c):
                if c >= 1:
                    act.wait_ge(hs_ok, c)
                for g, dst in ((0, rq), (1, ig)):
                    for k in range(2):
                        job = ("gate", c, g, k)
                        got_job(act, job)
                        read_job(sc.activation(dst[:, EH * k:EH * (k + 1)], bank(job)[:, 0:EH], ACT.Tanh, scale=0.5,
                                               bias=lru[:, 4 + g, c:c + 1]), job)
                    if g == 0:
                        job_read(act, ("gate", c, 0, 0))
                        job_read(act, ("gate", c, 0, 1))
                        sc.activation(rq[:], rq[:], ACT.Tanh, scale=lru[:, 3, c:c + 1],
                                      bias=lru[:, 3, c:c + 1]).then_inc(q_lru, 1)

            def gelu_path(c, t):
                got_tile(act, t)
                if c >= 2:
                    act.wait_ge(yt_ok, c - 1)
                elif c == 0:
                    job_read(act, ("smask", 1))
                read_tile(sc.activation(two(gel[c % 2][:]), acc(t), ACT.Gelu_apprx_tanh), t)

            def lru_root(c):
                act.wait_ge(q_lru, c + 1)
                if c >= 1:
                    act.wait_ge(hs_ok, c)
                root(sq[:], rq[:], sqrt_ok)

            def y_upper(c):
                act.wait_ge(yt_ok, c + 1)
                sc.copy(act_hi[:, c, :], hmul[c % 2][:]).then_inc(y_hi, 1)

            act.wait_ge(lru_v, 1)
            for c in range(DC):
                if c == 1:
                    sample_exp(0)
                    sample_exp(1)
                conv_line(c, FIRST_TILE["xr"] + 2 * c)
                if c == 1:
                    sample_turned()
                if c == 6:
                    sample_out_hi()
                round_weights(n + RING)
                if c >= 1:
                    y_upper(c - 1)
                gelu_path(c, FIRST_TILE["gr"] + 2 * c)
                round_weights(n + 1 + RING)
                n += 2
                gates(c)
                lru_root(c)
            y_upper(DC - 1)
            for k, job in enumerate(("st_a", "st_b")):
                got_job(act, job)
                read_job(sc.copy(orow[:, SEQ * k:SEQ * (k + 1)], bank(job)[0:NC, :]), job)

            def attend_exp(s):
                w = P * (s % TT + 1)
                job_read(act, ("qk", s))
                sc.activation(pr[s % 2][:, 0:w], pr[s % 2][:, 0:w], ACT.Exp, bias=stat[:, 24 + s % 2:25 + s % 2],
                              scale=-1.0, accum_out=stat[:, 26 + s % 2:27 + s % 2]).then_inc(exp_ok, 1)

            def attend_turned(s):
                w = P * (s % TT + 1)
                act.wait_ge(tr_done, s + 1)
                if s >= 2:
                    act.wait_ge(pv_done, s - 1)
                elif s == 0:
                    act.wait_ge(y_lo, DC)
                sc.copy(pT[s % 2][:, 0:s % TT + 1, :].rearrange("p k t -> p (k t)"), psX[2][:, 0:w])\
                    .then_inc(pT_ok, 1)

            def attend_out_hi(m):
                act.wait_ge(pv_done, 2 * TT * (m + 1))
                sc.copy(act_hi[:, 8 + m, 0:SEQ], psX[3][:]).then_inc(o_hi, 1)

            def attend(i):
                for s in (2 * i, 2 * i + 1):
                    if s < STEPS:
                        attend_exp(s)
                    if 1 <= s <= STEPS:
                        attend_turned(s - 1)
                    if s >= 9 and (s - 9) % 8 == 0:
                        attend_out_hi((s - 9) // 8)

            def gate_tanh(k, t):
                got_tile(act, t)
                if k >= 2:
                    tile_is_read(act, *(("rnn", k - 2) if k < DC + 2 else ("att", k - 2 - DC)))
                elif k == 0:
                    act.wait_ge(hs_ok, DC)
                    act.wait_ge(yt_ok, DC)
                read_tile(sc.activation(two(sg[k % 2][:]), acc(t), ACT.Tanh, scale=0.5), t)

            for j in range(DC):
                gate_tanh(j, FIRST_TILE["ga"] + 2 * j)
                round_weights(n + RING)
                attend(2 * j)
                round_weights(n + 1 + RING)
                attend(2 * j + 1)
                n += 2
            attend(2 * DC)

            def upper(dst, k, hi_ok, scale=1.0):
                sc.activation(dst, hmul[k % 2][:], ACT.Copy, scale=scale).then_inc(hi_ok, 1)

            for j in range(DC):
                gate_tanh(DC + j, FIRST_TILE["gb"] + 2 * j)
                round_weights(n + RING)
                round_weights(n + 1 + RING)
                if j >= 1:
                    act.wait_ge(m_t, j)
                    upper(act_hi[:, j - 1, :], j - 1, m_hi, 0.5)
                if j >= 1 and j - 1 <= TT:
                    t = j - 1
                    c0, c1 = (P * t, P * (t + 1)) if t < TT else (SEQ, T)
                    got_job(act, ("p", t))
                    sc.copy(p_hi[:, :, c0:c1], bank(("p", t))[:, 0:2 * (c1 - c0)].rearrange("p (k t) -> p k t", k=2))\
                        .then_inc(p_hi_ok, 1)
                n += 2
            act.wait_ge(m_t, DC)
            upper(act_hi[:, DC - 1, :], DC - 1, m_hi, 0.5)

            def square(k, c):
                x_is_new(act, k, c)
                i = DC * k + c
                if i >= 2:
                    act.wait_ge(sqacc_ok, i - 1)
                sc.activation(sqt[i % 2][:], x[:, c, :], ACT.Square).then_inc(sq_ok, 1)

            for j in range(DC):
                round_weights(n + RING)
                n += 1
                square(0, j)
            act.wait_ge(rb_v, 1)
            root(rb[:], rb[:], rb_a)
            for j in range(DC):
                t = FIRST_TILE["pp"] + j
                norm_hi(1, j)
                got_tile(act, t)
                read_tile(sc.copy(two(pp[:, j, :]), acc(t)), t)
                round_weights(n + RING)
                n += 1
            k = 0
            for half, (f0, fn) in enumerate(FFN_HALVES):
                t0 = FIRST_TILE["gate"] + half * (2 * FA + DC)
                for f in range(fn):
                    t = t0 + 2 * f
                    got_tile(act, t)
                    if k >= 2:
                        tile_is_read(act, "up", k - 2)
                    read_tile(sc.activation(two(sg[k % 2][:]), acc(t), ACT.Silu), t)
                    round_weights(n + RING)
                    round_weights(n + 1 + RING)
                    n += 2
                    if f >= 1:
                        tile_is_read(act, "up", k - 1)
                        upper(act_hi[:, f - 1, :], k - 1, f_hi)
                    k += 1
                tile_is_read(act, "up", k - 1)
                upper(act_hi[:, fn - 1, :], k - 1, f_hi)
                for j in range(DC):
                    round_weights(n + RING)
                    round_weights(n + 1 + RING)
                    n += 2
                    if half:
                        square(1, j)
            act.wait_ge(rb_v, 2)
            root(rb[:], rb[:], rb_a)
            for j in range(DC):
                norm_hi(2, j)
            for j in range(DC):
                t = FIRST_TILE["pg"] + j
                got_tile(act, t)
                if j >= 2:
                    act.wait_ge(xn_ok, j - 1)
                read_tile(sc.activation(two(sg[j % 2][:]), acc(t), ACT.Tanh, scale=0.5), t)
                round_weights(n + RING)
                n += 1
                if j >= 1:
                    square(2, j - 1)
                    sc.activation(pp[:, j - 1, :], x[:, j - 1, :], ACT.Copy,
                                  scale=prmT[:, j - 1, R_FIN:R_FIN + 1]).then_inc(xf_ok, 1)
            square(2, DC - 1)
            sc.activation(pp[:, DC - 1, :], x[:, DC - 1, :], ACT.Copy,
                          scale=prmT[:, DC - 1, R_FIN:R_FIN + 1]).then_inc(xf_ok, 1)
            act.wait_ge(fs_v, 1)
            root(stat[:, 48:48 + TT + 1], stat[:, 40:40 + TT + 1], fs_a)
            act.wait_ge(fs_a, 1)
            for t in range(TT + 1):
                rows = P if t < TT else NS
                job = ("y", t, 0)
                got_job(act, job)
                read_job(sc.activation(ytok[0:rows, t, 0:512], bank(job)[0:rows, :], ACT.Copy,
                                       scale=stat[0:rows, 48 + t:49 + t]), job)

        @block.vector
        def _(dve):
            v = nc.vector
            steps = [0]

            def link(ins):
                steps[0] += 1
                ins.then_inc(dve_step, 1)
                dve.wait_ge(dve_step, steps[0])

            def inverse_mean(ap, src):
                link(v.tensor_scalar(ap, src, 1.0 / D, EPS, ALU.mult, ALU.add))
                return v.reciprocal(ap, ap)

            def norm_scale(k, c, gain, factor):
                i = DC * k + c
                if c >= 2:
                    dve.wait_ge(n_hi, i - 1)
                    if c % 2:
                        dve.wait_ge(n_lo_p, 4 * k + (c - 2) // 2 + 1)
                    else:
                        dve.wait_ge(n_lo_v, 4 * k + (c - 2) // 2 + 1)
                v.scalar_tensor_tensor(hmul[c % 2][:], x[:, c, :], prmT[:, c, gain:gain + 1], factor,
                                       ALU.mult, ALU.mult).then_inc(n_t, 1)

            def norm_lo(k, c):
                dve.wait_ge(n_hi, DC * k + c + 1)
                v.tensor_tensor(h_lo[:, c, :], hmul[c % 2][:], h_hi[:, c, :].bitcast(F32), ALU.subtract)\
                    .then_inc(n_lo_v, 1)

            def norm(k, gain, factor):
                for c in range(DC):
                    norm_scale(k, c, gain, factor)
                    if c % 2 == 0:
                        norm_lo(k, c)

            v.memset(ones[:], 1.0).then_inc(ones_ok, 1)
            dve.wait_ge(ident_ok, 2)
            got_job(dve, ("x", 1))
            read_job(v.tensor_copy(x[:, 1, 0:SEQ], bank(("x", 1))), ("x", 1))
            dve.wait_ge(sq_done, TT + 1)
            inverse_mean(stat[:, 8:8 + TT + 1], stat[:, 0:TT + 1]).then_inc(rstd_v, 2)
            got_job(dve, ("x", 3))
            read_job(v.tensor_copy(x[:, 3, 0:SEQ], bank(("x", 3))), ("x", 3))
            dve.wait_ge(rstd_a, 1)
            for t in range(TT):
                ins = v.tensor_scalar(diag[:, t, :], ident[:], stat[:, 16 + t:17 + t], None, ALU.mult)
            ins.then_inc(diag_ok, 1)
            v.tensor_scalar(diag[0:NS, TT, 0:NS], ident[0:NS, 0:NS], stat[0:NS, 16 + TT:17 + TT], None, ALU.mult)\
                .then_inc(diag_ok, 1)
            got_job(dve, "rstd_a")
            read_job(v.tensor_copy(rb0[:, 0:SEQ], bank("rstd_a")), "rstd_a")
            got_job(dve, "rstd_b")
            read_job(v.tensor_copy(rb0[:, SEQ:T], bank("rstd_b")[:, 0:NS]), "rstd_b")
            for c in (5, 7):
                got_job(dve, ("x", c))
                read_job(v.tensor_copy(x[:, c, 0:SEQ], bank(("x", c))), ("x", c))
            job_read(dve, "rstd_a")
            job_read(dve, "rstd_b")
            job_read(dve, "prm")
            job_read(dve, ("x", DC - 2))
            job_read(dve, ("x", DC - 1))
            norm(0, R_MIX, rb0[:])

            for k, job in enumerate(("lines_a", "lines_b")):
                got_job(dve, job)
                w = LW // 2
                read_job(v.tensor_copy(lines[:, w * k:w * (k + 1)], bank(job)[0:NH, 0:w]), job)
            got_job(dve, "selT")
            read_job(v.tensor_copy(selT[:].rearrange("p g c -> p (g c)"), bank("selT")[:, 0:2 * NS]), "selT")

            dve.wait_ge(lru_a, 1)
            e, z, z2, s, sp_ = (lru[:, i, :] for i in (1, 2, 6, 7, 3))
            link(v.tensor_scalar(z, e, 2.0, None, ALU.add))
            link(v.reciprocal(z, z))
            link(v.tensor_tensor(z, z, e, ALU.mult))
            link(v.tensor_tensor(z2, z, z, ALU.mult))
            link(v.tensor_scalar(s, z2, 1.0 / 17, None, ALU.mult))
            for k in range(15, 1, -2):
                link(v.scalar_tensor_tensor(s, s, 1.0 / k, z2, ALU.add, ALU.mult))
            link(v.scalar_tensor_tensor(s, s, 1.0, z, ALU.add, ALU.mult))
            link(v.tensor_scalar(z, prmT[:, :, R_LAM], -1.0, 0.0, ALU.mult, ALU.max))
            link(v.scalar_tensor_tensor(s, s, 2.0, z, ALU.mult, ALU.add))
            v.tensor_scalar(sp_, s, 2.0, None, ALU.mult)
            v.tensor_scalar(lru[:, 4, :], prmT[:, :, R_BA], 0.5, None, ALU.mult)
            v.tensor_scalar(lru[:, 5, :], prmT[:, :, R_BX], 0.5, None, ALU.mult).then_inc(lru_v, 1)

            got_job(dve, "ik")
            kw = HD + NH
            src = bank("ik")[:, 0:(TT + 1) * kw].rearrange("p (t c) -> p t c", c=kw)
            link(v.tensor_copy(iktok[:, 0:TT, :], src[:, 0:TT, :]))
            read_job(v.tensor_copy(iktok[0:NS, TT, :], src[0:NS, TT, :]), "ik")
            job_read(dve, "ik")
            link(v.tensor_scalar(iwtok[:, 0:TT, :], iktok[:, 0:TT, HD:kw], NH ** -0.5, None, ALU.mult))
            v.tensor_scalar(iwtok[0:NS, TT, :], iktok[0:NS, TT, HD:kw], NH ** -0.5, None, ALU.mult)\
                .then_inc(iwcol_ok, 1)
            dve.wait_ge(iwcol_ok, 1)

            for st in range(NH * (TT - 1)):
                i, h = 1 + st // NH, st % NH
                w = P * (i + 1)
                job_read(dve, ("idx", st))
                r, wt = relu[st % 2][:, 0:w], iwtok[:, i, h:h + 1]
                if h == 0:
                    ins = v.tensor_scalar(score[i][:], r, wt, None, ALU.mult)
                else:
                    dve.wait_ge(idx_acc, st)
                    ins = v.scalar_tensor_tensor(score[i][:], r, wt, score[i][:], ALU.mult, ALU.add)
                ins.then_inc(idx_acc, 1)

            got_job(dve, "iwcol")
            dve.wait_ge(pool_const, 2)
            for g in range(2):
                src = bank("iwcol")[:, NH * g:NH * (g + 1)].unsqueeze(1).broadcast_to([P, NB // 2, NH])
                ins = v.tensor_tensor(iwsc[:], hm[:], src, ALU.mult)
                if g:
                    read_job(ins, "iwcol")
                    job_read(dve, "iwcol")
                else:
                    link(ins)
                link(v.tensor_reduce(stat[:, 60 + g:61 + g], iwsc[:].rearrange("p b h -> p (b h)"),
                                     mybir.AxisListType.X, ALU.add))
            link(v.tensor_scalar(stat[:, 60:62], stat[:, 60:62], HD ** -0.5, None, ALU.mult))
            dve.wait_ge(sdots, 1)
            for g in range(2):
                v.tensor_scalar(rs_s[:, g, :], psX[2 + g][:, 0:SK], 0.0, stat[:, 60 + g:61 + g], ALU.max, ALU.mult)\
                    .then_inc(rs_ok, 1)
            v.memset(score_s[:, SK:SK + 8], PAD).then_inc(ss_copied, 1)
            got_job(dve, "sidx")
            read_job(v.tensor_copy(score_s[:, 0:SK], bank("sidx")[0:NS, 0:SK]), "sidx")

            def top_k(work, keys, k, rows):
                for r in range(-(-k // 8)):
                    link(v.max(top8[0:rows, :], work[:, 0:keys]))
                    left = k - 8 * r
                    if left < 8:
                        link(v.memset(top8[0:rows, left:8], PAD))
                    link(v.match_replace(work[:], top8[0:rows, :], work[:], TAKEN))

            def to_mask(work):
                return v.tensor_scalar(work, work, TAKEN_BELOW, OFF, ALU.is_gt, ALU.mult)

            dve.wait_ge(masked_in, TT)
            top_k(score_s, SK, TOPK_S, NS)
            to_mask(score_s[:, 0:SK]).then_inc(topk_ok, 1)
            for i in range(1, TT):
                top_k(score[i], P * (i + 1), TOPK_P, P)
                to_mask(score[i][:]).then_inc(topk_ok, 1)

            dve.wait_ge(slogit_b, NB)
            dve.wait_ge(bias_in, 16 * 2 * NB // 2 * NJ)
            new = bias_n[:].unsqueeze(1).broadcast_to([P, NB, NJ])
            link(v.tensor_copy(bias_s[:, PAST:SK].rearrange("p (b j) -> p b j", j=NJ), new))
            for g in range(2):
                ins = v.tensor_tensor(ps_s[:, g, :], psX[2 + g][:, 0:SK], bias_s[:], ALU.add)
                link(ins)
            for g in range(2):
                job = ("smask", g)
                got_job(dve, job)
                read_job(v.tensor_tensor_reduce(ps_s[:, g, :], ps_s[:, g, :], bank(job)[:, 0:SK], -1.0, 3.0e38,
                                                ALU.add, ALU.min, sstat[:, g:g + 1]), job)

            def sample_normal():
                for g in range(2):
                    dve.wait_ge(sexp_ok, g + 1)
                    link(v.reciprocal(sstat[:, 4 + g:5 + g], sstat[:, 2 + g:3 + g]))
                    v.tensor_scalar(ps_s[:, g, :], ps_s[:, g, :], sstat[:, 4 + g:5 + g], None, ALU.mult)\
                        .then_inc(sp_ok, 1)

            def sample_out_lo():
                dve.wait_ge(so_hi, 2 * HP)
                for h in range(2):
                    rows = slice(HD * h, HD * (h + 1))
                    src = psX[2][rows, 0:HP * 64].rearrange("p (m b h j) -> p m b h j", m=HP, b=NB, h=2)
                    for m in range(HP):
                        def line(t):
                            return t[rows, 8 + m, SEQ:T].rearrange("p (b j) -> p b j", j=NJ)
                        v.tensor_tensor(line(act_lo), src[:, m, :, h, :], line(act_hi).bitcast(F32), ALU.subtract)\
                            .then_inc(so_lo, 1)

            def conv_taps(c):
                s = c % 2
                dve.wait_ge(tap0, c + 1)
                for j in range(1, CW):
                    link(v.scalar_tensor_tensor(xc[s][:], xe[s][:, j:j + EO], prmT[:, c, R_CW + j:R_CW + j + 1],
                                                xc[s][:], ALU.mult, ALU.add))
                v.tensor_copy(stO[:, c, C_CP:C_CS], xe[s][:, SEQ:S0])
                v.tensor_copy(stO[:, c, C_CS:C_HP].rearrange("p (b i) -> p b i", b=NB),
                              seqs(xe[s][:, S0:EXT])[:, :, NJ:ST]).then_inc(xc_ok, 1)

            def recurrence(c):
                s = c % 2
                dve.wait_ge(q_lru, c + 1)
                if c:
                    dve.wait_ge(yt_ok, c)
                link(v.tensor_scalar(hs[:], rq[:], 1.0, None, ALU.add))
                link(v.reciprocal(hs[:], hs[:]))
                dve.wait_ge(sqrt_ok, c + 1)
                link(v.tensor_tensor(sq[:], sq[:], hs[:], ALU.mult))
                v.tensor_scalar(rq[:], hs[:], 2.0, -1.0, ALU.mult, ALU.add)
                job_read(dve, ("gate", c, 1, 0))
                job_read(dve, ("gate", c, 1, 1))
                link(v.scalar_tensor_tensor(ig[:], ig[:], 1.0, xc[s][:], ALU.add, ALU.mult))
                link(v.tensor_tensor(ig[:], ig[:], sq[:], ALU.mult))
                link(v.memset(seqs(rq[:, SEQ:EO])[:, :, 0:CW - 1], 0.0))
                link(v.memset(seqs(ig[:, SEQ:EO])[:, :, 0:CW - 2], 0.0))
                ins = v.tensor_copy(seqs(ig[:, SEQ:EO])[:, :, CW - 2:CW - 1],
                                    prmT[:, c, R_SH:NR].rearrange("p (b i) -> p b i", i=1))
                ins.then_inc(u_ok, 1)
                dve.wait_ge(u_ok, c + 1)
                v.tensor_tensor_scan(hs[:], rq[:], ig[:], 0.0, ALU.mult, ALU.add).then_inc(hs_ok, 1)
                dve.wait_ge(hs_ok, c + 1)
                v.tensor_copy(stO[:, c, C_HP:C_HS], hs[:, SEQ - 1:SEQ])
                v.tensor_copy(stO[:, c, C_HS:NC].rearrange("p (b i) -> p b i", i=1), seqs(hs[:, SEQ:EO])[:, :, ST - 1:ST])
                tile_is_read(dve, "gr", c)
                if c >= 2:
                    dve.wait_ge(y_hi, c - 1)
                    dve.wait_ge(y_lo, c - 1)
                link(v.tensor_tensor(hmul[s][:, 0:SEQ], hs[:, 0:SEQ], gel[s][:, 0:SEQ], ALU.mult))
                v.tensor_tensor(hmul[s][:, SEQ:T].rearrange("p (b j) -> p b j", j=NJ),
                                seqs(hs[:, SEQ:EO])[:, :, CW - 1:ST],
                                gel[s][:, SEQ:T].rearrange("p (b j) -> p b j", j=NJ), ALU.mult).then_inc(yt_ok, 1)

            def y_lower(c):
                dve.wait_ge(y_hi, c + 1)
                if c == 5:
                    dve.wait_ge(spv_b, NB)
                v.tensor_tensor(act_lo[:, c, :], hmul[c % 2][:], act_hi[:, c, :].bitcast(F32), ALU.subtract)\
                    .then_inc(y_lo, 1)

            for c in range(DC):
                conv_taps(c)
                if c >= 1:
                    y_lower(c - 1)
                recurrence(c)
                if c == 0:
                    sample_normal()
                if c == 6:
                    sample_out_lo()
            y_lower(DC - 1)

            def logits(st):
                i = st % TT
                w = P * (i + 1)
                got_job(dve, ("qk", st))
                dve.wait_ge(tm_ok, st + 1)
                if st >= 2:
                    dve.wait_ge(tr_done, st - 1)
                read_job(v.tensor_tensor_reduce(pr[st % 2][:, 0:w], bank(("qk", st))[:, 0:w], tm[st % 2][:, 0:w],
                                                -1.0, 3.0e38, ALU.add, ALU.min, stat[:, 24 + st % 2:25 + st % 2]),
                         ("qk", st))

            def normal(st):
                w = P * (st % TT + 1)
                dve.wait_ge(exp_ok, st + 1)
                link(v.reciprocal(stat[:, 28 + st % 2:29 + st % 2], stat[:, 26 + st % 2:27 + st % 2]))
                v.tensor_scalar(pr[st % 2][:, 0:w], pr[st % 2][:, 0:w], stat[:, 28 + st % 2:29 + st % 2], None,
                                ALU.mult).then_inc(p_ok, 1)

            def attend_out_lo(m):
                dve.wait_ge(o_hi, m + 1)
                v.tensor_tensor(act_lo[:, 8 + m, 0:SEQ], psX[3][:], act_hi[:, 8 + m, 0:SEQ].bitcast(F32),
                                ALU.subtract).then_inc(o_lo, 1)

            def attend(i):
                for st in (2 * i, 2 * i + 1):
                    if st < STEPS:
                        logits(st)
                        normal(st)
                    if st >= 9 and (st - 9) % 8 == 0:
                        attend_out_lo((st - 9) // 8)

            for j in range(DC):
                attend(2 * j)
                t = FIRST_TILE["rnn"] + 2 * j
                got_tile(dve, t)
                tile_is_read(dve, "ga", j)
                if j == 0:
                    dve.wait_ge(x_saved, 16)
                read_tile(v.scalar_tensor_tensor(two(x[:, j, :]), two(sg[j % 2][:]), 1.0, acc(t), ALU.add, ALU.mult), t)
                attend(2 * j + 1)
            attend(2 * DC)

            def lower(dst, k, hi, hi_ok, lo_ok):
                dve.wait_ge(hi_ok, k + 1)
                v.tensor_tensor(dst, hmul[k % 2][:], hi.bitcast(F32), ALU.subtract).then_inc(lo_ok, 1)

            def merged_lower(k):
                dve.wait_ge(m_hi, k + 1)
                v.scalar_tensor_tensor(act_lo[:, k, :], hmul[k % 2][:], 0.5, act_hi[:, k, :].bitcast(F32),
                                       ALU.mult, ALU.subtract).then_inc(m_lo, 1)

            for j in range(DC):
                t = FIRST_TILE["att"] + 2 * j
                got_tile(dve, t)
                tile_is_read(dve, "gb", j)
                if j == 0:
                    dve.wait_ge(pv_done, STEPS)
                if j >= 2:
                    dve.wait_ge(m_hi, j - 1)
                    dve.wait_ge(m_lo, j - 1)
                read_tile(v.scalar_tensor_tensor(two(hmul[j % 2][:]), two(sg[j % 2][:]), 1.0, acc(t),
                                                 ALU.add, ALU.mult), t)
                tile_is_read(dve, "att", j)
                tile_is_read(dve, "rnn", j)
                v.tensor_tensor(hmul[j % 2][:], hmul[j % 2][:], x[:, j, :], ALU.add).then_inc(m_t, 1)
                if j >= 1:
                    merged_lower(j - 1)
                if j >= 1 and j - 1 <= TT:
                    tt = j - 1
                    c0, c1 = (P * tt, P * (tt + 1)) if tt < TT else (SEQ, T)
                    dve.wait_ge(p_hi_ok, tt + 1)
                    read_job(v.tensor_tensor(p_lo[:, :, c0:c1],
                                             bank(("p", tt))[:, 0:2 * (c1 - c0)].rearrange("p (k t) -> p k t", k=2),
                                             p_hi[:, :, c0:c1].bitcast(F32), ALU.subtract), ("p", tt))
            merged_lower(DC - 1)

            def add_square(k, c):
                i = DC * k + c
                dve.wait_ge(sq_ok, i + 1)
                if c == 0:
                    ins = v.tensor_copy(sqacc[:], sqt[i % 2][:])
                else:
                    dve.wait_ge(sqacc_ok, i)
                    ins = v.tensor_tensor(sqacc[:], sqacc[:], sqt[i % 2][:], ALU.add)
                ins.then_inc(sqacc_ok, 1)

            def row_factor(jobs):
                for k, job in enumerate(jobs):
                    got_job(dve, job)
                    half = rb[:, HT * k:HT * (k + 1)]
                    read_job(v.tensor_scalar(half, bank(job)[:, 0:HT], 1.0 / D, EPS, ALU.mult, ALU.add), job)
                    job_read(dve, job)
                v.reciprocal(rb[:], rb[:]).then_inc(rb_v, 1)

            dve.wait_ge(x_back, 16)
            for j in range(DC):
                t = FIRST_TILE["wo"] + j
                got_tile(dve, t)
                read_tile(v.tensor_tensor(two(x[:, j, :]), two(x[:, j, :]), acc(t), ALU.add), t)
                if j >= 1:
                    add_square(0, j - 1)
            add_square(0, DC - 1)
            row_factor(("ss1a", "ss1b"))
            dve.wait_ge(rb_a, 1)
            norm(1, R_FFN, rb[:])

            k = 0
            for half, (f0, fn) in enumerate(FFN_HALVES):
                t0 = FIRST_TILE["gate"] + half * (2 * FA + DC)
                for f in range(fn):
                    t = t0 + 2 * f + 1
                    tile_is_read(dve, "gate", k)
                    got_tile(dve, t)
                    if k >= 2:
                        dve.wait_ge(f_hi, k - 1)
                        dve.wait_ge(f_lo, k - 1)
                    elif k == 1:
                        dve.wait_ge(n_lo_p, 8)
                    read_tile(v.tensor_tensor(two(hmul[k % 2][:]), two(sg[k % 2][:]), acc(t), ALU.mult), t)
                    if f >= 1:
                        lower(act_lo[:, f - 1, :], k - 1, act_hi[:, f - 1, :], f_hi, f_lo)
                    k += 1
                lower(act_lo[:, fn - 1, :], k - 1, act_hi[:, fn - 1, :], f_hi, f_lo)
                for j in range(DC):
                    t = t0 + 2 * fn + j
                    got_tile(dve, t)
                    read_tile(v.tensor_tensor(two(x[:, j, :]), two(x[:, j, :]), acc(t), ALU.add), t)
                    if half and j >= 1:
                        add_square(1, j - 1)
            add_square(1, DC - 1)
            row_factor(("ss2a", "ss2b"))
            dve.wait_ge(rb_a, 2)
            norm(2, R_PLE, rb[:])
            for j in range(DC):
                t = FIRST_TILE["pg"] + j
                got_tile(dve, t)
                tile_is_read(dve, "pg", j)
                tile_is_read(dve, "pp", j)
                if j == 1:
                    dve.wait_ge(n_lo_p, 12)
                elif j >= 2:
                    dve.wait_ge(xn_ok, j - 1)
                link(v.scalar_tensor_tensor(hmul[j % 2][:], sg[j % 2][:], 1.0, pp[:, j, :], ALU.add, ALU.mult))
                v.scalar_tensor_tensor(x[:, j, :], hmul[j % 2][:], 0.5, x[:, j, :], ALU.mult, ALU.add)\
                    .then_inc(xn_ok, 1)
                if j >= 1:
                    add_square(2, j - 1)
            add_square(2, DC - 1)
            got_job(dve, "ss3")
            link(v.memset(stat[:, 40 + TT:41 + TT], float(D)))
            ins = v.tensor_copy(stat[:, 40:40 + TT], bank("ss3")[:, 0:TT])
            link(ins)
            ins = v.tensor_copy(stat[0:NS, 40 + TT:41 + TT], bank("ss3")[0:NS, TT:TT + 1])
            read_job(ins, "ss3")
            job_read(dve, "ss3")
            inverse_mean(stat[:, 40:40 + TT + 1], stat[:, 40:40 + TT + 1]).then_inc(fs_v, 1)
            dve.wait_ge(fs_a, 1)
            for t in range(TT + 1):
                rows = P if t < TT else NS
                job = ("y", t, 1)
                got_job(dve, job)
                read_job(v.tensor_scalar(ytok[0:rows, t, 512:D], bank(job)[0:rows, :], stat[0:rows, 48 + t:49 + t],
                                         None, ALU.mult), job)

        @block.gpsimd
        def _(pool):
            g_ = nc.gpsimd
            steps = [0]

            def link(ins):
                steps[0] += 1
                ins.then_inc(pool_step, 1)
                pool.wait_ge(pool_step, steps[0])

            def lower_weights(n):
                if n >= len(UNITS):
                    return
                _, _, (_, _, rc, _, cc, _, _) = UNITS[n]
                s = n % RING
                pool.wait_ge(w_hi, n + 1)
                g_.tensor_tensor(wlo[:, s, 0:rc, 0:cc], wraw[:, s, 0:rc, 0:cc], whi[:, s, 0:rc, 0:cc].bitcast(F32),
                                 ALU.subtract).then_inc(w_lo, 1)

            def norm_lo(k, c):
                pool.wait_ge(n_hi, DC * k + c + 1)
                g_.tensor_tensor(h_lo[:, c, :], hmul[c % 2][:], h_hi[:, c, :].bitcast(F32), ALU.subtract)\
                    .then_inc(n_lo_p, 1)

            def causal(ap, fill):
                return g_.affine_select(out=ap, in_=ap, compare_op=ALU.is_ge, fill=fill, base=0,
                                        pattern=[[-1, P]], channel_multiplier=1)

            def own_new_keys(ap, fill):
                v = ap.rearrange("p (b j) -> p b j", j=NJ)
                link(g_.affine_select(out=v, in_=v, compare_op=ALU.is_ge, fill=fill, base=0,
                                      pattern=[[-NJ, NB], [-1, NJ]], channel_multiplier=1))
                return g_.affine_select(out=v, in_=v, compare_op=ALU.is_ge, fill=fill, base=NJ - 1,
                                        pattern=[[NJ, NB], [0, NJ]], channel_multiplier=-1)

            link(g_.memset(ident[:], 0.0))
            g_.affine_select(out=ident[:], in_=ident[:], compare_op=ALU.not_equal, fill=1.0, base=0,
                             pattern=[[-1, P]], channel_multiplier=1).then_inc(ident_ok, 1)
            g_.memset(stat[:], 1.0).then_inc(pool_const, 1)
            g_.memset(iwtok[:], 0.0).then_inc(ident_ok, 1)
            link(g_.memset(mask0[:], 0.0))
            link(causal(mask0[:], OFF))
            for c in range(DC):
                if c < RING:
                    lower_weights(c)
                if c % 2:
                    norm_lo(0, c)
            job_read(pool, ("x", DC - 2))
            job_read(pool, ("x", DC - 1))
            link(g_.memset(sel[:], 0.0))
            v = sel[:].rearrange("p g (b h j) -> p (g b) h j", b=NB // 2, h=NH)
            link(g_.affine_select(out=v, in_=v, compare_op=ALU.not_equal, fill=1.0, base=0,
                                  pattern=[[-NJ, NB], [0, NH], [-1, NJ]], channel_multiplier=1))
            link(g_.memset(hm[:], 1.0))
            link(g_.affine_select(out=hm[:], in_=hm[:], compare_op=ALU.is_ge, fill=0.0, base=0,
                                  pattern=[[-NS, NB // 2], [-NJ, NH]], channel_multiplier=1))
            g_.affine_select(out=hm[:], in_=hm[:], compare_op=ALU.is_ge, fill=0.0, base=NJ - 1,
                             pattern=[[NS, NB // 2], [NJ, NH]], channel_multiplier=-1).then_inc(pool_const, 1)
            for n in range(len(UNITS)):
                if n == U["iq"] + HP - 1:
                    all_read(pool, "iq", HP)
                    pool.wait_ge(n_t, DC)
                    link(g_.memset(iqbd[:], 0.0))
                    for h in range(2):
                        rows = slice(HD * h, HD * (h + 1))
                        dst = iqbd[rows].rearrange("p b (m h j) -> p b m h j", h=2, j=NJ)[:, :, :, h, :]
                        src = iqT[rows, :, SEQ:T].rearrange("p m (b j) -> p b m j", j=NJ)
                        for m in range(HP):
                            g_.tensor_copy(dst[:, :, m, :], src[:, :, m, :]).then_inc(iqbd_ok, 1)
                        pool.wait_ge(iqbd_ok, HP * (h + 1))
                if n == U["xr"]:
                    job_read(pool, ("vout", TT))
                    for s in range(2):
                        ins = g_.memset(xe[s][:, 0:CW - 1], 0.0)
                        if s:
                            ins.then_inc(bd_zero, 1)
                        else:
                            link(ins)
                if n - U["pp"] in range(1, DC, 2):
                    norm_lo(1, n - U["pp"])
                lower_weights(n + RING)
                if n == U["q"] + HP:
                    for i in range(1, TT):
                        pool.wait_ge(idx_acc, NH * i)
                        causal(score[i][:, P * i:P * (i + 1)], MASKED).then_inc(masked_in, 1)
                    pool.wait_ge(ss_copied, 1)
                    job_read(pool, "sidx")
                    own_new_keys(score_s[:, PAST:SK], MASKED).then_inc(masked_in, 1)
                    pool.wait_ge(masked_in, TT)
                if n == U["q"] + HP + 1:
                    all_read(pool, "q", HP)
                    job_read(pool, ("iks", 3))
                    pool.wait_ge(sdots, 1)
                    link(g_.memset(qbd[:], 0.0))
                    for h in range(2):
                        rows = slice(HD * h, HD * (h + 1))
                        for m in range(HP):
                            c0 = NJ * (2 * m + h)
                            g_.tensor_copy(qbd[rows, :, m, c0:c0 + NJ],
                                           qT[rows, m, SEQ:T].rearrange("p (b j) -> p b j", j=NJ)).then_inc(qbd_ok, 1)
                        pool.wait_ge(qbd_ok, HP * (h + 1))
                    job_read(pool, ("idx", NH * (TT - 1) - 1))
                    g_.memset(bd[:], 0.0).then_inc(bd_zero, 1)
                if n == U["k"] + HP - 1:
                    pool.wait_ge(topk_ok, 1)
                    own_new_keys(score_s[:, PAST:SK], OFF).then_inc(mask_ok, 1)
                    pool.wait_ge(mask_ok, 1)
                if n == U["ga"] - 3:
                    for i in range(1, TT):
                        pool.wait_ge(topk_ok, 1 + i)
                        causal(score[i][:, P * i:P * (i + 1)], OFF).then_inc(mask_ok, 1)
                if U["ga"] <= n < U["gb"]:
                    for s in (2 * (n - U["ga"]), 2 * (n - U["ga"]) + 1):
                        h, i = s // TT, s % TT
                        w = P * (i + 1)
                        if i == 0:
                            pool.wait_ge(th_in[h % 2], 16 * (h // 2 + 1))
                        if s == 0:
                            pool.wait_ge(mask_ok, TT)
                        if s >= 2:
                            job_read(pool, ("qk", s - 2))
                        m = mask0 if i == 0 else score[i]
                        g_.tensor_tensor(tm[s % 2][:, 0:w], th[h % 2][:, SEQ - w:SEQ], m[:], ALU.add).then_inc(tm_ok, 1)
                if n == U["pg"] - 1:
                    for c in range(1, DC, 2):
                        norm_lo(2, c)

        @block.tensor
        def _(pe):
            te = nc.tensor

            def start_job(job):
                n = AUX[job]
                if n >= 2:
                    pe.wait_ge(aux_read[n % 2], n // 2)
                return bank(job)

            def end_job(ins):
                return ins.then_inc(aux_done, 1)

            def turn(out, src):
                rows = src.shape[0]
                return te.transpose(out, src, ident[0:rows, 0:rows])

            operands = {"h": (h_hi, h_lo), "y": (act_hi, act_lo), "m": (act_hi, act_lo), "f": (act_hi, act_lo),
                        "p": (p_hi, p_lo)}

            def wait_operand(n, c):
                kind = TILES[UNITS[n][0]][0]
                firsts = (0, FIRST[("gate", 0)], U["pg"])
                if n in firsts:
                    k = firsts.index(n)
                    if c % 2:
                        pe.wait_ge(n_lo_p, 4 * k + c // 2 + 1)
                    else:
                        pe.wait_ge(n_lo_v, 4 * k + c // 2 + 1)
                elif n == U["ga"] + 1:
                    pe.wait_ge(y_lo, c + 1)
                elif n == U["gb"] + 1:
                    pe.wait_ge(o_lo, c + 1)
                    pe.wait_ge(so_lo, 2 * HP)
                elif n == U["wo"]:
                    pe.wait_ge(m_lo, c + 1)
                elif n == U["pp"]:
                    job_read(pe, ("p", TT - 1))
                    job_read(pe, ("p", TT))
                elif n in (FIRST[("down", 0, False)], FIRST[("down", 0, False)] + 1):
                    pe.wait_ge(f_lo, c + 1)
                elif n in (FIRST[("down", 0, True)], FIRST[("down", 0, True)] + 1):
                    pe.wait_ge(f_lo, FA + c + 1)

            def run(n):
                t, part, (_, _, rc, _, cc, operand, k0) = UNITS[n]
                parts = len(TILES[t][2])
                s = n % RING
                if part == 0 and t >= 2:
                    pe.wait_ge(tile_read[t % 2], t // 2)
                pe.wait_ge(w_lo, n + 1)
                b0 = 2 * (t % 2)
                if operand == "o":
                    hi, lo = act_hi[:, 8:FA, :], act_lo[:, 8:FA, :]
                else:
                    hi, lo = operands[operand][0][:], operands[operand][1][:]
                for c in range(rc):
                    wait_operand(n, k0 + c)
                    for w, m in ((whi, hi), (whi, lo), (wlo, hi)):
                        for half in range(2):
                            ins = te.matmul(psD[0:cc, b0 + half, 0:HT], w[:, s, c, 0:cc],
                                            m[:, k0 + c, HT * half:HT * (half + 1)],
                                            start=(part == 0 and c == 0 and w is whi and m is hi),
                                            stop=(part == parts - 1 and c == rc - 1 and w is wlo))
                ins.then_inc(w_used, 1)

            def x_chunk(c):
                x_bank = start_job(("x", c))
                if c == 0:
                    for t in range(TT):
                        pe.wait_ge(x_in[t], 16)
                for t in range(TT):
                    ins = turn(x_bank[:, P * t:P * (t + 1)], xtok[:, t, P * c:P * (c + 1)])
                end_job(ins)

            pe.wait_ge(ident_ok, 1)
            pe.wait_ge(prm_in, 16 * 11)
            b = start_job("prm")
            for c in range(DC):
                ins = turn(b[:, NR * c:NR * (c + 1)], prm[:, P * c:P * (c + 1)])
            end_job(ins)
            b = start_job("xs")
            pe.wait_ge(x_in[TT], 16)
            for c in range(DC):
                ins = turn(b[:, NS * c:NS * (c + 1)], xtok[0:NS, TT, P * c:P * (c + 1)])
            end_job(ins)
            for c in range(4):
                x_chunk(c)
            b = start_job("rstd_a")
            pe.wait_ge(ones_ok, 1)
            pe.wait_ge(diag_ok, 2)
            for t in range(TT):
                ins = te.matmul(b[:, P * t:P * (t + 1)], ones[:], diag[:, t, :], start=True, stop=True)
            end_job(ins)
            b = start_job("rstd_b")
            end_job(te.matmul(b[:, 0:NS], ones[0:NS, :], diag[0:NS, TT, 0:NS], start=True, stop=True))
            for c in range(4, DC):
                x_chunk(c)
            run(0)
            pe.wait_ge(idxp_in, 16 * 2 * NB * NPG)
            for n in range(4):
                b = start_job(("iks", n))
                for k in range(4):
                    ins = turn(b[:, P * k:P * (k + 1)], idxp[:, 4 * n + k].rearrange("p r d -> p (r d)"))
                end_job(ins)
            pe.wait_ge(small_in, 32)
            w = LW // 2
            for k, job in enumerate(("lines_a", "lines_b")):
                b = start_job(job)
                end_job(te.matmul(b[0:NH, 0:w], relb[:], onehot[:, w * k:w * (k + 1)], start=True, stop=True))
            b = start_job("selT")
            pe.wait_ge(pool_const, 2)
            for g in range(2):
                ins = turn(b[:, NS * g:NS * (g + 1)], sel[:, g, :])
            end_job(ins)
            for n in range(1, U["q"]):
                run(n)
            b = start_job("ik")
            tile_is_read(pe, "ik", 0)
            kw = HD + NH
            for t in range(TT + 1):
                c0, c1 = (P * t, P * (t + 1)) if t < TT else (SEQ, T)
                ins = turn(b[0:c1 - c0, kw * t:kw * (t + 1)], ikw[0:kw, c0:c1])
            end_job(ins)

            def head_rows(h):
                return slice(HD * (h % 2), HD * (h % 2) + HD)

            def index_dots(s):
                i, h = 1 + s // NH, s % NH
                job = ("idx", s)
                b = start_job(job)
                end_job(te.matmul(b[:, 0:P * (i + 1)], iqT[head_rows(h), h // 2, P * i:P * (i + 1)],
                                  ik2[head_rows(h), 0:P * (i + 1)], start=True, stop=True))

            pe.wait_ge(ik_dup, 16)
            for j in range(HP):
                run(U["q"] + j)
                for s in range(6 * j, 6 * j + 6):
                    index_dots(s)

            pe.wait_ge(iwcol_ok, 1)
            job_read(pe, "selT")
            b = start_job("iwcol")
            for g in range(2):
                ins = te.matmul(b[:, NH * g:NH * (g + 1)], sel[:, g, :], iwtok[0:NS, TT, :], start=True, stop=True)
            end_job(ins)
            pe.wait_ge(iqbd_ok, 2 * HP)
            job_read(pe, ("iks", 2))
            job_read(pe, ("iks", 3))
            for q in range(NB):
                rows = slice(NS * (q % 4), NS * (q % 4) + NS)
                out = psX[2 + q // 4]
                te.matmul(out[rows, 0:PAST], iqbd[:, q, :], iks[:, q, :], start=True, stop=True,
                          tile_position=(0, NS * (q % 4)))
                ins = te.matmul(out[rows, PAST:SK], iqbd[:, q, :], ik2[:, SEQ:T], start=True, stop=True,
                                tile_position=(0, NS * (q % 4)))
            ins.then_inc(sdots, 1)
            run(U["k"])
            b = start_job("sidx")
            pe.wait_ge(rs_ok, 2)
            for g in range(2):
                ins = te.matmul(b[0:NS, 0:SK], selT[:, g, :], rs_s[:, g, :], start=(g == 0), stop=(g == 1))
            end_job(ins)
            for n in range(U["k"] + 1, U["v"] + 1):
                run(n)
            all_read(pe, "k", HP)
            for t in range(TT + 1):
                c0, c1 = (P * t, P * (t + 1)) if t < TT else (SEQ, T)
                b = start_job(("kout", t))
                for m in range(HP):
                    ins = turn(b[0:c1 - c0, P * m:P * (m + 1)], kT[:, m, c0:c1])
                end_job(ins)

            def past_logits(q):
                pe.wait_ge(kpg_in[q % 2], 16 * NPG * (q // 2 + 1))
                for g in range(NPG):
                    b = start_job(("kts", q, g))
                    for m in range(HP):
                        ins = turn(b[:, PG * m:PG * (m + 1)], kpg[q % 2][:, g, P * m:P * (m + 1)])
                    end_job(ins)
                if q == 0:
                    pe.wait_ge(qbd_ok, 2 * HP)
                job_read(pe, ("kts", q, 0))
                job_read(pe, ("kts", q, 1))
                rows = slice(NS * (q % 4), NS * (q % 4) + NS)
                out = psX[2 + q // 4]
                for m in range(HP):
                    te.matmul(out[rows, 0:PAST], qbd[:, q, m, :], kts[q % 2][:, m, :], start=(m == 0),
                              stop=(m == HP - 1), tile_position=(0, NS * (q % 4)))
                for m in range(HP):
                    ins = te.matmul(out[rows, PAST:SK], qbd[:, q, m, :], kT[:, m, SEQ:T], start=(m == 0),
                                    stop=(m == HP - 1), tile_position=(0, NS * (q % 4)))
                ins.then_inc(slogit_b, 1)

            for j in range(1, HP):
                run(U["v"] + j)
                past_logits(2 * j - 2)
                past_logits(2 * j - 1)
            run(U["xr"])
            past_logits(6)
            past_logits(7)
            all_read(pe, "v", HP)
            for t in range(TT + 1):
                c0, c1 = (P * t, P * (t + 1)) if t < TT else (SEQ, T)
                b = start_job(("vout", t))
                for m in range(HP):
                    ins = turn(b[0:c1 - c0, P * m:P * (m + 1)], vT[:, m, c0:c1])
                end_job(ins)

            def gate_sums(c):
                for g in range(2):
                    for k in range(2):
                        b = start_job(("gate", c, g, k))
                        if g == 0 and k == 0:
                            pe.wait_ge(xc_ok, c + 1)
                            if c == 0:
                                pe.wait_ge(bd_in, 64)
                        end_job(te.matmul(b[:, 0:EH], bd[:, c, g, :], xc[c % 2][:, EH * k:EH * (k + 1)],
                                          start=True, stop=True))

            def past_values(q):
                pe.wait_ge(kpg_in[q % 2], 16 * NPG * (NB // 2 + q // 2 + 1))
                g, r = q // 4, q % 4
                for m in range(HP):
                    out = psX[2][:, 64 * m + 8 * q:64 * m + 8 * q + 8]
                    c0 = NS * r + 8 * m
                    for k in range(NPG):
                        te.matmul(out, kpg[q % 2][:, k, P * m:P * (m + 1)], pts[:, k, g, c0:c0 + 8],
                                  start=(k == 0), stop=False)
                    ins = te.matmul(out, vtok_s[:, P * m:P * (m + 1)], ptn[:, g, c0:c0 + 8], start=False, stop=True)
                ins.then_inc(spv_b, 1)

            for n in range(U["xr"] + 1, U["ga"]):
                run(n)
                k = n - U["xr"]
                if k == 1:
                    pe.wait_ge(mask_ok, 1)
                    for g in range(2):
                        b = start_job(("smask", g))
                        end_job(te.matmul(b[:, 0:SK], sel[:, g, :], score_s[:, 0:SK], start=True, stop=True))
                if k % 2:
                    gate_sums(k // 2)
                if k == 2:
                    b = start_job("spt")
                    pe.wait_ge(sp_ok, 2)
                    for kk in range(NPG):
                        for g in range(2):
                            ins = turn(b[:, P * (2 * kk + g):P * (2 * kk + g + 1)], ps_s[:, g, PG * kk:PG * (kk + 1)])
                    end_job(ins)
                    b = start_job("spn")
                    for g in range(2):
                        ins = turn(b[0:NS, P * g:P * (g + 1)], ps_s[:, g, PAST:SK])
                    end_job(ins)
                if 3 <= k < 3 + NB:
                    if k == 3:
                        job_read(pe, "spt")
                        job_read(pe, "spn")
                        job_read(pe, ("vout", TT))
                    past_values(k - 3)

            def attend_products(s):
                h, i = s // TT, s % TT
                w = P * (i + 1)
                b = start_job(("qk", s))
                end_job(te.matmul(b[:, 0:w], qT[head_rows(h), h // 2, P * i:w], kT[head_rows(h), h // 2, 0:w],
                                  start=True, stop=True))

            def attend_turn(s):
                i = s % TT
                pe.wait_ge(p_ok, s + 1)
                if s == 0:
                    pe.wait_ge(so_lo, 2 * HP)
                else:
                    pe.wait_ge(pT_ok, s)
                for k in range(i + 1):
                    ins = turn(psX[2][:, P * k:P * (k + 1)], pr[s % 2][:, P * k:P * (k + 1)])
                ins.then_inc(tr_done, 1)

            def attend_values(s):
                h, i = s // TT, s % TT
                pe.wait_ge(pT_ok, s + 1)
                if s == 0:
                    job_read(pe, ("smask", 1))
                elif s % (2 * TT) == 0:
                    pe.wait_ge(o_lo, s // (2 * TT))
                for k in range(i + 1):
                    ins = te.matmul(psX[3][head_rows(h), P * i:P * (i + 1)], vtok[:, k, HD * h:HD * (h + 1)],
                                    pT[s % 2][:, k, :], start=(k == 0), stop=(k == i),
                                    tile_position=(0, HD * (h % 2)))
                ins.then_inc(pv_done, 1)

            for n in range(U["ga"], U["gb"]):
                run(n)
                if n == U["ga"]:
                    pe.wait_ge(yt_ok, DC)
                    for k, job in enumerate(("st_a", "st_b")):
                        b = start_job(job)
                        for c in range(4):
                            ins = turn(b[0:NC, P * c:P * (c + 1)], stO[:, 4 * k + c, :])
                        end_job(ins)
                last = n == U["gb"] - 1
                s0 = 2 * (n - U["ga"])
                for s in range(s0, s0 + (4 if last else 2)):
                    if s < STEPS:
                        attend_products(s)
                    if 1 <= s <= STEPS:
                        attend_turn(s - 1)
                    if 2 <= s <= STEPS + 1:
                        attend_values(s - 2)

            for n in range(U["gb"], U["wo"]):
                run(n)
                k = n - U["gb"]
                if k >= 2 and k % 2 == 0 and k // 2 - 1 <= TT:
                    t = k // 2 - 1
                    c0, c1 = (P * t, P * (t + 1)) if t < TT else (SEQ, T)
                    w = c1 - c0
                    b = start_job(("p", t))
                    pe.wait_ge(p_in, 32)
                    for kk in range(2):
                        ins = turn(b[:, w * kk:w * (kk + 1)], ptok[0:w, t, P * kk:P * (kk + 1)])
                    end_job(ins)

            def sum_squares(k, jobs):
                pe.wait_ge(sqacc_ok, DC * (k + 1))
                for half, job in enumerate(jobs):
                    b = start_job(job)
                    end_job(te.matmul(b[:, 0:HT], ones[:], sqacc[:, HT * half:HT * (half + 1)], start=True, stop=True))

            for n in range(U["wo"], U["pp"]):
                run(n)
            sum_squares(0, ("ss1a", "ss1b"))
            for n in range(U["pp"], U["pg"]):
                run(n)
            sum_squares(1, ("ss2a", "ss2b"))
            for n in range(U["pg"], len(UNITS)):
                run(n)
            b = start_job("ss3")
            pe.wait_ge(sqacc_ok, 3 * DC)
            for t in range(TT + 1):
                c0, c1 = (P * t, P * (t + 1)) if t < TT else (SEQ, T)
                ins = te.matmul(b[0:c1 - c0, t:t + 1], sqacc[:, c0:c1], ones[:, 0:1], start=True, stop=True)
            end_job(ins)
            pe.wait_ge(xf_ok, DC)
            for t in range(TT + 1):
                c0, c1 = (P * t, P * (t + 1)) if t < TT else (SEQ, T)
                for half in range(2):
                    b = start_job(("y", t, half))
                    for c in range(4):
                        ins = turn(b[0:c1 - c0, P * c:P * (c + 1)], pp[:, 4 * half + c, c0:c1])
                    end_job(ins)


_INS = ["x_prompt", "x_sample", "p_prompt", "p_sample", "cache_k", "cache_v", "cache_idx_k", "state_rglru_h",
        "state_conv", "page_table", "rel_bias", "norm_mix", "w_in", "conv_w", "conv_b", "w_rg_a", "b_rg_a",
        "w_rg_x", "b_rg_x", "lru_lambda", "w_rnn_out", "w_att_out", "w_o", "norm_ffn", "w_ffn_gate", "w_ffn_up",
        "w_ffn_down", "norm_ple", "w_ple_gate", "w_ple_proj", "norm_final"]
_OUTS = [("y_prompt", (1, SEQ, D)), ("y_sample", (NB, NJ, D)), ("k_prompt", (1, 1, SEQ, NH, HD)),
         ("v_prompt", (1, 1, SEQ, NH, HD)), ("idx_k_prompt", (1, 1, SEQ, HD)), ("h_prompt", (1, 1, D)),
         ("conv_prompt", (1, 1, CW - 1, D)), ("k_sample", (1, NB, NJ, NH, HD)), ("v_sample", (1, NB, NJ, NH, HD)),
         ("idx_k_sample", (1, NB, NJ, HD)), ("h_sample", (1, NB, D)), ("conv_sample", (1, NB, CW - 1, D))]


def kernel(**inputs):
    import numpy as _np
    import concourse.bacc as _bacc
    from concourse import mybir as _mybir
    from concourse.bass_utils import run_bass_kernel_spmd as _run

    nc = _bacc.Bacc("TRN2", target_bir_lowering=False, num_devices=1)
    arrays, ins, outs = {}, {}, {}
    held = {name: _np.ascontiguousarray(inputs[name]) for name in _INS}
    held["bias_onehot"] = bias_onehot()
    for name, array in held.items():
        arrays[f"in_{name}"] = array
        ins[name] = nc.dram_tensor(f"in_{name}", array.shape, _mybir.dt.from_np(array.dtype),
                                   kind="ExternalInput").ap()
    for name, shape in _OUTS:
        outs[name] = nc.dram_tensor(f"out_{name}", shape, _mybir.dt.float32, kind="ExternalOutput").ap()
    hybrid_decoder_step(nc, ins, outs)
    r = _run(nc, [arrays], core_ids=[0])
    return tuple(r.results[0][f"out_{name}"] for name, _ in _OUTS)
```

```python
from contextlib import ExitStack

import numpy as np

import concourse.bass as bass
from concourse import mybir

F32 = mybir.dt.float32
F32R = mybir.dt.float32r
I32 = mybir.dt.int32
ALU = mybir.AluOpType
ACT = mybir.ActivationFunctionType

P = 128
D = 1024
DC = D // P
SEQ = 512
NB = 8
NJ = 4
NS = NB * NJ
T = SEQ + NS
HT = T // 2
TT = SEQ // P
NH = 8
HD = 64
ATT = NH * HD
HP = NH // 2
PG = 128
NPG = 2
PAST = NPG * PG
SK = PAST + NS
DFF = 2816
FC = DFF // P
PD = 256
EPS = 1e-6
TOPK_P = SEQ // 4
TOPK_S = (PAST + NJ) // 4
NBUCK = 32
LW = 640
LMAX = 511
MASKED = -3.0e38
TAKEN = -3.4e38
TAKEN_BELOW = -3.3e38
PAD = -3.2e38
OFF = -1.0e30
RING = 4
UC = 8
CW = 4
EXT = CW - 1 + SEQ + NB * (CW - 1 + NJ)
EO = EXT - (CW - 1)
EH = EO // 2
S0 = SEQ + CW - 1
ST = CW - 1 + NJ
FA = 12
FFN_HALVES = ((0, FA), (FA, FC - FA))

R_MIX, R_FFN, R_PLE, R_FIN, R_CW, R_CB, R_BA, R_BX, R_LAM, R_SC, R_SH = 0, 1, 2, 3, 4, 8, 9, 10, 11, 12, 36
NR = 44
C_CP, C_CS, C_HP, C_HS, NC = 0, 3, 27, 28, 36

W_AT = dict(xr=0, gr=D, q=2 * D, k=2 * D + ATT, v=2 * D + 2 * ATT, iq=2 * D + 3 * ATT,
            ik=2 * D + 4 * ATT, ga=2 * D + 4 * ATT + HD + NH, gb=3 * D + 4 * ATT + HD + NH)


def plan_tiles():
    def w_in(kind, j, cols=P):
        return (kind, j, [("w_in", 0, DC, W_AT[kind] + P * j, cols, "h", 0)])

    def square(kind, j, weight, operand, chunks=DC):
        return (kind, j, [(weight, 0, chunks, P * j, P, operand, 0)])

    tiles = [w_in("iq", j) for j in range(HP)] + [w_in("ik", 0, HD + NH)]
    for kind in ("q", "k", "v"):
        tiles += [w_in(kind, j) for j in range(HP)]
    tiles.append(w_in("xr", 0))
    for c in range(DC):
        tiles += [w_in("xr", c + 1)] * (c + 1 < DC) + [w_in("gr", c)]
    for j in range(DC):
        tiles += [w_in("ga", j), square("rnn", j, "w_rnn_out", "y")]
    for j in range(DC):
        tiles += [w_in("gb", j), square("att", j, "w_att_out", "o", HP)]
    tiles += [square("wo", j, "w_o", "m") for j in range(DC)]
    pp = [square("pp", j, "w_ple_proj", "p", PD // P) for j in range(DC)]
    tiles += pp[0:DC // 2]
    for f0, fn in FFN_HALVES:
        for f in range(f0, f0 + fn):
            tiles += [square("gate", f, "w_ffn_gate", "h"), square("up", f, "w_ffn_up", "h")]
        half = fn // 2
        for j in range(DC):
            tiles.append(("down", j, [("w_ffn_down", f0 + half * k, half, P * j, P, "f", half * k)
                                      for k in range(2)]))
    tiles += pp[DC // 2:]
    tiles += [square("pg", j, "w_ple_gate", "h") for j in range(DC)]
    return tiles


TILES = plan_tiles()
UNITS = [(t, k, u) for t, (_, _, us) in enumerate(TILES) for k, u in enumerate(us)]
FIRST = {}
for _n, (_t, _k, _u) in enumerate(UNITS):
    FIRST.setdefault(TILES[_t][:2] if TILES[_t][0] != "down" else ("down", TILES[_t][1], UNITS[_n][2][1] >= FA), _n)
FIRST_TILE = {}
for _t, (_k, _j, _u) in enumerate(TILES):
    FIRST_TILE.setdefault(_k, _t)
NTH = {}
for _t, (_k, _j, _u) in enumerate(TILES):
    NTH[(_k, _j, _k == "down" and _u[0][1] >= FA)] = _t
LAST_UNIT = {t: n for n, (t, _, _) in enumerate(UNITS)}
STEPS = NH * TT
OROW_CHUNK = 5


def plan_aux():
    jobs = ["prm", "xs", ("x", 0), ("x", 1), "rstd_a", "rstd_b"] + [("x", c) for c in range(2, DC)]
    jobs += [("iks", n) for n in range(4)] + ["lines_a", "lines_b", "selT"]
    jobs += ["ik"] + [("idx", s) for s in range(NH * (TT - 1))] + ["iwcol", "sidx"]
    jobs += [("kout", t) for t in range(TT + 1)]
    for b in range(NB - 1):
        jobs += [("kts", b, 0), ("kts", b, 1)]
    jobs += [("vout", 0), ("vout", 1), ("kts", NB - 1, 0), ("kts", NB - 1, 1), ("vout", 2), ("vout", 3), ("vout", TT)]
    jobs += [("smask", 0), ("smask", 1)]
    for c in range(DC):
        jobs += [("gate", c, 0, 0), ("gate", c, 0, 1), ("gate", c, 1, 0), ("gate", c, 1, 1)]
        if c == 0:
            jobs += ["spt", "spn"]
    for s in range(STEPS):
        jobs.append(("qk", s))
        if s == 3:
            jobs += ["st_a", "st_b"]
    jobs += [("p", t) for t in range(TT + 1)]
    jobs += ["ss1a", "ss1b", "ss2a", "ss2b", "ss3"]
    for t in range(TT + 1):
        jobs += [("y", t, 0), ("y", t, 1)]
    return jobs


AUX = {name: n for n, name in enumerate(plan_aux())}


def bias_onehot():
    n = np.maximum(LMAX - np.arange(LW), 0)
    exact = NBUCK // 2
    nf = np.maximum(n, 1).astype(np.float32)
    large = exact + (np.log(nf / np.float32(exact)) / np.float32(np.log(128 / exact))
                     * np.float32(NBUCK - exact)).astype(np.int32)
    bucket = np.where(n < exact, n, np.minimum(large, NBUCK - 1))
    return (np.arange(NBUCK)[:, None] == bucket[None, :]).astype(np.float32)


def hybrid_decoder_step(nc, a, o):
    n_pool = a["cache_k"].shape[1]
    free = [16512]
    spot = {}

    def place(name, shape, dt=F32, over=None, plus=0):
        size = 4 * int(np.prod(shape[1:]))
        if over is None:
            spot[name] = free[0]
            free[0] += (size + 31) // 32 * 32
        else:
            spot[name] = spot[over] + plus
        assert spot[name] + size <= 229344, (name, spot[name] + size - 229344)
        return nc.alloc_sbuf_tensor_at(name, shape, dt, offset=spot[name])

    wraw = place("wraw", [P, RING, UC, P])
    whi = place("whi", [P, RING, UC, P], F32R)
    wlo = place("wlo", [P, RING, UC, P], F32R)
    h_hi = place("h_hi", [P, DC, T], F32R)
    h_lo = place("h_lo", [P, DC, T], F32R)
    act_hi = place("act_hi", [P, FA, T], F32R)
    act_lo = place("act_lo", [P, FA, T], F32R)
    x = place("x", [P, DC, T])
    qT = place("qT", [P, HP, T])
    kT = place("kT", [P, HP, T])
    vtok = place("vtok", [P, TT, ATT])
    iqT = place("iqT", [P, HP, T])
    ikw = place("ikw", [P, T])
    ik2 = place("ik2", [P, T])
    score = [None] + [place(f"score{i}", [P, P * (i + 1)]) for i in range(1, TT)]
    score_s = place("score_s", [NS, SK + 8])
    mask0 = place("mask0", [P, P])
    ident = place("ident", [P, P])
    ones = place("ones", [P, P])
    prmT = place("prmT", [P, DC, NR])
    iwtok = place("iwtok", [P, TT + 1, NH])
    vtok_s = place("vtok_s", [NS, ATT])
    lru = place("lru", [P, 8, DC])
    stat = place("stat", [P, 64])
    sstat = place("sstat", [P, 8])
    top8 = place("top8", [P, 8])
    pt = place("pt", [1, NB * NPG], I32)
    hmul = [place(f"hmul{i}", [P, T]) for i in range(2)]
    tail = place("tail", [P, 1120])
    nbuf = hmul + [place(f"nbuf{i}", [P, T], F32, "tail", 4 * T * i) for i in range(2)]
    xtok = place("xtok", [P, TT + 1, D], F32, "act_hi")
    rb0 = place("rb0", [P, T], F32, "act_hi", 20480)
    lines = place("lines", [NH, LW], F32, "act_hi", 22656)
    idxp = place("idxp", [P, NB * NPG, 2, HD], F32, "act_lo")
    iks = place("iks", [P, NB, PAST], F32, "act_lo", 8192)
    prm = place("prm", [NR, D], F32, "act_lo", 17408)
    onehot = place("onehot", [NBUCK, LW], F32, "act_lo", 21504)
    relb = place("relb", [NBUCK, NH], F32, "act_lo", 24064)
    junk = place("junk", [P, D], F32, "iqT")
    diag = place("diag", [P, TT + 1, P], F32, "iqT", 4096)
    relu = [place(f"relu{i}", [P, SEQ], F32, "act_lo", 17920 + 2048 * i) for i in range(2)]
    iqbd = place("iqbd", [P, NB, NS], F32, "act_hi")
    rs_s = place("rs_s", [P, 2, SK], F32, "act_hi", 4096)
    sel = place("sel", [NS, 2, P], F32, "act_hi", 6400)
    selT = place("selT", [P, 2, NS], F32, "act_hi", 7424)
    hm = place("hm", [P, NB // 2, NH], F32, "act_hi", 7680)
    iwsc = place("iwsc", [P, NB // 2, NH], F32, "act_hi", 7808)
    iktok = place("iktok", [P, TT + 1, HD + NH], F32, "act_hi", 7936)
    vT = place("vT", [P, HP, T], F32, "x", 4 * T * (DC - HP))
    ktok = [place(f"ktok{i}", [P, ATT], F32, "act_lo", 2048 * i) for i in range(2)]
    kpg = [place(f"kpg{i}", [P, NPG, ATT], F32, "act_hi", 17408 + 4096 * i) for i in range(2)]
    kts = [place(f"kts{i}", [P, HP, PAST], F32, "act_lo", 17920 + 4096 * i) for i in range(2)]
    pts = place("pts", [P, NPG, 2, P], F32, "act_lo", 12032)
    ptn = place("ptn", [NS, 2, P], F32, "act_lo", 14080)
    ps_s = place("ps_s", [P, 2, SK], F32, "act_lo", 15104)
    qbd = place("qbd", [P, NB, HP, NS], F32, "act_hi", 13312)
    bias_s = place("bias_s", [P, SK], F32, "ikw")
    bias_n = place("bias_n", [P, NJ], F32, "ikw", 1152)
    bd = place("bd", [P, DC, 2, P], F32, "iqT")
    line = 4 * (EXT + 5)
    xe = [place(f"xe{i}", [P, EXT], F32, "x", line * i) for i in range(2)]
    xc = [place(f"xc{i}", [P, EO], F32, "x", line * (2 + i)) for i in range(2)]
    rq = place("rq", [P, EO], F32, "x", line * 4)
    ig = place("ig", [P, EO], F32, "x", line * 5)
    sq = place("sq", [P, EO], F32, "x", line * 6)
    stO = place("stO", [P, DC, NC], F32, "x", line * 7)
    hs = place("hs", [P, EO], F32, "tail")
    gel = [place(f"gel{i}", [P, T], F32, "tail" if i else "ikw", 2304 if i else 2176) for i in range(2)]
    orow = place("orow", [NC, D], F32, "x", 4 * T * OROW_CHUNK)
    th = [place(f"th{i}", [P, SEQ], F32, "iqT", 2048 * i) for i in range(2)]
    tm = [place(f"tm{i}", [P, SEQ], F32, "iqT", 4096 + 2048 * i) for i in range(2)]
    pr = [place(f"pr{i}", [P, SEQ], F32, "vtok_s" if i == 2 else "ikw", 2048 * i % 4096) for i in range(3)]
    pT = [place(f"pT{i}", [P, TT, P], F32, "hmul0", 2048 * i) for i in range(2)]
    sg = [place(f"sg{i}", [P, T], F32, "tail", 2176 * i) for i in range(2)]
    p_hi = place("p_hi", [P, PD // P, T], F32R, "vtok")
    p_lo = place("p_lo", [P, PD // P, T], F32R, "ikw")
    ptok = place("ptok", [P, TT + 1, PD], F32, "qT")
    pp = place("pp", [P, DC, T], F32, "qT")
    sqacc = place("sqacc", [P, T], F32, "iqT")
    sqt = [place(f"sqt{i}", [P, T], F32, "iqT", 2176 * (1 + i)) for i in range(2)]
    rb = place("rb", [P, T], F32, "iqT", 2176 * 3)
    ytok = place("ytok", [P, TT + 1, D], F32, "h_hi")

    psD = nc.alloc_psum_tensor("psD", [P, 4, 512], F32)
    psX = [nc.alloc_psum_tensor(f"psX{i}", [P, 512], F32)[:] for i in range(4)]

    lines_d = nc.dram_tensor("bias_lines", [NH, P, LW], F32, kind="Internal").ap()
    x_d = nc.dram_tensor("x_saved", [P, DC * T], F32, kind="Internal").ap()

    ctx = ExitStack()
    with ctx:
        def sem(name):
            return ctx.enter_context(nc.semaphore(name))

        def sems(name, n):
            return [sem(f"{name}{i}") for i in range(n)]

        w_loaded = sems("w_loaded", RING)
        w_hi, w_lo, w_used = sem("w_hi"), sem("w_lo"), sem("w_used")
        tile_read = sems("tile_read", 2)
        aux_done, aux_read = sem("aux_done"), sems("aux_read", 2)
        x_in, prm_in, page_in, idxp_in = sems("x_in", TT + 1), sem("prm_in"), sem("page_in"), sem("idxp_in")
        small_in, bd_in, bias_in = sem("small_in"), sem("bd_in"), sem("bias_in")
        kpg_in, th_in, p_in, x_back = sems("kpg_in", 2), sems("th_in", 2), sem("p_in"), sem("x_back")
        ik_dup, lines_saved, x_saved = sem("ik_dup"), sem("lines_saved"), sem("x_kept")
        out_done, ktok_out = sem("out_done"), sems("ktok_out", 2)
        ident_ok, ones_ok, pool_const = sem("ident_ok"), sem("ones_ok"), sem("pool_const")
        dve_step, pool_step, act_step = sem("dve_step"), sem("pool_step"), sem("act_step")
        sq_done, rstd_v, rstd_a, diag_ok = sem("sq_done"), sem("rstd_v"), sem("rstd_a"), sem("diag_ok")
        n_t, n_hi, n_lo_v, n_lo_p = sem("n_t"), sem("n_hi"), sem("n_lo_v"), sem("n_lo_p")
        xn_ok, sq_ok, sqacc_ok, rb_v, rb_a = sem("xn_ok"), sem("sq_ok"), sem("sqacc_ok"), sem("rb_v"), sem("rb_a")
        idx_acc, iqbd_ok, iwcol_ok, sdots = sem("idx_acc"), sem("iqbd_ok"), sem("iwcol_ok"), sem("sdots")
        rs_ok, ss_copied, masked_in = sem("rs_ok"), sem("ss_copied"), sem("masked_in")
        topk_ok, topk_s_ok, mask_ok = sem("topk_ok"), sem("topk_s_ok"), sem("mask_ok")
        qbd_ok, slogit_b, sexp_ok, sp_ok = sem("qbd_ok"), sem("slogit_b"), sem("sexp_ok"), sem("sp_ok")
        spv_b, so_hi, so_lo = sem("spv_b"), sem("so_hi"), sem("so_lo")
        lru_a, lru_v, bd_zero, xe_ok, tap0 = sem("lru_a"), sem("lru_v"), sem("bd_zero"), sem("xe_ok"), sem("tap0")
        xc_ok, q_lru, sqrt_ok, u_ok, hs_ok = sem("xc_ok"), sem("q_lru"), sem("sqrt_ok"), sem("u_ok"), sem("hs_ok")
        yt_ok, y_hi, y_lo = sem("yt_ok"), sem("y_hi"), sem("y_lo")
        tm_ok, exp_ok, p_ok, tr_done = sem("tm_ok"), sem("exp_ok"), sem("p_ok"), sem("tr_done")
        pT_ok, pv_done, o_hi, o_lo = sem("pT_ok"), sem("pv_done"), sem("o_hi"), sem("o_lo")
        m_t, m_hi, m_lo, p_hi_ok = sem("m_t"), sem("m_hi"), sem("m_lo"), sem("p_hi_ok")
        f_hi, f_lo, xf_ok, fs_v, fs_a = sem("f_hi"), sem("f_lo"), sem("xf_ok"), sem("fs_v"), sem("fs_a")

        def tiles_of(kind):
            return [t for t, (k, _, _) in enumerate(TILES) if k == kind]

        def acc(t):
            s = 2 * (t % 2)
            return psD[:, s:s + 2, 0:HT]

        def two(ap):
            return ap.rearrange("p (a b) -> p a b", a=2)

        def seqs(ap):
            return ap.rearrange("p (b c) -> p b c", c=ST)

        def bank(job):
            return psX[AUX[job] % 2]

        def got_tile(eng, t):
            eng.wait_ge(w_used, LAST_UNIT[t] + 1)

        def got_job(eng, job):
            eng.wait_ge(aux_done, AUX[job] + 1)

        def read_job(ins, job):
            return ins.then_inc(aux_read[AUX[job] % 2], 1)

        def read_tile(ins, t):
            return ins.then_inc(tile_read[t % 2], 1)

        def job_read(eng, job):
            n = AUX[job]
            eng.wait_ge(aux_read[n % 2], n // 2 + 1)

        def tile_is_read(eng, kind, j, last=False):
            t = NTH[(kind, j, last)]
            eng.wait_ge(tile_read[t % 2], t // 2 + 1)

        def all_read(eng, kind, n):
            tile_is_read(eng, kind, n - 2)
            tile_is_read(eng, kind, n - 1)

        def x_is_new(eng, k, c):
            if k == 0:
                tile_is_read(eng, "wo", c)
            elif k == 1:
                tile_is_read(eng, "down", c, True)
            else:
                eng.wait_ge(xn_ok, c + 1)

        U = {k: FIRST[(k, 0)] for k in ("iq", "ik", "q", "k", "v", "xr", "ga", "gb", "wo", "pp", "pg")}
        U["pp2"] = FIRST[("pp", DC // 2)]
        h_last = (0, U["wo"], FIRST[("down", 0, True)])
        block = ctx.enter_context(nc.Block())

        @block.sync
        def _(sp):
            def load(n):
                if n >= len(UNITS):
                    return
                _, _, (w, r0, rc, c0, cc, _, _) = UNITS[n]
                if n >= RING:
                    sp.wait_ge(w_lo, n - RING + 1)
                src = a[w][0, P * r0:P * (r0 + rc), c0:c0 + cc].rearrange("(c p) n -> p c n", p=P)
                sp.dma_start(wraw[:, n % RING, 0:rc, 0:cc], src).then_inc(w_loaded[n % RING], 16)

            def pages(dst, pool, b, got):
                for g in range(NPG):
                    page = sp.value_load(pt[0:1, NPG * b + g:NPG * b + g + 1], min_val=0, max_val=n_pool - 1)
                    src = a[pool][0, bass.ds(page, 1)].rearrange("o s h d -> (o s) (h d)")
                    sp.dma_start(dst[:, g, :], src).then_inc(got, 16)

            for t in range(TT):
                sp.dma_start(xtok[:, t, :], a["x_prompt"][0, P * t:P * (t + 1), :]).then_inc(x_in[t], 16)
            sp.dma_start(xtok[0:NS, TT, :], a["x_sample"].rearrange("b j d -> (b j) d")).then_inc(x_in[TT], 16)
            for row, name in ((R_MIX, "norm_mix"), (R_FFN, "norm_ffn"), (R_PLE, "norm_ple"), (R_CB, "conv_b"),
                              (R_BA, "b_rg_a"), (R_BX, "b_rg_x"), (R_LAM, "lru_lambda")):
                sp.dma_start(prm[row:row + 1, :], a[name]).then_inc(prm_in, 16)
            sp.dma_start(prm[R_FIN:R_FIN + 1, :], a["norm_final"].rearrange("(o d) -> o d", o=1)).then_inc(prm_in, 16)
            sp.dma_start(prm[R_CW:R_CW + CW, :], a["conv_w"][0]).then_inc(prm_in, 16)
            sp.dma_start(prm[R_SC:R_SH, :], a["state_conv"][0].rearrange("b i d -> (b i) d")).then_inc(prm_in, 16)
            sp.dma_start(prm[R_SH:NR, :], a["state_rglru_h"][0]).then_inc(prm_in, 16)
            for n in range(RING):
                load(n)
            sp.dma_start(pt[:], a["page_table"].rearrange("(o b) g -> o (b g)", o=1)).then_inc(page_in, 16)
            sp.dma_start(onehot[:], a["bias_onehot"]).then_inc(small_in, 16)
            sp.dma_start(relb[:], a["rel_bias"]).then_inc(small_in, 16)
            sp.wait_ge(page_in, 16)
            for b in range(NB):
                for g in range(NPG):
                    page = sp.value_load(pt[0:1, NPG * b + g:NPG * b + g + 1], min_val=0, max_val=n_pool - 1)
                    src = a["cache_idx_k"][0, bass.ds(page, 1)].rearrange("o s d -> (o s) d")
                    for r in range(2):
                        sp.dma_start(idxp[:, NPG * b + g, r, :], src).then_inc(idxp_in, 16)
            job_read(sp, ("x", DC - 2))
            job_read(sp, ("x", DC - 1))
            sp.dma_start(x_d, x[:].rearrange("p c t -> p (c t)")).then_inc(x_saved, 16)
            for n in range(RING, 8):
                load(n)
            job_read(sp, "lines_a")
            job_read(sp, "lines_b")
            sp.dma_start(lines_d, lines[:].unsqueeze(1).broadcast_to([NH, P, LW])).then_inc(lines_saved, 16)
            tile_is_read(sp, "ik", 0)
            sp.dma_start(ik2[HD:P, :], ikw[0:HD, :]).then_inc(ik_dup, 16)
            load(8)
            job_read(sp, "ik")
            sp.dma_start(o["idx_k_prompt"][0, 0].rearrange("(t p) d -> p t d", p=P),
                         iktok[:, 0:TT, 0:HD]).then_inc(out_done, 16)
            sp.dma_start(o["idx_k_sample"][0].rearrange("b j d -> (b j) d"),
                         iktok[0:NS, TT, 0:HD]).then_inc(out_done, 16)
            for n in range(9, 13):
                load(n)
            sp.wait_ge(lines_saved, 16)
            sp.wait_ge(ik_dup, 16)
            for g in range(NB // 2):
                for jj in range(NJ):
                    rows = bias_s[NS * g + jj:NS * (g + 1):NJ, 0:PAST]
                    sp.dma_start(rows, lines_d[:, 0, LMAX - PAST - jj:LMAX - jj]).then_inc(bias_in, 16)
                    rows = bias_n[NS * g + jj:NS * (g + 1):NJ, :]
                    sp.dma_start(rows, lines_d[:, 0, LMAX - jj:LMAX - jj + NJ]).then_inc(bias_in, 16)
            for n in range(13, 16):
                load(n)
            for b in range(2):
                pages(kpg[b], "cache_k", b, kpg_in[b])
            sp.wait_ge(bd_zero, 1)
            for g, w in enumerate(("w_rg_a", "w_rg_x")):
                for h in range(2):
                    sp.dma_start(bd[HD * h:HD * (h + 1), :, g, HD * h:HD * (h + 1)],
                                 a[w][0].rearrange("(c h) k d -> h k c d", h=2)[h]).then_inc(bd_in, 16)
            load(16)
            for t in range(TT + 1):
                load(17 + t)
                rows = P if t < TT else NS
                job_read(sp, ("kout", t))
                dst = (o["k_prompt"][0, 0, P * t:P * (t + 1)].rearrange("s h d -> s (h d)") if t < TT
                       else o["k_sample"][0].rearrange("b j h d -> (b j) (h d)"))
                sp.dma_start(dst, ktok[t % 2][0:rows, :]).then_inc(ktok_out[t % 2], 16)
            for b in range(2, NB):
                job_read(sp, ("kts", b - 2, 1))
                pages(kpg[b % 2], "cache_k", b, kpg_in[b % 2])
                if b in (2, 3, 5):
                    load({2: 22, 3: 23, 5: 24}[b])
            for b in range(2):
                job_read(sp, ("kts", NB - 2 + b, 1))
                pages(kpg[b], "cache_v", b, kpg_in[b])
            for t in range(TT + 1):
                job_read(sp, ("vout", t))
                dst = (o["v_prompt"][0, 0, P * t:P * (t + 1)].rearrange("s h d -> s (h d)") if t < TT
                       else o["v_sample"][0].rearrange("b j h d -> (b j) (h d)"))
                sp.dma_start(dst, vtok[:, t, :] if t < TT else vtok_s[:]).then_inc(out_done, 16)
            load(25)
            load(26)
            for b in range(2, NB):
                load(25 + b)
                sp.wait_ge(spv_b, b - 1)
                pages(kpg[b % 2], "cache_v", b, kpg_in[b % 2])
            for n in range(33, 39):
                load(n)
            n = 39
            job_read(sp, ("gate", DC - 1, 1, 1))
            for h in range(NH):
                if h >= 2:
                    sp.wait_ge(tm_ok, TT * (h - 1))
                src = bass.AP(tensor=lines_d.tensor, offset=LW * P * h + P - 1, ap=[[LW - 1, P], [1, SEQ]])
                sp.dma_start(th[h % 2][:], src).then_inc(th_in[h % 2], 16)
                if h >= 1:
                    load(n)
                    load(n + 1)
                    n += 2
                if h == 1:
                    job_read(sp, "st_a")
                    job_read(sp, "st_b")
                    sp.dma_start(o["conv_prompt"][0, 0], orow[C_CP:C_CS, :]).then_inc(out_done, 16)
                    sp.dma_start(o["conv_sample"][0].rearrange("b i d -> (b i) d"), orow[C_CS:C_HP, :])\
                        .then_inc(out_done, 16)
                    sp.dma_start(o["h_prompt"][0], orow[C_HP:C_HS, :]).then_inc(out_done, 16)
                    sp.dma_start(o["h_sample"][0], orow[C_HS:NC, :]).then_inc(out_done, 16)
            while n < U["gb"] + RING + 1:
                load(n)
                n += 1
            sp.wait_ge(pv_done, STEPS)
            sp.dma_start(ptok[:, 0:TT, :], a["p_prompt"][0, 0].rearrange("(t p) d -> p t d", p=P)).then_inc(p_in, 16)
            sp.dma_start(ptok[0:NS, TT, :], a["p_sample"][0].rearrange("b j d -> (b j) d")).then_inc(p_in, 16)
            while n < U["wo"] + 4:
                load(n)
                n += 1
            sp.wait_ge(m_t, DC)
            sp.dma_start(x[:].rearrange("p c t -> p (c t)"), x_d).then_inc(x_back, 16)
            while n < len(UNITS):
                load(n)
                n += 1
            for t in range(TT + 1):
                rows = P if t < TT else NS
                job_read(sp, ("y", t, 0))
                job_read(sp, ("y", t, 1))
                dst = (o["y_prompt"][0, P * t:P * (t + 1), :] if t < TT
                       else o["y_sample"].rearrange("b j d -> (b j) d"))
                sp.dma_start(dst, ytok[0:rows, t, :]).then_inc(out_done, 16)
            sp.wait_ge(out_done, 16 * (2 + TT + 1 + 4 + TT + 1))
            sp.wait_ge(ktok_out[0], 16 * 3)
            sp.wait_ge(ktok_out[1], 16 * 2)
            sp.wait_ge(x_saved, 16)

        @block.scalar
        def _(act):
            sc = nc.scalar
            steps = [0]

            def link(ins):
                steps[0] += 1
                ins.then_inc(act_step, 1)
                act.wait_ge(act_step, steps[0])

            def round_weights(n):
                if n >= len(UNITS):
                    return
                _, _, (_, _, rc, _, cc, _, _) = UNITS[n]
                act.wait_ge(w_loaded[n % RING], 16 * (n // RING + 1))
                if n >= RING:
                    act.wait_ge(w_used, n - RING + 1)
                sc.copy(whi[:, n % RING, 0:rc, 0:cc], wraw[:, n % RING, 0:rc, 0:cc]).then_inc(w_hi, 1)

            def norm_hi(k, c):
                act.wait_ge(n_t, DC * k + c + 1)
                if k and c == 0:
                    act.wait_ge(w_used, h_last[k])
                sc.copy(h_hi[:, c, :], nbuf[c % 4][:]).then_inc(n_hi, 1)

            def root(dst, src, signal):
                sc.activation(dst, src, ACT.Sqrt).then_inc(signal, 1)

            for t in range(TT + 1):
                rows = P if t < TT else NS
                act.wait_ge(x_in[t], 16)
                if t:
                    act.wait_ge(sq_done, t)
                else:
                    act.wait_ge(pool_const, 1)
                sc.activation(junk[0:rows, :], xtok[0:rows, t, :], ACT.Square,
                              accum_out=stat[0:rows, t:t + 1]).then_inc(sq_done, 1)
            got_job(act, "prm")
            read_job(sc.copy(prmT[:], bank("prm")[:, 0:DC * NR].rearrange("p (c r) -> p c r", r=NR)), "prm")
            act.wait_ge(rstd_v, 2)
            root(stat[:, 16:16 + TT + 1], stat[:, 8:8 + TT + 1], rstd_a)
            got_job(act, "xs")
            read_job(sc.copy(x[:, :, SEQ:T], bank("xs")[:, 0:DC * NS].rearrange("p (c s) -> p c s", s=NS)), "xs")

            def x_chunk(c):
                got_job(act, ("x", c))
                read_job(sc.copy(x[:, c, 0:SEQ], bank(("x", c))), ("x", c))

            x_chunk(0)
            round_weights(0)
            x_chunk(2)
            x_chunk(4)
            x_chunk(5)
            norm_hi(0, 0)
            x_chunk(6)
            norm_hi(0, 1)
            x_chunk(7)
            for c in range(2, DC):
                if c % 2:
                    round_weights(c // 2)
                norm_hi(0, c)
            job_read(act, "prm")
            link(sc.activation(lru[:, 0, :], prmT[:, :, R_LAM], ACT.Abs))
            sc.activation(lru[:, 1, :], lru[:, 0, :], ACT.Exp, scale=-1.0).then_inc(lru_a, 1)
            n = 0
            for t in tiles_of("iq"):
                got_tile(act, t)
                act.wait_ge(diag_ok, 2)
                read_tile(sc.copy(two(iqT[:, t, :]), acc(t)), t)
                round_weights(n + RING)
                n += 1
                if n == U["ik"]:
                    for k in range(4):
                        got_job(act, ("iks", k))
                        dst = iks[:, 2 * k:2 * k + 2, :].rearrange("p b s -> p (b s)")
                        read_job(sc.copy(dst, bank(("iks", k))), ("iks", k))
            t = tiles_of("ik")[0]
            got_tile(act, t)
            link(sc.copy(two(ikw[0:HD + NH, :]), acc(t)[0:HD + NH]))
            read_tile(sc.copy(two(ik2[0:HD, :]), acc(t)[0:HD]), t)
            round_weights(n + RING)
            n += 1

            def index_relu(s):
                got_job(act, ("idx", s))
                if s >= 2:
                    act.wait_ge(idx_acc, s - 1)
                w = P * (2 + s // NH)
                read_job(sc.activation(relu[s % 2][:, 0:w], bank(("idx", s))[:, 0:w], ACT.Relu, scale=HD ** -0.5),
                         ("idx", s))

            def key_rows(t):
                rows = P if t < TT else NS
                got_job(act, ("kout", t))
                if t >= 2:
                    act.wait_ge(ktok_out[t % 2], 16 * (t // 2))
                else:
                    job_read(act, ("iks", 3))
                    job_read(act, ("iks", 2))
                read_job(sc.copy(ktok[t % 2][0:rows, :], bank(("kout", t))[0:rows, :]), ("kout", t))

            def value_rows(t):
                rows = P if t < TT else NS
                got_job(act, ("vout", t))
                dst = vtok[:, t, :] if t < TT else vtok_s[:]
                read_job(sc.copy(dst, bank(("vout", t))[0:rows, :]), ("vout", t))

            def past_keys(b):
                for g in range(NPG):
                    got_job(act, ("kts", b, g))
                    if b >= 2 and g == 0:
                        act.wait_ge(slogit_b, b - 1)
                    dst = kts[b % 2][:, :, PG * g:PG * (g + 1)]
                    src = bank(("kts", b, g))[:].rearrange("p (m s) -> p m s", s=PG)
                    read_job(sc.copy(dst, src), ("kts", b, g))

            for kind, dst, scale in (("q", qT, HD ** -0.5), ("k", kT, 1.0), ("v", vT, 1.0)):
                for t in tiles_of(kind):
                    j = TILES[t][1]
                    if kind == "q":
                        for s in range(6 * j, 6 * j + 6):
                            index_relu(s)
                    if kind == "v":
                        if j == 0:
                            act.wait_ge(x_saved, 16)
                            key_rows(0)
                        elif j == 1:
                            key_rows(2)
                        elif j == 2:
                            key_rows(TT)
                            past_keys(0)
                        else:
                            past_keys(2)
                    got_tile(act, t)
                    read_tile(sc.activation(two(dst[:, j, :]), acc(t), ACT.Copy, scale=scale), t)
                    round_weights(n + RING)
                    n += 1
                    if kind == "v" and j <= 1:
                        key_rows(2 * j + 1)
                    elif kind == "v":
                        past_keys(2 * j - 3)
            def sample_exp(g):
                job_read(act, ("smask", g))
                sc.activation(ps_s[:, g, :], ps_s[:, g, :], ACT.Exp, bias=sstat[:, g:g + 1], scale=-1.0,
                              accum_out=sstat[:, 2 + g:3 + g]).then_inc(sexp_ok, 1)

            def sample_turned():
                got_job(act, "spt")
                read_job(sc.copy(pts[:].rearrange("p a g q -> p (a g q)"), bank("spt")), "spt")
                got_job(act, "spn")
                read_job(sc.copy(ptn[:].rearrange("p g q -> p (g q)"), bank("spn")[0:NS, 0:2 * P]), "spn")

            def sample_out_hi():
                act.wait_ge(spv_b, NB)
                for h in range(2):
                    src = psX[2][HD * h:HD * (h + 1), 0:HP * 64].rearrange("p (m b h j) -> p m b h j", m=HP, b=NB, h=2)
                    for m in range(HP):
                        sc.copy(act_hi[HD * h:HD * (h + 1), 8 + m, SEQ:T].rearrange("p (b j) -> p b j", j=NJ),
                                src[:, m, :, h, :]).then_inc(so_hi, 1)

            def conv_line(c, t):
                s = c % 2
                if c >= 2:
                    act.wait_ge(u_ok, c - 1)
                else:
                    act.wait_ge(bd_zero, 2)
                got_tile(act, t)
                ps = acc(t)
                sc.copy(seqs(xe[s][:, S0:EXT])[:, :, 0:CW - 1],
                        prmT[:, c, R_SC:R_SH].rearrange("p (b i) -> p b i", b=NB)).then_inc(xe_ok, 1)
                sc.copy(xe[s][:, CW - 1:CW - 1 + HT], ps[:, 0, :]).then_inc(xe_ok, 1)
                sc.copy(xe[s][:, CW - 1 + HT:S0], ps[:, 1, 0:SEQ - HT]).then_inc(xe_ok, 1)
                read_tile(sc.copy(seqs(xe[s][:, S0:EXT])[:, :, CW - 1:ST],
                                  ps[:, 1, SEQ - HT:HT].rearrange("p (b j) -> p b j", j=NJ)), t)
                act.wait_ge(xe_ok, 3 * (c + 1))
                tile_is_read(act, "xr", c)
                sc.activation(xc[s][:], xe[s][:, 0:EO], ACT.Identity, scale=prmT[:, c, R_CW:R_CW + 1],
                              bias=prmT[:, c, R_CB:R_CB + 1]).then_inc(tap0, 1)

            def gates(c):
                if c >= 1:
                    act.wait_ge(hs_ok, c)
                else:
                    act.wait_ge(lru_v, 1)
                    job_read(act, ("vout", TT))
                for g, dst in ((0, rq), (1, ig)):
                    for k in range(2):
                        job = ("gate", c, g, k)
                        got_job(act, job)
                        read_job(sc.activation(dst[:, EH * k:EH * (k + 1)], bank(job)[:, 0:EH], ACT.Tanh, scale=0.5,
                                               bias=lru[:, 4 + g, c:c + 1]), job)
                    if g == 0:
                        job_read(act, ("gate", c, 0, 0))
                        job_read(act, ("gate", c, 0, 1))
                        sc.activation(rq[:], rq[:], ACT.Tanh, scale=lru[:, 3, c:c + 1],
                                      bias=lru[:, 3, c:c + 1]).then_inc(q_lru, 1)

            def gelu_path(c, t):
                got_tile(act, t)
                if c >= 2:
                    act.wait_ge(yt_ok, c - 1)
                elif c == 0:
                    job_read(act, ("smask", 1))
                read_tile(sc.activation(two(gel[c % 2][:]), acc(t), ACT.Gelu_apprx_tanh), t)

            def lru_root(c):
                act.wait_ge(q_lru, c + 1)
                if c >= 1:
                    act.wait_ge(hs_ok, c)
                root(sq[:], rq[:], sqrt_ok)

            def y_upper(c):
                act.wait_ge(yt_ok, c + 1)
                sc.copy(act_hi[:, c, :], hmul[c % 2][:]).then_inc(y_hi, 1)

            past_keys(4)
            conv_line(0, NTH[("xr", 0, False)])
            round_weights(n + RING)
            n += 1
            past_keys(5)
            past_keys(6)
            value_rows(0)
            value_rows(1)
            past_keys(7)
            for tt in range(2, TT + 1):
                value_rows(tt)

            sample_exp(0)
            sample_exp(1)
            for c in range(DC):
                gates(c)
                if c == 0:
                    sample_turned()
                lru_root(c)
                if c + 1 < DC:
                    conv_line(c + 1, NTH[("xr", c + 1, False)])
                    round_weights(n + RING)
                    n += 1
                if c >= 1:
                    y_upper(c - 1)
                if c == 5:
                    sample_out_hi()
                gelu_path(c, NTH[("gr", c, False)])
                round_weights(n + RING)
                n += 1
            y_upper(DC - 1)

            def attend_exp(s):
                w = P * (s % TT + 1)
                job_read(act, ("qk", s))
                sc.activation(pr[s % 3][:, 0:w], pr[s % 3][:, 0:w], ACT.Exp, bias=stat[:, 24 + s % 2:25 + s % 2],
                              scale=-1.0, accum_out=stat[:, 26 + s % 2:27 + s % 2]).then_inc(exp_ok, 1)

            def attend_turned(s):
                w = P * (s % TT + 1)
                act.wait_ge(tr_done, s + 1)
                if s >= 2:
                    act.wait_ge(pv_done, s - 1)
                elif s == 0:
                    act.wait_ge(y_lo, DC)
                sc.copy(pT[s % 2][:, 0:s % TT + 1, :].rearrange("p k t -> p (k t)"), psX[2][:, 0:w])\
                    .then_inc(pT_ok, 1)

            def attend_out_hi(m):
                act.wait_ge(pv_done, 2 * TT * (m + 1))
                sc.copy(act_hi[:, 8 + m, 0:SEQ], psX[3][:]).then_inc(o_hi, 1)

            def attend(s):
                if 2 <= s < STEPS + 2:
                    attend_turned(s - 2)
                if s < STEPS:
                    attend_exp(s)
                if s >= 10 and (s - 10) % 8 == 0:
                    attend_out_hi((s - 10) // 8)

            def gate_tanh(k, t):
                got_tile(act, t)
                if k >= 2:
                    tile_is_read(act, *(("rnn", k - 2) if k < DC + 2 else ("att", k - 2 - DC)))
                elif k == 0:
                    act.wait_ge(hs_ok, DC)
                    act.wait_ge(yt_ok, DC)
                read_tile(sc.activation(two(sg[k % 2][:]), acc(t), ACT.Tanh, scale=0.5), t)

            def state_rows():
                for k, job in enumerate(("st_a", "st_b")):
                    got_job(act, job)
                    read_job(sc.copy(orow[:, SEQ * k:SEQ * (k + 1)], bank(job)[0:NC, :]), job)

            for i in range(2 * DC):
                attend(2 * i)
                if i % 2 == 0:
                    gate_tanh(i // 2, FIRST_TILE["ga"] + i)
                round_weights(n + RING)
                n += 1
                attend(2 * i + 1)
                if i == 1:
                    state_rows()
            attend(STEPS)

            def upper(dst, k, hi_ok, scale=1.0):
                sc.activation(dst, hmul[k % 2][:], ACT.Copy, scale=scale).then_inc(hi_ok, 1)

            for j in range(DC):
                gate_tanh(DC + j, FIRST_TILE["gb"] + 2 * j)
                round_weights(n + RING)
                if j == 0:
                    attend(STEPS + 1)
                    attend(STEPS + 2)
                round_weights(n + 1 + RING)
                if j >= 1:
                    act.wait_ge(m_t, j)
                    upper(act_hi[:, j - 1, :], j - 1, m_hi, 0.5)
                if j >= 1 and j - 1 <= TT:
                    t = j - 1
                    c0, c1 = (P * t, P * (t + 1)) if t < TT else (SEQ, T)
                    got_job(act, ("p", t))
                    sc.copy(p_hi[:, :, c0:c1], bank(("p", t))[:, 0:2 * (c1 - c0)].rearrange("p (k t) -> p k t", k=2))\
                        .then_inc(p_hi_ok, 1)
                n += 2
            act.wait_ge(m_t, DC)
            upper(act_hi[:, DC - 1, :], DC - 1, m_hi, 0.5)

            def square(k, c):
                x_is_new(act, k, c)
                i = DC * k + c
                if i >= 2:
                    act.wait_ge(sqacc_ok, i - 1)
                sc.activation(sqt[i % 2][:], x[:, c, :], ACT.Square).then_inc(sq_ok, 1)

            for j in range(DC):
                round_weights(n + RING)
                n += 1
                square(0, j)
            def projection(j0):
                nonlocal n
                for j in range(j0, j0 + DC // 2):
                    t = NTH[("pp", j, False)]
                    got_tile(act, t)
                    read_tile(sc.copy(two(pp[:, j, :]), acc(t)), t)
                    round_weights(n + RING)
                    n += 1

            def row_root(k):
                for half in range(2):
                    act.wait_ge(rb_v, 2 * k + half + 1)
                    part = rb[:, HT * half:HT * (half + 1)]
                    root(part, part, rb_a)

            projection(0)
            row_root(0)
            for j in range(DC):
                norm_hi(1, j)
            k = 0
            for half, (f0, fn) in enumerate(FFN_HALVES):
                t0 = FIRST_TILE["gate"] + half * (2 * FA + DC)
                for f in range(fn):
                    t = t0 + 2 * f
                    got_tile(act, t)
                    if k >= 2:
                        tile_is_read(act, "up", k - 2)
                    read_tile(sc.activation(two(sg[k % 2][:]), acc(t), ACT.Silu), t)
                    round_weights(n + RING)
                    round_weights(n + 1 + RING)
                    n += 2
                    if f >= 1:
                        tile_is_read(act, "up", k - 1)
                        upper(act_hi[:, f - 1, :], k - 1, f_hi)
                    k += 1
                tile_is_read(act, "up", k - 1)
                upper(act_hi[:, fn - 1, :], k - 1, f_hi)
                for j in range(DC):
                    round_weights(n + RING)
                    round_weights(n + 1 + RING)
                    n += 2
                    if half:
                        square(1, j)
            projection(DC // 2)
            row_root(1)
            for j in range(DC):
                norm_hi(2, j)
            for j in range(DC):
                t = FIRST_TILE["pg"] + j
                got_tile(act, t)
                if j >= 2:
                    act.wait_ge(xn_ok, j - 1)
                read_tile(sc.activation(two(sg[j % 2][:]), acc(t), ACT.Tanh, scale=0.5), t)
                round_weights(n + RING)
                n += 1
                if j >= 1:
                    square(2, j - 1)
                    sc.activation(pp[:, j - 1, :], x[:, j - 1, :], ACT.Copy,
                                  scale=prmT[:, j - 1, R_FIN:R_FIN + 1]).then_inc(xf_ok, 1)
            square(2, DC - 1)
            sc.activation(pp[:, DC - 1, :], x[:, DC - 1, :], ACT.Copy,
                          scale=prmT[:, DC - 1, R_FIN:R_FIN + 1]).then_inc(xf_ok, 1)
            act.wait_ge(fs_v, 1)
            root(stat[:, 48:48 + TT + 1], stat[:, 40:40 + TT + 1], fs_a)
            act.wait_ge(fs_a, 1)
            for t in range(TT + 1):
                rows = P if t < TT else NS
                job = ("y", t, 0)
                got_job(act, job)
                read_job(sc.activation(ytok[0:rows, t, 0:512], bank(job)[0:rows, :], ACT.Copy,
                                       scale=stat[0:rows, 48 + t:49 + t]), job)

        @block.vector
        def _(dve):
            v = nc.vector
            steps = [0]

            def link(ins):
                steps[0] += 1
                ins.then_inc(dve_step, 1)
                dve.wait_ge(dve_step, steps[0])

            def inverse_mean(ap, src):
                link(v.tensor_scalar(ap, src, 1.0 / D, EPS, ALU.mult, ALU.add))
                return v.reciprocal(ap, ap)

            def norm_scale(k, c, gain, factor):
                if c >= 4:
                    dve.wait_ge(n_hi, DC * k + c - 3)
                    dve.wait_ge(n_lo_p if c % 2 else n_lo_v, 4 * k + c // 2 - 1)
                v.scalar_tensor_tensor(nbuf[c % 4][:], x[:, c, :], prmT[:, c, gain:gain + 1], factor,
                                       ALU.mult, ALU.mult).then_inc(n_t, 1)

            def norm_lo(k, c):
                dve.wait_ge(n_hi, DC * k + c + 1)
                v.tensor_tensor(h_lo[:, c, :], nbuf[c % 4][:], h_hi[:, c, :].bitcast(F32), ALU.subtract)\
                    .then_inc(n_lo_v, 1)

            def norm(k, gain, factor):
                for c in range(DC):
                    if k == 0:
                        job_read(dve, ("x", c))
                    norm_scale(k, c, gain, factor)
                    if c % 2:
                        norm_lo(k, c - 1)

            v.memset(ones[:], 1.0).then_inc(ones_ok, 1)
            dve.wait_ge(ident_ok, 2)
            dve.wait_ge(sq_done, TT + 1)
            inverse_mean(stat[:, 8:8 + TT + 1], stat[:, 0:TT + 1]).then_inc(rstd_v, 2)
            dve.wait_ge(rstd_a, 1)
            for t in range(TT):
                ins = v.tensor_scalar(diag[:, t, :], ident[:], stat[:, 16 + t:17 + t], None, ALU.mult)
            ins.then_inc(diag_ok, 1)
            v.tensor_scalar(diag[0:NS, TT, 0:NS], ident[0:NS, 0:NS], stat[0:NS, 16 + TT:17 + TT], None, ALU.mult)\
                .then_inc(diag_ok, 1)
            got_job(dve, ("x", 1))
            read_job(v.tensor_copy(x[:, 1, 0:SEQ], bank(("x", 1))), ("x", 1))
            got_job(dve, "rstd_a")
            read_job(v.tensor_copy(rb0[:, 0:SEQ], bank("rstd_a")), "rstd_a")
            got_job(dve, "rstd_b")
            read_job(v.tensor_copy(rb0[:, SEQ:T], bank("rstd_b")[:, 0:NS]), "rstd_b")
            got_job(dve, ("x", 3))
            read_job(v.tensor_copy(x[:, 3, 0:SEQ], bank(("x", 3))), ("x", 3))
            job_read(dve, "rstd_a")
            job_read(dve, "rstd_b")
            job_read(dve, "prm")
            job_read(dve, "xs")
            norm(0, R_MIX, rb0[:])

            for k, job in enumerate(("lines_a", "lines_b")):
                got_job(dve, job)
                w = LW // 2
                read_job(v.tensor_copy(lines[:, w * k:w * (k + 1)], bank(job)[0:NH, 0:w]), job)
            got_job(dve, "selT")
            read_job(v.tensor_copy(selT[:].rearrange("p g c -> p (g c)"), bank("selT")[:, 0:2 * NS]), "selT")

            dve.wait_ge(lru_a, 1)
            e, z, z2, s, sp_ = (lru[:, i, :] for i in (1, 2, 6, 7, 3))
            link(v.tensor_scalar(z, e, 2.0, None, ALU.add))
            link(v.reciprocal(z, z))
            link(v.tensor_tensor(z, z, e, ALU.mult))
            link(v.tensor_tensor(z2, z, z, ALU.mult))
            link(v.tensor_scalar(s, z2, 1.0 / 17, None, ALU.mult))
            for k in range(15, 1, -2):
                link(v.scalar_tensor_tensor(s, s, 1.0 / k, z2, ALU.add, ALU.mult))
            link(v.scalar_tensor_tensor(s, s, 1.0, z, ALU.add, ALU.mult))
            link(v.tensor_scalar(z, prmT[:, :, R_LAM], -1.0, 0.0, ALU.mult, ALU.max))
            link(v.scalar_tensor_tensor(s, s, 2.0, z, ALU.mult, ALU.add))
            v.tensor_scalar(sp_, s, 2.0, None, ALU.mult)
            v.tensor_scalar(lru[:, 4, :], prmT[:, :, R_BA], 0.5, None, ALU.mult)
            v.tensor_scalar(lru[:, 5, :], prmT[:, :, R_BX], 0.5, None, ALU.mult).then_inc(lru_v, 1)

            def conv_taps(c):
                s = c % 2
                dve.wait_ge(tap0, c + 1)
                for j in range(1, CW):
                    ins = v.scalar_tensor_tensor(xc[s][:], xe[s][:, j:j + EO], prmT[:, c, R_CW + j:R_CW + j + 1],
                                                 xc[s][:], ALU.mult, ALU.add)
                    if j < CW - 1:
                        link(ins)
                    else:
                        ins.then_inc(xc_ok, 1)

            got_job(dve, "ik")
            kw = HD + NH
            src = bank("ik")[:, 0:(TT + 1) * kw].rearrange("p (t c) -> p t c", c=kw)
            link(v.tensor_copy(iktok[:, 0:TT, :], src[:, 0:TT, :]))
            read_job(v.tensor_copy(iktok[0:NS, TT, :], src[0:NS, TT, :]), "ik")
            job_read(dve, "ik")
            link(v.tensor_scalar(iwtok[:, 0:TT, :], iktok[:, 0:TT, HD:kw], NH ** -0.5, None, ALU.mult))
            v.tensor_scalar(iwtok[0:NS, TT, :], iktok[0:NS, TT, HD:kw], NH ** -0.5, None, ALU.mult)\
                .then_inc(iwcol_ok, 1)
            dve.wait_ge(iwcol_ok, 1)

            def to_mask(work):
                return v.tensor_scalar(work, work, TAKEN_BELOW, OFF, ALU.is_gt, ALU.mult)

            def top_round(work, keys, k, rows, r):
                link(v.max(top8[0:rows, :], work[:, 0:keys]))
                left = k - 8 * r
                if left < 8:
                    link(v.memset(top8[0:rows, left:8], PAD))
                link(v.match_replace(work[:], top8[0:rows, :], work[:], TAKEN))

            def top_rounds(i, first, last):
                if first == 0:
                    dve.wait_ge(masked_in, i)
                for r in range(first, last):
                    top_round(score[i], P * (i + 1), TOPK_P, P, r)
                if last == TOPK_P // 8:
                    to_mask(score[i][:]).then_inc(topk_ok, 1)

            done = 0
            for st in range(NH * (TT - 1)):
                i, h = 1 + st // NH, st % NH
                w = P * (i + 1)
                job_read(dve, ("idx", st))
                r, wt = relu[st % 2][:, 0:w], iwtok[:, i, h:h + 1]
                if h == 0:
                    ins = v.tensor_scalar(score[i][:], r, wt, None, ALU.mult)
                else:
                    dve.wait_ge(idx_acc, st)
                    ins = v.scalar_tensor_tensor(score[i][:], r, wt, score[i][:], ALU.mult, ALU.add)
                ins.then_inc(idx_acc, 1)
                if st >= 12:
                    more = 5 if st == 17 else 1
                    top_rounds(1, done, done + more)
                    done += more
            assert done == TOPK_P // 8

            got_job(dve, "iwcol")
            dve.wait_ge(pool_const, 2)
            for g in range(2):
                src = bank("iwcol")[:, NH * g:NH * (g + 1)].unsqueeze(1).broadcast_to([P, NB // 2, NH])
                ins = v.tensor_tensor(iwsc[:], hm[:], src, ALU.mult)
                if g:
                    read_job(ins, "iwcol")
                    job_read(dve, "iwcol")
                else:
                    link(ins)
                link(v.tensor_reduce(stat[:, 60 + g:61 + g], iwsc[:].rearrange("p b h -> p (b h)"),
                                     mybir.AxisListType.X, ALU.add))
            link(v.tensor_scalar(stat[:, 60:62], stat[:, 60:62], HD ** -0.5, None, ALU.mult))
            top_rounds(2, 0, 4)
            dve.wait_ge(sdots, 1)
            for g in range(2):
                v.tensor_scalar(rs_s[:, g, :], psX[2 + g][:, 0:SK], 0.0, stat[:, 60 + g:61 + g], ALU.max, ALU.mult)\
                    .then_inc(rs_ok, 1)
            v.memset(score_s[:, SK:SK + 8], PAD).then_inc(ss_copied, 1)
            got_job(dve, "sidx")
            read_job(v.tensor_copy(score_s[:, 0:SK], bank("sidx")[0:NS, 0:SK]), "sidx")

            dve.wait_ge(masked_in, TT)
            for r in range(-(-TOPK_S // 8)):
                top_round(score_s, SK, TOPK_S, NS, r)
            to_mask(score_s[:, 0:SK]).then_inc(topk_s_ok, 1)
            top_rounds(2, 4, TOPK_P // 8)
            top_rounds(3, 0, TOPK_P // 8)

            conv_taps(0)
            dve.wait_ge(slogit_b, NB)
            dve.wait_ge(bias_in, 16 * 2 * NB // 2 * NJ)
            new = bias_n[:].unsqueeze(1).broadcast_to([P, NB, NJ])
            link(v.tensor_copy(bias_s[:, PAST:SK].rearrange("p (b j) -> p b j", j=NJ), new))
            for g in range(2):
                ins = v.tensor_tensor(ps_s[:, g, :], psX[2 + g][:, 0:SK], bias_s[:], ALU.add)
                link(ins)
            for g in range(2):
                job = ("smask", g)
                got_job(dve, job)
                read_job(v.tensor_tensor_reduce(ps_s[:, g, :], ps_s[:, g, :], bank(job)[:, 0:SK], -1.0, 3.0e38,
                                                ALU.add, ALU.min, sstat[:, g:g + 1]), job)

            def sample_normal():
                for g in range(2):
                    dve.wait_ge(sexp_ok, g + 1)
                    link(v.reciprocal(sstat[:, 4 + g:5 + g], sstat[:, 2 + g:3 + g]))
                    v.tensor_scalar(ps_s[:, g, :], ps_s[:, g, :], sstat[:, 4 + g:5 + g], None, ALU.mult)\
                        .then_inc(sp_ok, 1)

            def sample_out_lo():
                dve.wait_ge(so_hi, 2 * HP)
                for h in range(2):
                    rows = slice(HD * h, HD * (h + 1))
                    src = psX[2][rows, 0:HP * 64].rearrange("p (m b h j) -> p m b h j", m=HP, b=NB, h=2)
                    for m in range(HP):
                        def line(t):
                            return t[rows, 8 + m, SEQ:T].rearrange("p (b j) -> p b j", j=NJ)
                        v.tensor_tensor(line(act_lo), src[:, m, :, h, :], line(act_hi).bitcast(F32), ALU.subtract)\
                            .then_inc(so_lo, 1)

            def recurrence(c):
                s = c % 2
                dve.wait_ge(q_lru, c + 1)
                if c:
                    dve.wait_ge(yt_ok, c)
                link(v.tensor_scalar(hs[:], rq[:], 1.0, None, ALU.add))
                link(v.reciprocal(hs[:], hs[:]))
                v.tensor_copy(stO[:, c, C_CP:C_CS], xe[s][:, SEQ:S0])
                v.tensor_copy(stO[:, c, C_CS:C_HP].rearrange("p (b i) -> p b i", b=NB),
                              seqs(xe[s][:, S0:EXT])[:, :, NJ:ST])
                dve.wait_ge(sqrt_ok, c + 1)
                link(v.tensor_tensor(sq[:], sq[:], hs[:], ALU.mult))
                v.tensor_scalar(rq[:], hs[:], 2.0, -1.0, ALU.mult, ALU.add)
                job_read(dve, ("gate", c, 1, 0))
                job_read(dve, ("gate", c, 1, 1))
                link(v.scalar_tensor_tensor(ig[:], ig[:], 1.0, xc[s][:], ALU.add, ALU.mult))
                link(v.tensor_tensor(ig[:], ig[:], sq[:], ALU.mult))
                link(v.memset(seqs(rq[:, SEQ:EO])[:, :, 0:CW - 1], 0.0))
                link(v.memset(seqs(ig[:, SEQ:EO])[:, :, 0:CW - 2], 0.0))
                ins = v.tensor_copy(seqs(ig[:, SEQ:EO])[:, :, CW - 2:CW - 1],
                                    prmT[:, c, R_SH:NR].rearrange("p (b i) -> p b i", i=1))
                ins.then_inc(u_ok, 1)
                dve.wait_ge(u_ok, c + 1)
                v.tensor_tensor_scan(hs[:], rq[:], ig[:], 0.0, ALU.mult, ALU.add).then_inc(hs_ok, 1)
                dve.wait_ge(hs_ok, c + 1)
                v.tensor_copy(stO[:, c, C_HP:C_HS], hs[:, SEQ - 1:SEQ])
                v.tensor_copy(stO[:, c, C_HS:NC].rearrange("p (b i) -> p b i", i=1), seqs(hs[:, SEQ:EO])[:, :, ST - 1:ST])

            def branch(c):
                s = c % 2
                tile_is_read(dve, "gr", c)
                if c >= 2:
                    dve.wait_ge(y_hi, c - 1)
                    dve.wait_ge(y_lo, c - 1)
                link(v.tensor_tensor(hmul[s][:, 0:SEQ], hs[:, 0:SEQ], gel[s][:, 0:SEQ], ALU.mult))
                v.tensor_tensor(hmul[s][:, SEQ:T].rearrange("p (b j) -> p b j", j=NJ),
                                seqs(hs[:, SEQ:EO])[:, :, CW - 1:ST],
                                gel[s][:, SEQ:T].rearrange("p (b j) -> p b j", j=NJ), ALU.mult).then_inc(yt_ok, 1)

            sample_normal()
            for c in range(DC):
                recurrence(c)
                if c + 1 < DC:
                    conv_taps(c + 1)
                branch(c)
                if c == 5:
                    sample_out_lo()
            dve.wait_ge(y_lo, DC - 1)
            dve.wait_ge(y_hi, DC)
            v.tensor_tensor(act_lo[:, DC - 1, :], hmul[1][:], act_hi[:, DC - 1, :].bitcast(F32), ALU.subtract)\
                .then_inc(y_lo, 1)

            def logits(st):
                i = st % TT
                w = P * (i + 1)
                got_job(dve, ("qk", st))
                dve.wait_ge(tm_ok, st + 1)
                if st >= 3:
                    dve.wait_ge(tr_done, st - 2)
                read_job(v.tensor_tensor_reduce(pr[st % 3][:, 0:w], bank(("qk", st))[:, 0:w], tm[st % 2][:, 0:w],
                                                -1.0, 3.0e38, ALU.add, ALU.min, stat[:, 24 + st % 2:25 + st % 2]),
                         ("qk", st))

            def normal(st):
                w = P * (st % TT + 1)
                dve.wait_ge(exp_ok, st + 1)
                link(v.reciprocal(stat[:, 28 + st % 2:29 + st % 2], stat[:, 26 + st % 2:27 + st % 2]))
                v.tensor_scalar(pr[st % 3][:, 0:w], pr[st % 3][:, 0:w], stat[:, 28 + st % 2:29 + st % 2], None,
                                ALU.mult).then_inc(p_ok, 1)

            def attend_out_lo(m):
                dve.wait_ge(o_hi, m + 1)
                v.tensor_tensor(act_lo[:, 8 + m, 0:SEQ], psX[3][:], act_hi[:, 8 + m, 0:SEQ].bitcast(F32),
                                ALU.subtract).then_inc(o_lo, 1)

            def attend(st):
                if st < STEPS:
                    logits(st)
                if 1 <= st <= STEPS:
                    normal(st - 1)
                if st >= 10 and (st - 10) % 8 == 0:
                    attend_out_lo((st - 10) // 8)

            for i in range(2 * DC):
                attend(2 * i)
                if i % 2:
                    j = i // 2
                    t = FIRST_TILE["rnn"] + 2 * j
                    got_tile(dve, t)
                    tile_is_read(dve, "ga", j)
                    if j == 0:
                        dve.wait_ge(x_saved, 16)
                    if j == OROW_CHUNK:
                        dve.wait_ge(out_done, 16 * (2 + TT + 1 + 4))
                    read_tile(v.scalar_tensor_tensor(two(x[:, j, :]), two(sg[j % 2][:]), 1.0, acc(t),
                                                     ALU.add, ALU.mult), t)
                attend(2 * i + 1)
            for st in range(STEPS, STEPS + 3):
                attend(st)

            def lower(dst, k, hi, hi_ok, lo_ok):
                dve.wait_ge(hi_ok, k + 1)
                v.tensor_tensor(dst, hmul[k % 2][:], hi.bitcast(F32), ALU.subtract).then_inc(lo_ok, 1)

            def merged_lower(k):
                dve.wait_ge(m_hi, k + 1)
                v.scalar_tensor_tensor(act_lo[:, k, :], hmul[k % 2][:], 0.5, act_hi[:, k, :].bitcast(F32),
                                       ALU.mult, ALU.subtract).then_inc(m_lo, 1)

            for j in range(DC):
                t = FIRST_TILE["att"] + 2 * j
                got_tile(dve, t)
                tile_is_read(dve, "gb", j)
                if j == 0:
                    dve.wait_ge(pv_done, STEPS)
                if j >= 2:
                    dve.wait_ge(m_hi, j - 1)
                    dve.wait_ge(m_lo, j - 1)
                read_tile(v.scalar_tensor_tensor(two(hmul[j % 2][:]), two(sg[j % 2][:]), 1.0, acc(t),
                                                 ALU.add, ALU.mult), t)
                tile_is_read(dve, "att", j)
                tile_is_read(dve, "rnn", j)
                v.tensor_tensor(hmul[j % 2][:], hmul[j % 2][:], x[:, j, :], ALU.add).then_inc(m_t, 1)
                if j >= 1:
                    merged_lower(j - 1)
                if j >= 1 and j - 1 <= TT:
                    tt = j - 1
                    c0, c1 = (P * tt, P * (tt + 1)) if tt < TT else (SEQ, T)
                    dve.wait_ge(p_hi_ok, tt + 1)
                    read_job(v.tensor_tensor(p_lo[:, :, c0:c1],
                                             bank(("p", tt))[:, 0:2 * (c1 - c0)].rearrange("p (k t) -> p k t", k=2),
                                             p_hi[:, :, c0:c1].bitcast(F32), ALU.subtract), ("p", tt))
            merged_lower(DC - 1)

            def add_square(k, c):
                i = DC * k + c
                dve.wait_ge(sq_ok, i + 1)
                if c == 0:
                    ins = v.tensor_copy(sqacc[:], sqt[i % 2][:])
                else:
                    dve.wait_ge(sqacc_ok, i)
                    ins = v.tensor_tensor(sqacc[:], sqacc[:], sqt[i % 2][:], ALU.add)
                ins.then_inc(sqacc_ok, 1)

            def row_factor(jobs):
                for k, job in enumerate(jobs):
                    got_job(dve, job)
                    half = rb[:, HT * k:HT * (k + 1)]
                    read_job(v.tensor_scalar(half, bank(job)[:, 0:HT], 1.0 / D, EPS, ALU.mult, ALU.add), job)
                    job_read(dve, job)
                    v.reciprocal(half, half).then_inc(rb_v, 1)

            dve.wait_ge(x_back, 16)
            for j in range(DC):
                t = FIRST_TILE["wo"] + j
                got_tile(dve, t)
                read_tile(v.tensor_tensor(two(x[:, j, :]), two(x[:, j, :]), acc(t), ALU.add), t)
                if j >= 1:
                    add_square(0, j - 1)
            add_square(0, DC - 1)
            row_factor(("ss1a", "ss1b"))
            dve.wait_ge(rb_a, 2)
            norm(1, R_FFN, rb[:])

            k = 0
            for half, (f0, fn) in enumerate(FFN_HALVES):
                t0 = FIRST_TILE["gate"] + half * (2 * FA + DC)
                for f in range(fn):
                    t = t0 + 2 * f + 1
                    tile_is_read(dve, "gate", k)
                    got_tile(dve, t)
                    if k >= 2:
                        dve.wait_ge(f_hi, k - 1)
                        dve.wait_ge(f_lo, k - 1)
                    elif k == 1:
                        dve.wait_ge(n_lo_p, 8)
                    read_tile(v.tensor_tensor(two(hmul[k % 2][:]), two(sg[k % 2][:]), acc(t), ALU.mult), t)
                    if f >= 1:
                        lower(act_lo[:, f - 1, :], k - 1, act_hi[:, f - 1, :], f_hi, f_lo)
                    k += 1
                lower(act_lo[:, fn - 1, :], k - 1, act_hi[:, fn - 1, :], f_hi, f_lo)
                for j in range(DC):
                    t = t0 + 2 * fn + j
                    got_tile(dve, t)
                    read_tile(v.tensor_tensor(two(x[:, j, :]), two(x[:, j, :]), acc(t), ALU.add), t)
                    if half and j >= 1:
                        add_square(1, j - 1)
            add_square(1, DC - 1)
            row_factor(("ss2a", "ss2b"))
            dve.wait_ge(rb_a, 4)
            norm(2, R_PLE, rb[:])
            for j in range(DC):
                t = FIRST_TILE["pg"] + j
                got_tile(dve, t)
                tile_is_read(dve, "pg", j)
                tile_is_read(dve, "pp", j)
                if j == 1:
                    dve.wait_ge(n_lo_p, 12)
                elif j >= 2:
                    dve.wait_ge(xn_ok, j - 1)
                link(v.scalar_tensor_tensor(hmul[j % 2][:], sg[j % 2][:], 1.0, pp[:, j, :], ALU.add, ALU.mult))
                v.scalar_tensor_tensor(x[:, j, :], hmul[j % 2][:], 0.5, x[:, j, :], ALU.mult, ALU.add)\
                    .then_inc(xn_ok, 1)
                if j >= 1:
                    add_square(2, j - 1)
            add_square(2, DC - 1)
            got_job(dve, "ss3")
            link(v.memset(stat[:, 40 + TT:41 + TT], float(D)))
            ins = v.tensor_copy(stat[:, 40:40 + TT], bank("ss3")[:, 0:TT])
            link(ins)
            ins = v.tensor_copy(stat[0:NS, 40 + TT:41 + TT], bank("ss3")[0:NS, TT:TT + 1])
            read_job(ins, "ss3")
            job_read(dve, "ss3")
            inverse_mean(stat[:, 40:40 + TT + 1], stat[:, 40:40 + TT + 1]).then_inc(fs_v, 1)
            dve.wait_ge(fs_a, 1)
            for t in range(TT + 1):
                rows = P if t < TT else NS
                job = ("y", t, 1)
                got_job(dve, job)
                read_job(v.tensor_scalar(ytok[0:rows, t, 512:D], bank(job)[0:rows, :], stat[0:rows, 48 + t:49 + t],
                                         None, ALU.mult), job)

        @block.gpsimd
        def _(pool):
            g_ = nc.gpsimd
            steps = [0]

            def link(ins):
                steps[0] += 1
                ins.then_inc(pool_step, 1)
                pool.wait_ge(pool_step, steps[0])

            def lower_weights(n):
                if n >= len(UNITS):
                    return
                _, _, (_, _, rc, _, cc, _, _) = UNITS[n]
                s = n % RING
                pool.wait_ge(w_hi, n + 1)
                g_.tensor_tensor(wlo[:, s, 0:rc, 0:cc], wraw[:, s, 0:rc, 0:cc], whi[:, s, 0:rc, 0:cc].bitcast(F32),
                                 ALU.subtract).then_inc(w_lo, 1)

            def norm_lo(k, c):
                pool.wait_ge(n_hi, DC * k + c + 1)
                g_.tensor_tensor(h_lo[:, c, :], nbuf[c % 4][:], h_hi[:, c, :].bitcast(F32), ALU.subtract)\
                    .then_inc(n_lo_p, 1)

            def y_lower(c):
                pool.wait_ge(y_hi, c + 1)
                if c == 0:
                    pool.wait_ge(ktok_out[0], 16 * 3)
                    pool.wait_ge(ktok_out[1], 16 * 2)
                if c == 5:
                    pool.wait_ge(spv_b, NB)
                g_.tensor_tensor(act_lo[:, c, :], hmul[c % 2][:], act_hi[:, c, :].bitcast(F32), ALU.subtract)\
                    .then_inc(y_lo, 1)

            def causal(ap, fill):
                return g_.affine_select(out=ap, in_=ap, compare_op=ALU.is_ge, fill=fill, base=0,
                                        pattern=[[-1, P]], channel_multiplier=1)

            def own_new_keys(ap, fill):
                v = ap.rearrange("p (b j) -> p b j", j=NJ)
                link(g_.affine_select(out=v, in_=v, compare_op=ALU.is_ge, fill=fill, base=0,
                                      pattern=[[-NJ, NB], [-1, NJ]], channel_multiplier=1))
                return g_.affine_select(out=v, in_=v, compare_op=ALU.is_ge, fill=fill, base=NJ - 1,
                                        pattern=[[NJ, NB], [0, NJ]], channel_multiplier=-1)

            link(g_.memset(ident[:], 0.0))
            g_.affine_select(out=ident[:], in_=ident[:], compare_op=ALU.not_equal, fill=1.0, base=0,
                             pattern=[[-1, P]], channel_multiplier=1).then_inc(ident_ok, 1)
            g_.memset(stat[:], 1.0).then_inc(pool_const, 1)
            g_.memset(iwtok[:], 0.0).then_inc(ident_ok, 1)
            link(g_.memset(mask0[:], 0.0))
            link(causal(mask0[:], OFF))
            lower_weights(0)
            for c in range(1, DC, 2):
                norm_lo(0, c)
                if c < DC - 1:
                    lower_weights(1 + c // 2)
            job_read(pool, ("x", DC - 2))
            job_read(pool, ("x", DC - 1))
            link(g_.memset(sel[:], 0.0))
            v = sel[:].rearrange("p g (b h j) -> p (g b) h j", b=NB // 2, h=NH)
            link(g_.affine_select(out=v, in_=v, compare_op=ALU.not_equal, fill=1.0, base=0,
                                  pattern=[[-NJ, NB], [0, NH], [-1, NJ]], channel_multiplier=1))
            link(g_.memset(hm[:], 1.0))
            link(g_.affine_select(out=hm[:], in_=hm[:], compare_op=ALU.is_ge, fill=0.0, base=0,
                                  pattern=[[-NS, NB // 2], [-NJ, NH]], channel_multiplier=1))
            g_.affine_select(out=hm[:], in_=hm[:], compare_op=ALU.is_ge, fill=0.0, base=NJ - 1,
                             pattern=[[NS, NB // 2], [NJ, NH]], channel_multiplier=-1).then_inc(pool_const, 1)
            for n in range(len(UNITS)):
                if n == U["q"] + 1:
                    all_read(pool, "iq", HP)
                    pool.wait_ge(n_t, DC)
                    link(g_.memset(iqbd[:], 0.0))
                    for h in range(2):
                        rows = slice(HD * h, HD * (h + 1))
                        dst = iqbd[rows].rearrange("p b (m h j) -> p b m h j", h=2, j=NJ)[:, :, :, h, :]
                        src = iqT[rows, :, SEQ:T].rearrange("p m (b j) -> p b m j", j=NJ)
                        for m in range(HP):
                            g_.tensor_copy(dst[:, :, m, :], src[:, :, m, :]).then_inc(iqbd_ok, 1)
                        pool.wait_ge(iqbd_ok, HP * (h + 1))
                if n - U["q"] in range(2, 2 + TT - 1):
                    i = n - U["q"] - 1
                    pool.wait_ge(idx_acc, NH * i)
                    causal(score[i][:, P * i:P * (i + 1)], MASKED).then_inc(masked_in, 1)
                if n == U["xr"] - 1:
                    pool.wait_ge(x_saved, 16)
                    for s in range(2):
                        ins = g_.memset(xe[s][:, 0:CW - 1], 0.0)
                        if s:
                            ins.then_inc(bd_zero, 1)
                        else:
                            link(ins)
                if n == FIRST[("gate", 0)]:
                    for c in range(1, DC, 2):
                        norm_lo(1, c)
                if U["ga"] <= n < U["gb"]:
                    for s in (2 * (n - U["ga"]), 2 * (n - U["ga"]) + 1):
                        h, i = s // TT, s % TT
                        w = P * (i + 1)
                        if i == 0:
                            pool.wait_ge(th_in[h % 2], 16 * (h // 2 + 1))
                        if s == 0:
                            pool.wait_ge(mask_ok, TT)
                        if s >= 2:
                            job_read(pool, ("qk", s - 2))
                        m = mask0 if i == 0 else score[i]
                        g_.tensor_tensor(tm[s % 2][:, 0:w], th[h % 2][:, SEQ - w:SEQ], m[:], ALU.add).then_inc(tm_ok, 1)
                if TILES[UNITS[n][0]][0] == "gr" and TILES[UNITS[n][0]][1] >= 1:
                    y_lower(TILES[UNITS[n][0]][1] - 1)
                lower_weights(n + RING)
                if n == U["q"] + HP:
                    pool.wait_ge(ss_copied, 1)
                    job_read(pool, "sidx")
                    own_new_keys(score_s[:, PAST:SK], MASKED).then_inc(masked_in, 1)
                    pool.wait_ge(masked_in, TT)
                if n == U["q"] + HP + 1:
                    all_read(pool, "q", HP)
                    job_read(pool, ("iks", 3))
                    pool.wait_ge(sdots, 1)
                    link(g_.memset(qbd[:], 0.0))
                    for h in range(2):
                        rows = slice(HD * h, HD * (h + 1))
                        for m in range(HP):
                            c0 = NJ * (2 * m + h)
                            g_.tensor_copy(qbd[rows, :, m, c0:c0 + NJ],
                                           qT[rows, m, SEQ:T].rearrange("p (b j) -> p b j", j=NJ)).then_inc(qbd_ok, 1)
                        pool.wait_ge(qbd_ok, HP * (h + 1))
                    job_read(pool, ("idx", NH * (TT - 1) - 1))
                    g_.memset(bd[:], 0.0).then_inc(bd_zero, 1)
                if n == U["k"] + HP - 1:
                    pool.wait_ge(topk_s_ok, 1)
                    own_new_keys(score_s[:, PAST:SK], OFF).then_inc(mask_ok, 1)
                    pool.wait_ge(mask_ok, 1)
                if n == U["ga"] - 3:
                    for i in range(1, TT):
                        pool.wait_ge(topk_ok, i)
                        causal(score[i][:, P * i:P * (i + 1)], OFF).then_inc(mask_ok, 1)
                if n == U["pg"] - 1:
                    for c in range(1, DC, 2):
                        norm_lo(2, c)

        @block.tensor
        def _(pe):
            te = nc.tensor

            def start_job(job):
                n = AUX[job]
                if n >= 2:
                    pe.wait_ge(aux_read[n % 2], n // 2)
                return bank(job)

            def end_job(ins):
                return ins.then_inc(aux_done, 1)

            def turn(out, src):
                rows = src.shape[0]
                return te.transpose(out, src, ident[0:rows, 0:rows])

            operands = {"h": (h_hi, h_lo), "y": (act_hi, act_lo), "m": (act_hi, act_lo), "f": (act_hi, act_lo),
                        "p": (p_hi, p_lo)}

            def wait_operand(n, c):
                kind = TILES[UNITS[n][0]][0]
                firsts = (0, FIRST[("gate", 0)], U["pg"])
                if n in firsts:
                    k = firsts.index(n)
                    if c % 2:
                        pe.wait_ge(n_lo_p, 4 * k + c // 2 + 1)
                    else:
                        pe.wait_ge(n_lo_v, 4 * k + c // 2 + 1)
                elif n == U["ga"] + 1:
                    pe.wait_ge(y_lo, c + 1)
                elif n == U["gb"] + 1:
                    pe.wait_ge(o_lo, c + 1)
                    pe.wait_ge(so_lo, 2 * HP)
                elif n == U["wo"]:
                    pe.wait_ge(m_lo, c + 1)
                elif n == U["pp"]:
                    job_read(pe, ("p", TT - 1))
                    job_read(pe, ("p", TT))
                elif n in (FIRST[("down", 0, False)], FIRST[("down", 0, False)] + 1):
                    pe.wait_ge(f_lo, c + 1)
                elif n in (FIRST[("down", 0, True)], FIRST[("down", 0, True)] + 1):
                    pe.wait_ge(f_lo, FA + c + 1)

            def run(n, first=True, last=True):
                t, part, (_, _, rc, _, cc, operand, k0) = UNITS[n]
                parts = len(TILES[t][2])
                s = n % RING
                if first:
                    if part == 0 and t >= 2:
                        pe.wait_ge(tile_read[t % 2], t // 2)
                    pe.wait_ge(w_lo, n + 1)
                b0 = 2 * (t % 2)
                if operand == "o":
                    hi, lo = act_hi[:, 8:FA, :], act_lo[:, 8:FA, :]
                else:
                    hi, lo = operands[operand][0][:], operands[operand][1][:]
                for c in range(0 if first else rc // 2, rc if last else rc // 2):
                    wait_operand(n, k0 + c)
                    for w, m in ((whi, hi), (whi, lo), (wlo, hi)):
                        for half in range(2):
                            ins = te.matmul(psD[0:cc, b0 + half, 0:HT], w[:, s, c, 0:cc],
                                            m[:, k0 + c, HT * half:HT * (half + 1)],
                                            start=(part == 0 and c == 0 and w is whi and m is hi),
                                            stop=(part == parts - 1 and c == rc - 1 and w is wlo))
                if last:
                    ins.then_inc(w_used, 1)

            def run_around(n, work):
                run(n, last=False)
                work()
                run(n, first=False)

            def x_chunk(c):
                x_bank = start_job(("x", c))
                if c == 0:
                    for t in range(TT):
                        pe.wait_ge(x_in[t], 16)
                for t in range(TT):
                    ins = turn(x_bank[:, P * t:P * (t + 1)], xtok[:, t, P * c:P * (c + 1)])
                end_job(ins)

            pe.wait_ge(ident_ok, 1)
            pe.wait_ge(prm_in, 16 * 11)
            b = start_job("prm")
            for c in range(DC):
                ins = turn(b[:, NR * c:NR * (c + 1)], prm[:, P * c:P * (c + 1)])
            end_job(ins)
            b = start_job("xs")
            pe.wait_ge(x_in[TT], 16)
            for c in range(DC):
                ins = turn(b[:, NS * c:NS * (c + 1)], xtok[0:NS, TT, P * c:P * (c + 1)])
            end_job(ins)
            for c in range(2):
                x_chunk(c)
            b = start_job("rstd_a")
            pe.wait_ge(ones_ok, 1)
            pe.wait_ge(diag_ok, 2)
            for t in range(TT):
                ins = te.matmul(b[:, P * t:P * (t + 1)], ones[:], diag[:, t, :], start=True, stop=True)
            end_job(ins)
            b = start_job("rstd_b")
            end_job(te.matmul(b[:, 0:NS], ones[0:NS, :], diag[0:NS, TT, 0:NS], start=True, stop=True))
            for c in range(2, DC):
                x_chunk(c)
            run(0)
            for n in range(1, U["ik"]):
                run(n)
            pe.wait_ge(idxp_in, 16 * 2 * NB * NPG)
            for n in range(4):
                b = start_job(("iks", n))
                for k in range(4):
                    ins = turn(b[:, P * k:P * (k + 1)], idxp[:, 4 * n + k].rearrange("p r d -> p (r d)"))
                end_job(ins)
            pe.wait_ge(small_in, 32)
            w = LW // 2
            for k, job in enumerate(("lines_a", "lines_b")):
                b = start_job(job)
                end_job(te.matmul(b[0:NH, 0:w], relb[:], onehot[:, w * k:w * (k + 1)], start=True, stop=True))
            b = start_job("selT")
            pe.wait_ge(pool_const, 2)
            for g in range(2):
                ins = turn(b[:, NS * g:NS * (g + 1)], sel[:, g, :])
            end_job(ins)
            run(U["ik"])
            run(U["q"], last=False)
            b = start_job("ik")
            tile_is_read(pe, "ik", 0)
            kw = HD + NH
            for t in range(TT + 1):
                c0, c1 = (P * t, P * (t + 1)) if t < TT else (SEQ, T)
                ins = turn(b[0:c1 - c0, kw * t:kw * (t + 1)], ikw[0:kw, c0:c1])
            end_job(ins)

            def head_rows(h):
                return slice(HD * (h % 2), HD * (h % 2) + HD)

            def index_dots(s):
                i, h = 1 + s // NH, s % NH
                job = ("idx", s)
                b = start_job(job)
                end_job(te.matmul(b[:, 0:P * (i + 1)], iqT[head_rows(h), h // 2, P * i:P * (i + 1)],
                                  ik2[head_rows(h), 0:P * (i + 1)], start=True, stop=True))

            pe.wait_ge(ik_dup, 16)
            for j in range(HP):
                run(U["q"] + j, first=j > 0)
                for s in range(6 * j, 6 * j + 6):
                    index_dots(s)

            pe.wait_ge(iwcol_ok, 1)
            job_read(pe, "selT")
            b = start_job("iwcol")
            for g in range(2):
                ins = te.matmul(b[:, NH * g:NH * (g + 1)], sel[:, g, :], iwtok[0:NS, TT, :], start=True, stop=True)
            end_job(ins)
            pe.wait_ge(iqbd_ok, 2 * HP)
            job_read(pe, ("iks", 2))
            job_read(pe, ("iks", 3))
            for q in range(NB):
                rows = slice(NS * (q % 4), NS * (q % 4) + NS)
                out = psX[2 + q // 4]
                te.matmul(out[rows, 0:PAST], iqbd[:, q, :], iks[:, q, :], start=True, stop=True,
                          tile_position=(0, NS * (q % 4)))
                ins = te.matmul(out[rows, PAST:SK], iqbd[:, q, :], ik2[:, SEQ:T], start=True, stop=True,
                                tile_position=(0, NS * (q % 4)))
            ins.then_inc(sdots, 1)
            run(U["k"])
            b = start_job("sidx")
            pe.wait_ge(rs_ok, 2)
            for g in range(2):
                ins = te.matmul(b[0:NS, 0:SK], selT[:, g, :], rs_s[:, g, :], start=(g == 0), stop=(g == 1))
            end_job(ins)
            for n in range(U["k"] + 1, U["v"]):
                run(n)

            def rows_out(kind, src, t):
                c0, c1 = (P * t, P * (t + 1)) if t < TT else (SEQ, T)
                b = start_job((kind, t))
                for m in range(HP):
                    ins = turn(b[0:c1 - c0, P * m:P * (m + 1)], src[:, m, c0:c1])
                end_job(ins)

            def past_turn(q):
                pe.wait_ge(kpg_in[q % 2], 16 * NPG * (q // 2 + 1))
                for g in range(NPG):
                    b = start_job(("kts", q, g))
                    for m in range(HP):
                        ins = turn(b[:, PG * m:PG * (m + 1)], kpg[q % 2][:, g, P * m:P * (m + 1)])
                    end_job(ins)

            def past_logits(q):
                if q == 0:
                    pe.wait_ge(qbd_ok, 2 * HP)
                job_read(pe, ("kts", q, 0))
                job_read(pe, ("kts", q, 1))
                rows = slice(NS * (q % 4), NS * (q % 4) + NS)
                out = psX[2 + q // 4]
                for m in range(HP):
                    te.matmul(out[rows, 0:PAST], qbd[:, q, m, :], kts[q % 2][:, m, :], start=(m == 0),
                              stop=(m == HP - 1), tile_position=(0, NS * (q % 4)))
                for m in range(HP):
                    ins = te.matmul(out[rows, PAST:SK], qbd[:, q, m, :], kT[:, m, SEQ:T], start=(m == 0),
                                    stop=(m == HP - 1), tile_position=(0, NS * (q % 4)))
                ins.then_inc(slogit_b, 1)

            def k_rows_first():
                all_read(pe, "k", HP)
                rows_out("kout", kT, 0)

            run_around(U["v"], k_rows_first)
            rows_out("kout", kT, 1)
            run_around(U["v"] + 1, lambda: rows_out("kout", kT, 2))
            rows_out("kout", kT, 3)

            def k_rows_last():
                rows_out("kout", kT, TT)
                past_turn(0)

            def past_step(q):
                past_turn(q)
                past_logits(q - 1)

            run_around(U["v"] + 2, k_rows_last)
            past_step(1)
            run_around(U["v"] + 3, lambda: past_step(2))
            past_step(3)
            run_around(U["xr"], lambda: past_step(4))
            past_step(5)
            past_step(6)
            all_read(pe, "v", HP)
            rows_out("vout", vT, 0)
            rows_out("vout", vT, 1)
            past_step(7)
            for t in range(2, TT + 1):
                rows_out("vout", vT, t)
            past_logits(7)

            def gate_sums(c, g):
                for k in range(2):
                    b = start_job(("gate", c, g, k))
                    if g == 0 and k == 0:
                        pe.wait_ge(xc_ok, c + 1)
                        if c == 0:
                            pe.wait_ge(bd_in, 64)
                    end_job(te.matmul(b[:, 0:EH], bd[:, c, g, :], xc[c % 2][:, EH * k:EH * (k + 1)],
                                      start=True, stop=True))

            def past_values(q):
                pe.wait_ge(kpg_in[q % 2], 16 * NPG * (NB // 2 + q // 2 + 1))
                g, r = q // 4, q % 4
                for m in range(HP):
                    out = psX[2][:, 64 * m + 8 * q:64 * m + 8 * q + 8]
                    c0 = NS * r + 8 * m
                    for k in range(NPG):
                        te.matmul(out, kpg[q % 2][:, k, P * m:P * (m + 1)], pts[:, k, g, c0:c0 + 8],
                                  start=(k == 0), stop=False)
                    ins = te.matmul(out, vtok_s[:, P * m:P * (m + 1)], ptn[:, g, c0:c0 + 8], start=False, stop=True)
                ins.then_inc(spv_b, 1)

            pe.wait_ge(mask_ok, 1)
            for g in range(2):
                b = start_job(("smask", g))
                end_job(te.matmul(b[:, 0:SK], sel[:, g, :], score_s[:, 0:SK], start=True, stop=True))
            run(U["xr"] + 1)
            gate_sums(0, 0)
            gate_sums(0, 1)
            b = start_job("spt")
            pe.wait_ge(sp_ok, 2)
            for kk in range(NPG):
                for g in range(2):
                    ins = turn(b[:, P * (2 * kk + g):P * (2 * kk + g + 1)], ps_s[:, g, PG * kk:PG * (kk + 1)])
            end_job(ins)
            b = start_job("spn")
            for g in range(2):
                ins = turn(b[0:NS, P * g:P * (g + 1)], ps_s[:, g, PAST:SK])
            end_job(ins)
            run(U["xr"] + 2)
            job_read(pe, "spt")
            job_read(pe, "spn")
            job_read(pe, ("vout", TT))
            past_values(0)
            for c in range(1, DC):
                n = U["xr"] + 1 + 2 * c
                run_around(n, lambda: gate_sums(c, 0))
                gate_sums(c, 1)
                if 2 * c - 1 < NB:
                    past_values(2 * c - 1)
                if c + 1 < DC:
                    run(n + 1)
                if 2 * c < NB:
                    past_values(2 * c)

            def attend_products(s):
                h, i = s // TT, s % TT
                w = P * (i + 1)
                b = start_job(("qk", s))
                end_job(te.matmul(b[:, 0:w], qT[head_rows(h), h // 2, P * i:w], kT[head_rows(h), h // 2, 0:w],
                                  start=True, stop=True))

            def attend_turn(s):
                i = s % TT
                pe.wait_ge(p_ok, s + 1)
                if s == 0:
                    pe.wait_ge(so_lo, 2 * HP)
                else:
                    pe.wait_ge(pT_ok, s)
                for k in range(i + 1):
                    ins = turn(psX[2][:, P * k:P * (k + 1)], pr[s % 3][:, P * k:P * (k + 1)])
                ins.then_inc(tr_done, 1)

            def attend_values(s):
                h, i = s // TT, s % TT
                pe.wait_ge(pT_ok, s + 1)
                if s == 0:
                    job_read(pe, ("smask", 1))
                elif s % (2 * TT) == 0:
                    pe.wait_ge(o_lo, s // (2 * TT))
                for k in range(i + 1):
                    ins = te.matmul(psX[3][head_rows(h), P * i:P * (i + 1)], vtok[:, k, HD * h:HD * (h + 1)],
                                    pT[s % 2][:, k, :], start=(k == 0), stop=(k == i),
                                    tile_position=(0, HD * (h % 2)))
                ins.then_inc(pv_done, 1)

            def attend(s):
                if s < STEPS:
                    attend_products(s)
                if 2 <= s < STEPS + 2:
                    attend_turn(s - 2)
                if 3 <= s:
                    attend_values(s - 3)

            for n in range(U["ga"], U["gb"]):
                s = 2 * (n - U["ga"])
                run_around(n, lambda: attend(s))
                attend(s + 1)
                if n == U["ga"] + 1:
                    for k, job in enumerate(("st_a", "st_b")):
                        b = start_job(job)
                        for c in range(4):
                            ins = turn(b[0:NC, P * c:P * (c + 1)], stO[:, 4 * k + c, :])
                        end_job(ins)
            run_around(U["gb"], lambda: attend(STEPS))
            attend(STEPS + 1)
            attend(STEPS + 2)

            for n in range(U["gb"] + 1, U["wo"]):
                run(n)
                k = n - U["gb"]
                if k >= 2 and k % 2 == 0 and k // 2 - 1 <= TT:
                    t = k // 2 - 1
                    c0, c1 = (P * t, P * (t + 1)) if t < TT else (SEQ, T)
                    w = c1 - c0
                    b = start_job(("p", t))
                    pe.wait_ge(p_in, 32)
                    for kk in range(2):
                        ins = turn(b[:, w * kk:w * (kk + 1)], ptok[0:w, t, P * kk:P * (kk + 1)])
                    end_job(ins)

            def sum_squares(k, jobs):
                pe.wait_ge(sqacc_ok, DC * (k + 1))
                for half, job in enumerate(jobs):
                    b = start_job(job)
                    end_job(te.matmul(b[:, 0:HT], ones[:], sqacc[:, HT * half:HT * (half + 1)], start=True, stop=True))

            for n in range(U["wo"], U["pp"] + 2):
                run(n)
            sum_squares(0, ("ss1a", "ss1b"))
            for n in range(U["pp"] + 2, U["pp2"] + 2):
                run(n)
            sum_squares(1, ("ss2a", "ss2b"))
            for n in range(U["pp2"] + 2, U["pg"]):
                run(n)
            for n in range(U["pg"], len(UNITS)):
                run(n)
            b = start_job("ss3")
            pe.wait_ge(sqacc_ok, 3 * DC)
            for t in range(TT + 1):
                c0, c1 = (P * t, P * (t + 1)) if t < TT else (SEQ, T)
                ins = te.matmul(b[0:c1 - c0, t:t + 1], sqacc[:, c0:c1], ones[:, 0:1], start=True, stop=True)
            end_job(ins)
            pe.wait_ge(xf_ok, DC)
            for t in range(TT + 1):
                c0, c1 = (P * t, P * (t + 1)) if t < TT else (SEQ, T)
                for half in range(2):
                    b = start_job(("y", t, half))
                    for c in range(4):
                        ins = turn(b[0:c1 - c0, P * c:P * (c + 1)], pp[:, 4 * half + c, c0:c1])
                    end_job(ins)


_INS = ["x_prompt", "x_sample", "p_prompt", "p_sample", "cache_k", "cache_v", "cache_idx_k", "state_rglru_h",
        "state_conv", "page_table", "rel_bias", "norm_mix", "w_in", "conv_w", "conv_b", "w_rg_a", "b_rg_a",
        "w_rg_x", "b_rg_x", "lru_lambda", "w_rnn_out", "w_att_out", "w_o", "norm_ffn", "w_ffn_gate", "w_ffn_up",
        "w_ffn_down", "norm_ple", "w_ple_gate", "w_ple_proj", "norm_final"]
_OUTS = [("y_prompt", (1, SEQ, D)), ("y_sample", (NB, NJ, D)), ("k_prompt", (1, 1, SEQ, NH, HD)),
         ("v_prompt", (1, 1, SEQ, NH, HD)), ("idx_k_prompt", (1, 1, SEQ, HD)), ("h_prompt", (1, 1, D)),
         ("conv_prompt", (1, 1, CW - 1, D)), ("k_sample", (1, NB, NJ, NH, HD)), ("v_sample", (1, NB, NJ, NH, HD)),
         ("idx_k_sample", (1, NB, NJ, HD)), ("h_sample", (1, NB, D)), ("conv_sample", (1, NB, CW - 1, D))]


def kernel(**inputs):
    import numpy as _np
    import concourse.bacc as _bacc
    from concourse import mybir as _mybir
    from concourse.bass_utils import run_bass_kernel_spmd as _run

    nc = _bacc.Bacc("TRN2", target_bir_lowering=False, num_devices=1)
    arrays, ins, outs = {}, {}, {}
    held = {name: _np.ascontiguousarray(inputs[name]) for name in _INS}
    held["bias_onehot"] = bias_onehot()
    for name, array in held.items():
        arrays[f"in_{name}"] = array
        ins[name] = nc.dram_tensor(f"in_{name}", array.shape, _mybir.dt.from_np(array.dtype),
                                   kind="ExternalInput").ap()
    for name, shape in _OUTS:
        outs[name] = nc.dram_tensor(f"out_{name}", shape, _mybir.dt.float32, kind="ExternalOutput").ap()
    hybrid_decoder_step(nc, ins, outs)
    r = _run(nc, [arrays], core_ids=[0])
    return tuple(r.results[0][f"out_{name}"] for name, _ in _OUTS)
```

```python
from contextlib import ExitStack

import numpy as np

import concourse.bass as bass
from concourse import mybir

F32 = mybir.dt.float32
F32R = mybir.dt.float32r
I32 = mybir.dt.int32
ALU = mybir.AluOpType
ACT = mybir.ActivationFunctionType

P = 128
D = 1024
DC = D // P
SEQ = 512
NB = 8
NJ = 4
NS = NB * NJ
T = SEQ + NS
HT = T // 2
TT = SEQ // P
NH = 8
HD = 64
ATT = NH * HD
HP = NH // 2
PG = 128
NPG = 2
PAST = NPG * PG
SK = PAST + NS
DFF = 2816
FC = DFF // P
PD = 256
EPS = 1e-6
TOPK_P = SEQ // 4
TOPK_S = (PAST + NJ) // 4
NBUCK = 32
LW = 640
LMAX = 511
MASKED = -3.0e38
TAKEN = -3.4e38
TAKEN_BELOW = -3.3e38
PAD = -3.2e38
OFF = -1.0e30
RING = 4
UC = 8
CW = 4
EXT = CW - 1 + SEQ + NB * (CW - 1 + NJ)
EO = EXT - (CW - 1)
EH = EO // 2
S0 = SEQ + CW - 1
ST = CW - 1 + NJ
FA = 12
FFN_HALVES = ((0, FA), (FA, FC - FA))

R_MIX, R_FFN, R_PLE, R_FIN, R_CW, R_CB, R_BA, R_BX, R_LAM, R_SC, R_SH = 0, 1, 2, 3, 4, 8, 9, 10, 11, 12, 36
NR = 44
C_CP, C_CS, C_HP, C_HS, NC = 0, 3, 27, 28, 36

W_AT = dict(xr=0, gr=D, q=2 * D, k=2 * D + ATT, v=2 * D + 2 * ATT, iq=2 * D + 3 * ATT,
            ik=2 * D + 4 * ATT, ga=2 * D + 4 * ATT + HD + NH, gb=3 * D + 4 * ATT + HD + NH)


def plan_tiles():
    def w_in(kind, j, cols=P):
        return (kind, j, [("w_in", 0, DC, W_AT[kind] + P * j, cols, "h", 0)])

    def square(kind, j, weight, operand, chunks=DC):
        return (kind, j, [(weight, 0, chunks, P * j, P, operand, 0)])

    tiles = [w_in("iq", j) for j in range(HP)] + [w_in("ik", 0, HD + NH)]
    for kind in ("q", "k", "v"):
        tiles += [w_in(kind, j) for j in range(HP)]
    tiles.append(w_in("xr", 0))
    for c in range(DC):
        tiles += [w_in("xr", c + 1)] * (c + 1 < DC) + [w_in("gr", c)]
    for j in range(DC):
        tiles += [w_in("ga", j), square("rnn", j, "w_rnn_out", "y")]
    for j in range(DC):
        tiles += [w_in("gb", j), square("att", j, "w_att_out", "o", HP)]
    tiles += [square("wo", j, "w_o", "m") for j in range(DC)]
    pp = [square("pp", j, "w_ple_proj", "p", PD // P) for j in range(DC)]
    tiles += pp[0:DC // 2]
    for f0, fn in FFN_HALVES:
        for f in range(f0, f0 + fn):
            tiles += [square("gate", f, "w_ffn_gate", "h"), square("up", f, "w_ffn_up", "h")]
        half = fn // 2
        for j in range(DC):
            tiles.append(("down", j, [("w_ffn_down", f0 + half * k, half, P * j, P, "f", half * k)
                                      for k in range(2)]))
    tiles += pp[DC // 2:]
    tiles += [square("pg", j, "w_ple_gate", "h") for j in range(DC)]
    return tiles


TILES = plan_tiles()
UNITS = [(t, k, u) for t, (_, _, us) in enumerate(TILES) for k, u in enumerate(us)]
FIRST = {}
for _n, (_t, _k, _u) in enumerate(UNITS):
    FIRST.setdefault(TILES[_t][:2] if TILES[_t][0] != "down" else ("down", TILES[_t][1], UNITS[_n][2][1] >= FA), _n)
FIRST_TILE = {}
for _t, (_k, _j, _u) in enumerate(TILES):
    FIRST_TILE.setdefault(_k, _t)
NTH = {}
for _t, (_k, _j, _u) in enumerate(TILES):
    NTH[(_k, _j, _k == "down" and _u[0][1] >= FA)] = _t
LAST_UNIT = {t: n for n, (t, _, _) in enumerate(UNITS)}
STEPS = NH * TT
SO_CHUNK = 5
OROW_CHUNK = 5


def plan_aux():
    jobs = ["prm", "xs", ("x", 0), ("x", 1), "rstd_a", "rstd_b"] + [("x", c) for c in range(2, DC)]
    jobs += [("iks", n) for n in range(4)] + ["lines_a", "lines_b", "selT"]
    jobs += ["ik"] + [("idx", s) for s in range(NH * (TT - 1))] + ["iwcol", "sidx"]
    jobs += [("kout", t) for t in range(TT + 1)]
    for b in range(NB - 1):
        jobs += [("kts", b, 0), ("kts", b, 1)]
    jobs += [("vout", t) for t in range(TT + 1)] + [("kts", NB - 1, 0), ("kts", NB - 1, 1)]
    jobs += [("smask", 0), ("smask", 1)]
    for c in range(DC):
        jobs += [("gate", c, 0, 0), ("gate", c, 0, 1), ("gate", c, 1, 0), ("gate", c, 1, 1)]
        if c == 0:
            jobs += ["spt", "spn"]
        if c == SO_CHUNK:
            jobs.append("so")
    for s in range(STEPS):
        jobs.append(("qk", s))
        if s == 3:
            jobs += ["st_a", "st_b"]
    jobs += [("p", t) for t in range(TT + 1)]
    jobs += [("ss", 1), ("ss", 2), ("ss", 3)]
    return jobs


AUX = {name: n for n, name in enumerate(plan_aux())}


def bias_onehot():
    n = np.maximum(LMAX - np.arange(LW), 0)
    exact = NBUCK // 2
    nf = np.maximum(n, 1).astype(np.float32)
    large = exact + (np.log(nf / np.float32(exact)) / np.float32(np.log(128 / exact))
                     * np.float32(NBUCK - exact)).astype(np.int32)
    bucket = np.where(n < exact, n, np.minimum(large, NBUCK - 1))
    return (np.arange(NBUCK)[:, None] == bucket[None, :]).astype(np.float32)


def hybrid_decoder_step(nc, a, o):
    n_pool = a["cache_k"].shape[1]
    free = [16512]
    spot = {}

    def place(name, shape, dt=F32, over=None, plus=0):
        size = 4 * int(np.prod(shape[1:]))
        if over is None:
            spot[name] = free[0]
            free[0] += (size + 31) // 32 * 32
        else:
            spot[name] = spot[over] + plus
        assert spot[name] + size <= 229344, (name, spot[name] + size - 229344)
        return nc.alloc_sbuf_tensor_at(name, shape, dt, offset=spot[name])

    wraw = place("wraw", [P, RING, UC, P])
    whi = place("whi", [P, RING, UC, P], F32R)
    wlo = place("wlo", [P, RING, UC, P], F32R)
    h_hi = place("h_hi", [P, DC, T], F32R)
    h_lo = place("h_lo", [P, DC, T], F32R)
    act_hi = place("act_hi", [P, FA, T], F32R)
    act_lo = place("act_lo", [P, FA, T], F32R)
    x = place("x", [P, DC, T])
    qT = place("qT", [P, HP, T])
    kT = place("kT", [P, HP, T])
    vtok = place("vtok", [P, TT, ATT])
    iqT = place("iqT", [P, HP, T])
    ikw = place("ikw", [P, T])
    ik2 = place("ik2", [P, T])
    score = [None] + [place(f"score{i}", [P, P * (i + 1)]) for i in range(1, TT)]
    score_s = place("score_s", [NS, SK + 8])
    mask0 = place("mask0", [P, P])
    ident = place("ident", [P, P])
    ones = place("ones", [P, P])
    prmT = place("prmT", [P, DC, NR])
    iwtok = place("iwtok", [P, TT + 1, NH])
    vtok_s = place("vtok_s", [NS, ATT])
    lru = place("lru", [P, 8, DC])
    stat = place("stat", [P, 64])
    sstat = place("sstat", [P, 8])
    top8 = place("top8", [P, 8])
    pt = place("pt", [1, NB * NPG], I32)
    hmul = [place(f"hmul{i}", [P, T]) for i in range(2)]
    tail = place("tail", [P, 1120])
    nbuf = hmul + [place(f"nbuf{i}", [P, T], F32, "tail", 4 * T * i) for i in range(2)]
    xtok = place("xtok", [P, TT + 1, D], F32, "act_hi")
    rb0 = place("rb0", [P, T], F32, "act_hi", 20480)
    lines = place("lines", [NH, LW], F32, "act_hi", 22656)
    idxp = place("idxp", [P, NB * NPG, 2, HD], F32, "act_lo")
    iks = place("iks", [P, NB, PAST], F32, "act_lo", 8192)
    prm = place("prm", [NR, D], F32, "act_lo", 17408)
    onehot = place("onehot", [NBUCK, LW], F32, "act_lo", 21504)
    relb = place("relb", [NBUCK, NH], F32, "act_lo", 24064)
    junk = place("junk", [P, D], F32, "iqT")
    diag = place("diag", [P, TT + 1, P], F32, "iqT", 4096)
    relu = [place(f"relu{i}", [P, SEQ], F32, "act_lo", 17920 + 2048 * i) for i in range(2)]
    iqbd = place("iqbd", [P, NB, NS], F32, "act_hi")
    rs_s = place("rs_s", [P, 2, SK], F32, "act_hi", 4096)
    sel = place("sel", [NS, 2, P], F32, "act_hi", 6400)
    selT = place("selT", [P, 2, NS], F32, "act_hi", 7424)
    hm = place("hm", [P, NB // 2, NH], F32, "act_hi", 7680)
    iwsc = place("iwsc", [P, NB // 2, NH], F32, "act_hi", 7808)
    iktok = place("iktok", [P, TT + 1, HD + NH], F32, "act_hi", 7936)
    vT = place("vT", [P, HP, T], F32, "x", 4 * T * (DC - HP))
    ktok = [place(f"ktok{i}", [P, ATT], F32, "act_lo", 2048 * i) for i in range(2)]
    kpg = [place(f"kpg{i}", [P, NPG, ATT], F32, "act_hi", 17408 + 4096 * i) for i in range(2)]
    kts = [place(f"kts{i}", [P, HP, PAST], F32, "act_lo", 17920 + 4096 * i) for i in range(2)]
    pts = place("pts", [P, NPG, 2, P], F32, "act_lo", 12032)
    ptn = place("ptn", [NS, 2, P], F32, "act_lo", 14080)
    ps_s = place("ps_s", [P, 2, SK], F32, "act_lo", 15104)
    qbd = place("qbd", [P, HP, NB, NS], F32, "act_hi", 13312)
    own = [place(f"own{i}", [P, ATT], F32, "act_lo", 17920 + 2048 * i) for i in range(2)]
    selT2 = place("selT2", [P, 2, NS], F32, "iqT", 4 * DC * 2 * P)
    bias_s = place("bias_s", [P, SK], F32, "ikw")
    bias_n = place("bias_n", [P, NJ], F32, "ikw", 1152)
    bd = place("bd", [P, DC, 2, P], F32, "iqT")
    line = 4 * (EXT + 5)
    xe = [place(f"xe{i}", [P, EXT], F32, "x", line * i) for i in range(2)]
    xc = [place(f"xc{i}", [P, EO], F32, "x", line * (2 + i)) for i in range(2)]
    rq = place("rq", [P, EO], F32, "x", line * 4)
    ig = place("ig", [P, EO], F32, "x", line * 5)
    sq = place("sq", [P, EO], F32, "x", line * 6)
    stO = place("stO", [P, DC, NC], F32, "x", line * 7)
    hs = place("hs", [P, EO], F32, "tail")
    gel = [place(f"gel{i}", [P, T], F32, "tail" if i else "ikw", 2304 if i else 2176) for i in range(2)]
    orow = place("orow", [NC, D], F32, "x", 4 * T * OROW_CHUNK)
    th = [place(f"th{i}", [P, SEQ], F32, "iqT", 2048 * i) for i in range(2)]
    tm = [place(f"tm{i}", [P, SEQ], F32, "iqT", 4096 + 2048 * i) for i in range(2)]
    pr = [place(f"pr{i}", [P, SEQ], F32, "vtok_s" if i == 2 else "ikw", 2048 * i % 4096) for i in range(3)]
    pT = [place(f"pT{i}", [P, TT, P], F32, "hmul0", 2048 * i) for i in range(2)]
    sg = [place(f"sg{i}", [P, T], F32, "tail", 2176 * i) for i in range(2)]
    p_hi = place("p_hi", [P, PD // P, T], F32R, "vtok")
    p_lo = place("p_lo", [P, PD // P, T], F32R, "ikw")
    ptok = place("ptok", [P, TT + 1, PD], F32, "qT")
    pp = place("pp", [P, DC, T], F32, "qT")
    sqacc = place("sqacc", [P, T], F32, "iqT")
    sqt = [place(f"sqt{i}", [P, T], F32, "iqT", 2176 * (1 + i)) for i in range(2)]
    spread = place("spread", [P, TT + 1, P], F32, "vtok", 4 * T * (PD // P))
    ytok = place("ytok", [P, TT + 1, D], F32, "act_hi")

    psD = nc.alloc_psum_tensor("psD", [P, 4, 512], F32)
    psX = [nc.alloc_psum_tensor(f"psX{i}", [P, 512], F32)[:] for i in range(2)]
    held = nc.alloc_psum_tensor("held", [P, 2, 512], F32)
    psX += [held[:, 0, :], held[:, 1, :]]

    lines_d = nc.dram_tensor("bias_lines", [NH, P, LW], F32, kind="Internal").ap()
    x_d = nc.dram_tensor("x_saved", [P, DC * T], F32, kind="Internal").ap()

    ctx = ExitStack()
    with ctx:
        def sem(name):
            return ctx.enter_context(nc.semaphore(name))

        def sems(name, n):
            return [sem(f"{name}{i}") for i in range(n)]

        w_loaded = sems("w_loaded", RING)
        w_hi, w_lo, w_used = sem("w_hi"), sem("w_lo"), sem("w_used")
        tile_read = sems("tile_read", 2)
        aux_done, aux_read = sem("aux_done"), sems("aux_read", 2)
        x_in, prm_in, page_in, idxp_in = sems("x_in", TT + 1), sem("prm_in"), sem("page_in"), sem("idxp_in")
        small_in, bd_in, bias_in = sem("small_in"), sem("bd_in"), sem("bias_in")
        kpg_in, th_in, p_in, x_back = sems("kpg_in", 2), sems("th_in", 2), sem("p_in"), sem("x_back")
        ik_dup, lines_saved, x_saved = sem("ik_dup"), sem("lines_saved"), sem("x_kept")
        out_done, ktok_out = sem("out_done"), sems("ktok_out", 2)
        ident_ok, ones_ok, pool_const = sem("ident_ok"), sem("ones_ok"), sem("pool_const")
        dve_step, pool_step, act_step = sem("dve_step"), sem("pool_step"), sem("act_step")
        sq_done, rstd_v, rstd_a, diag_ok = sem("sq_done"), sem("rstd_v"), sem("rstd_a"), sem("diag_ok")
        n_t, n_hi, n_lo_v, n_lo_p = sem("n_t"), sem("n_hi"), sem("n_lo_v"), sem("n_lo_p")
        xn_ok, sq_ok, sqacc_ok, spread_ok, rb_ok = sem("xn_ok"), sem("sq_ok"), sem("sqacc_ok"), sem("spread_ok"), sem("rb_ok")
        idx_acc, iqbd_ok, iwcol_ok, sdots = sem("idx_acc"), sem("iqbd_ok"), sem("iwcol_ok"), sem("sdots")
        rs_ok, ss_copied, masked_in = sem("rs_ok"), sem("ss_copied"), sem("masked_in")
        topk_ok, topk_s_ok, mask_ok = sem("topk_ok"), sem("topk_s_ok"), sem("mask_ok")
        qbd_ok, slogit_b, sexp_ok, sp_ok = sem("qbd_ok"), sem("slogit_b"), sem("sexp_ok"), sem("sp_ok")
        spv_b, own_ok, so_hi = sem("spv_b"), sem("own_ok"), sem("so_hi")
        lru_a, lru_v, bd_zero, xe_ok, tap0 = sem("lru_a"), sem("lru_v"), sem("bd_zero"), sem("xe_ok"), sem("tap0")
        xc_ok, q_lru, sqrt_ok, u_ok, hs_ok = sem("xc_ok"), sem("q_lru"), sem("sqrt_ok"), sem("u_ok"), sem("hs_ok")
        yt_ok, y_hi, y_lo = sem("yt_ok"), sem("y_hi"), sem("y_lo")
        tm_ok, exp_ok, p_ok, tr_done = sem("tm_ok"), sem("exp_ok"), sem("p_ok"), sem("tr_done")
        pT_ok, pv_done, o_hi, o_lo = sem("pT_ok"), sem("pv_done"), sem("o_hi"), sem("o_lo")
        m_t, m_hi, m_lo, p_hi_ok = sem("m_t"), sem("m_hi"), sem("m_lo"), sem("p_hi_ok")
        f_hi, f_lo, xf_ok, fs_v, fs_a = sem("f_hi"), sem("f_lo"), sem("xf_ok"), sem("fs_v"), sem("fs_a")
        y_turned, y_half = sem("y_turned"), sems("y_half", 2)

        def tiles_of(kind):
            return [t for t, (k, _, _) in enumerate(TILES) if k == kind]

        def acc(t):
            s = 2 * (t % 2)
            return psD[:, s:s + 2, 0:HT]

        def two(ap):
            return ap.rearrange("p (a b) -> p a b", a=2)

        def seqs(ap):
            return ap.rearrange("p (b c) -> p b c", c=ST)

        def bank(job):
            return psX[AUX[job] % 2]

        y_order = [(t, 0) for t in range(TT)] + [(t, 1) for t in range(TT)] + [(TT, 0), (TT, 1)]
        y_pairs = [psD[:, 2 * (t % 2) + k, :] for t in (len(TILES) - 2, len(TILES) - 1) for k in range(2)]
        y_bank = [psX[2], psX[3], *y_pairs, psX[1 - AUX[("ss", 3)] % 2], bank(("ss", 3)), psX[2], psX[3]]

        def ffn_iterations(eng, pairs, body):
            body(0)
            with eng.Fori(1, pairs // 2 - 1) as it:
                body(it)
            body(pairs // 2 - 1)

        def chunk(tensor, c):
            return tensor[:, c, :] if isinstance(c, int) else tensor[:, bass.ds(c, 1), :].rearrange("p o t -> p (o t)")

        def got_tile(eng, t, it=0):
            eng.wait_ge(w_used, LAST_UNIT[t] + 1 + 4 * it)

        def got_job(eng, job):
            eng.wait_ge(aux_done, AUX[job] + 1)

        def read_job(ins, job):
            return ins.then_inc(aux_read[AUX[job] % 2], 1)

        def read_tile(ins, t):
            return ins.then_inc(tile_read[t % 2], 1)

        def job_read(eng, job):
            n = AUX[job]
            eng.wait_ge(aux_read[n % 2], n // 2 + 1)

        def tile_is_read(eng, kind, j, last=False, it=0):
            t = NTH[(kind, j, last)]
            eng.wait_ge(tile_read[t % 2], t // 2 + 1 + 2 * it)

        def all_read(eng, kind, n):
            tile_is_read(eng, kind, n - 2)
            tile_is_read(eng, kind, n - 1)

        dve_lowers, pool_lowers = (0, 1, 2, 4, 6), (3, 5, 7)

        def norm_is_split(eng, k, c):
            s, mine = (n_lo_v, dve_lowers) if c in dve_lowers else (n_lo_p, pool_lowers)
            eng.wait_ge(s, len(mine) * k + mine.index(c) + 1)

        def x_is_new(eng, k, c):
            if k == 0:
                tile_is_read(eng, "wo", c)
            elif k == 1:
                tile_is_read(eng, "down", c, True)
            else:
                eng.wait_ge(xn_ok, c + 1)

        U = {k: FIRST[(k, 0)] for k in ("iq", "ik", "q", "k", "v", "xr", "ga", "gb", "wo", "pp", "pg")}
        U["pp2"] = FIRST[("pp", DC // 2)]
        h_last = (0, U["wo"], FIRST[("down", 0, True)])
        block = ctx.enter_context(nc.Block())

        @block.sync
        def _(sp):
            def load(n, it=0):
                _, _, (w, r0, rc, c0, cc, _, _) = UNITS[n]
                if n >= RING:
                    sp.wait_ge(w_lo, n - RING + 1 + 4 * it)
                columns = slice(c0, c0 + cc) if isinstance(it, int) else bass.ds(c0 + 2 * P * it, cc)
                src = a[w][0, P * r0:P * (r0 + rc), columns].rearrange("(c p) n -> p c n", p=P)
                sp.dma_start(wraw[:, n % RING, 0:rc, 0:cc], src).then_inc(w_loaded[n % RING], 16)

            def pages(dst, pool, b, got):
                for g in range(NPG):
                    page = sp.value_load(pt[0:1, NPG * b + g:NPG * b + g + 1], min_val=0, max_val=n_pool - 1)
                    src = a[pool][0, bass.ds(page, 1)].rearrange("o s h d -> (o s) (h d)")
                    sp.dma_start(dst[:, g, :], src).then_inc(got, 16)

            for t in range(TT):
                sp.dma_start(xtok[:, t, :], a["x_prompt"][0, P * t:P * (t + 1), :]).then_inc(x_in[t], 16)
            sp.dma_start(xtok[0:NS, TT, :], a["x_sample"].rearrange("b j d -> (b j) d")).then_inc(x_in[TT], 16)
            for row, name in ((R_MIX, "norm_mix"), (R_FFN, "norm_ffn"), (R_PLE, "norm_ple"), (R_CB, "conv_b"),
                              (R_BA, "b_rg_a"), (R_BX, "b_rg_x"), (R_LAM, "lru_lambda")):
                sp.dma_start(prm[row:row + 1, :], a[name]).then_inc(prm_in, 16)
            sp.dma_start(prm[R_FIN:R_FIN + 1, :], a["norm_final"].rearrange("(o d) -> o d", o=1)).then_inc(prm_in, 16)
            sp.dma_start(prm[R_CW:R_CW + CW, :], a["conv_w"][0]).then_inc(prm_in, 16)
            sp.dma_start(prm[R_SC:R_SH, :], a["state_conv"][0].rearrange("b i d -> (b i) d")).then_inc(prm_in, 16)
            sp.dma_start(prm[R_SH:NR, :], a["state_rglru_h"][0]).then_inc(prm_in, 16)
            for n in range(RING):
                load(n)
            sp.dma_start(pt[:], a["page_table"].rearrange("(o b) g -> o (b g)", o=1)).then_inc(page_in, 16)
            sp.dma_start(onehot[:], a["bias_onehot"]).then_inc(small_in, 16)
            sp.dma_start(relb[:], a["rel_bias"]).then_inc(small_in, 16)
            sp.wait_ge(page_in, 16)
            for b in range(NB):
                for g in range(NPG):
                    page = sp.value_load(pt[0:1, NPG * b + g:NPG * b + g + 1], min_val=0, max_val=n_pool - 1)
                    src = a["cache_idx_k"][0, bass.ds(page, 1)].rearrange("o s d -> (o s) d")
                    sp.dma_start(idxp[:, NPG * b + g], src.unsqueeze(1).broadcast_to([PG, 2, HD])).then_inc(idxp_in, 16)
                if b == NB // 2 - 1:
                    load(RING)
            job_read(sp, ("x", DC - 2))
            job_read(sp, ("x", DC - 1))
            sp.dma_start(x_d, x[:].rearrange("p c t -> p (c t)")).then_inc(x_saved, 16)
            for n in range(RING + 1, 8):
                load(n)
            job_read(sp, "lines_a")
            job_read(sp, "lines_b")
            sp.dma_start(lines_d, lines[:].unsqueeze(1).broadcast_to([NH, P, LW])).then_inc(lines_saved, 16)
            tile_is_read(sp, "ik", 0)
            sp.dma_start(ik2[HD:P, :], ikw[0:HD, :]).then_inc(ik_dup, 16)
            load(8)
            job_read(sp, "ik")
            sp.dma_start(o["idx_k_prompt"][0, 0].rearrange("(t p) d -> p t d", p=P),
                         iktok[:, 0:TT, 0:HD]).then_inc(out_done, 16)
            sp.dma_start(o["idx_k_sample"][0].rearrange("b j d -> (b j) d"),
                         iktok[0:NS, TT, 0:HD]).then_inc(out_done, 16)
            for n in range(9, 13):
                load(n)
            sp.wait_ge(lines_saved, 16)
            sp.wait_ge(ik_dup, 16)
            for g in range(NB // 2):
                for jj in range(NJ):
                    rows = bias_s[NS * g + jj:NS * (g + 1):NJ, 0:PAST]
                    sp.dma_start(rows, lines_d[:, 0, LMAX - PAST - jj:LMAX - jj]).then_inc(bias_in, 16)
                    rows = bias_n[NS * g + jj:NS * (g + 1):NJ, :]
                    sp.dma_start(rows, lines_d[:, 0, LMAX - jj:LMAX - jj + NJ]).then_inc(bias_in, 16)
            for n in range(13, 16):
                load(n)
            for b in range(2):
                pages(kpg[b], "cache_k", b, kpg_in[b])
            sp.wait_ge(bd_zero, 1)
            for g, w in enumerate(("w_rg_a", "w_rg_x")):
                for h in range(2):
                    sp.dma_start(bd[HD * h:HD * (h + 1), :, g, HD * h:HD * (h + 1)],
                                 a[w][0].rearrange("(c h) k d -> h k c d", h=2)[h]).then_inc(bd_in, 16)
            load(16)
            for t in range(TT + 1):
                load(17 + t)
                rows = P if t < TT else NS
                job_read(sp, ("kout", t))
                dst = (o["k_prompt"][0, 0, P * t:P * (t + 1)].rearrange("s h d -> s (h d)") if t < TT
                       else o["k_sample"][0].rearrange("b j h d -> (b j) (h d)"))
                sp.dma_start(dst, ktok[t % 2][0:rows, :]).then_inc(ktok_out[t % 2], 16)
            for b in range(2, NB):
                job_read(sp, ("kts", b - 2, 1))
                pages(kpg[b % 2], "cache_k", b, kpg_in[b % 2])
                if b in (2, 3, 5):
                    load({2: 22, 3: 23, 5: 24}[b])
            for b in range(2):
                job_read(sp, ("kts", NB - 2 + b, 1))
                pages(kpg[b], "cache_v", b, kpg_in[b])
            for t in range(TT + 1):
                job_read(sp, ("vout", t))
                dst = (o["v_prompt"][0, 0, P * t:P * (t + 1)].rearrange("s h d -> s (h d)") if t < TT
                       else o["v_sample"][0].rearrange("b j h d -> (b j) (h d)"))
                sp.dma_start(dst, vtok[:, t, :] if t < TT else vtok_s[:]).then_inc(out_done, 16)
            load(25)
            load(26)
            for b in range(2, NB):
                load(25 + b)
                sp.wait_ge(spv_b, b - 1)
                pages(kpg[b % 2], "cache_v", b, kpg_in[b % 2])
            for n in range(33, 39):
                load(n)
            n = 39
            job_read(sp, ("gate", DC - 1, 1, 1))
            for h in range(NH):
                if h >= 2:
                    sp.wait_ge(tm_ok, TT * (h - 1))
                src = bass.AP(tensor=lines_d.tensor, offset=LW * P * h + P - 1, ap=[[LW - 1, P], [1, SEQ]])
                sp.dma_start(th[h % 2][:], src).then_inc(th_in[h % 2], 16)
                if h >= 1:
                    load(n)
                    load(n + 1)
                    n += 2
                if h == 1:
                    job_read(sp, "st_a")
                    job_read(sp, "st_b")
                    sp.dma_start(o["conv_prompt"][0, 0], orow[C_CP:C_CS, :]).then_inc(out_done, 16)
                    sp.dma_start(o["conv_sample"][0].rearrange("b i d -> (b i) d"), orow[C_CS:C_HP, :])\
                        .then_inc(out_done, 16)
                    sp.dma_start(o["h_prompt"][0], orow[C_HP:C_HS, :]).then_inc(out_done, 16)
                    sp.dma_start(o["h_sample"][0], orow[C_HS:NC, :]).then_inc(out_done, 16)
            while n < U["gb"] + RING + 1:
                load(n)
                n += 1
            sp.wait_ge(pv_done, STEPS)
            sp.dma_start(ptok[:, 0:TT, :], a["p_prompt"][0, 0].rearrange("(t p) d -> p t d", p=P)).then_inc(p_in, 16)
            sp.dma_start(ptok[0:NS, TT, :], a["p_sample"][0].rearrange("b j d -> (b j) d")).then_inc(p_in, 16)
            while n < U["wo"] + 4:
                load(n)
                n += 1
            sp.wait_ge(m_t, DC)
            sp.dma_start(x[:].rearrange("p c t -> p (c t)"), x_d).then_inc(x_back, 16)
            for half, (f0, fn) in enumerate(FFN_HALVES):
                while n < FIRST[("gate", f0)]:
                    load(n)
                    n += 1
                with sp.Fori(0, fn // 2) as it:
                    for k in range(4):
                        load(n + k, it)
                n += 2 * fn
            while n < len(UNITS):
                load(n)
                n += 1
            for t in range(TT + 1):
                rows = P if t < TT else NS
                sp.wait_ge(y_half[0], t + 1)
                sp.wait_ge(y_half[1], t + 1)
                dst = (o["y_prompt"][0, P * t:P * (t + 1), :] if t < TT
                       else o["y_sample"].rearrange("b j d -> (b j) d"))
                sp.dma_start(dst, ytok[0:rows, t, :]).then_inc(out_done, 16)
            sp.wait_ge(out_done, 16 * (2 + TT + 1 + 4 + TT + 1))
            sp.wait_ge(ktok_out[0], 16 * 3)
            sp.wait_ge(ktok_out[1], 16 * 2)
            sp.wait_ge(x_saved, 16)

        @block.scalar
        def _(act):
            sc = nc.scalar
            steps = [0]

            def link(ins):
                steps[0] += 1
                ins.then_inc(act_step, 1)
                act.wait_ge(act_step, steps[0])

            def round_weights(n, it=0):
                if n >= len(UNITS):
                    return
                _, _, (_, _, rc, _, cc, _, _) = UNITS[n]
                act.wait_ge(w_loaded[n % RING], 16 * (n // RING + 1 + it))
                if n >= RING:
                    act.wait_ge(w_used, n - RING + 1 + 4 * it)
                sc.copy(whi[:, n % RING, 0:rc, 0:cc], wraw[:, n % RING, 0:rc, 0:cc]).then_inc(w_hi, 1)

            def norm_hi(k, c):
                act.wait_ge(n_t, DC * k + c + 1)
                if k and c == 0:
                    act.wait_ge(w_used, h_last[k])
                sc.copy(h_hi[:, c, :], nbuf[c % 4][:]).then_inc(n_hi, 1)

            def root(dst, src, signal):
                sc.activation(dst, src, ACT.Sqrt).then_inc(signal, 1)

            for t in range(TT + 1):
                rows = P if t < TT else NS
                act.wait_ge(x_in[t], 16)
                if t:
                    act.wait_ge(sq_done, t)
                else:
                    act.wait_ge(pool_const, 1)
                sc.activation(junk[0:rows, :], xtok[0:rows, t, :], ACT.Square,
                              accum_out=stat[0:rows, t:t + 1]).then_inc(sq_done, 1)
            got_job(act, "prm")
            read_job(sc.copy(prmT[:], bank("prm")[:, 0:DC * NR].rearrange("p (c r) -> p c r", r=NR)), "prm")
            act.wait_ge(rstd_v, 2)
            root(stat[:, 16:16 + TT + 1], stat[:, 8:8 + TT + 1], rstd_a)
            got_job(act, "xs")
            read_job(sc.copy(x[:, :, SEQ:T], bank("xs")[:, 0:DC * NS].rearrange("p (c s) -> p c s", s=NS)), "xs")

            def x_chunk(c):
                got_job(act, ("x", c))
                read_job(sc.copy(x[:, c, 0:SEQ], bank(("x", c))), ("x", c))

            x_chunk(0)
            round_weights(0)
            round_weights(1)
            x_chunk(2)
            x_chunk(4)
            x_chunk(5)
            norm_hi(0, 0)
            x_chunk(6)
            norm_hi(0, 1)
            x_chunk(7)
            for c in range(2, DC):
                if c in (3, 7):
                    round_weights(2 + c // 7)
                norm_hi(0, c)
            job_read(act, "prm")
            link(sc.activation(lru[:, 0, :], prmT[:, :, R_LAM], ACT.Abs))
            sc.activation(lru[:, 1, :], lru[:, 0, :], ACT.Exp, scale=-1.0).then_inc(lru_a, 1)
            n = 0
            for t in tiles_of("iq"):
                got_tile(act, t)
                act.wait_ge(diag_ok, 2)
                read_tile(sc.copy(two(iqT[:, t, :]), acc(t)), t)
                round_weights(n + RING)
                n += 1
                if n == U["ik"]:
                    for k in range(4):
                        got_job(act, ("iks", k))
                        dst = iks[:, 2 * k:2 * k + 2, :].rearrange("p b s -> p (b s)")
                        read_job(sc.copy(dst, bank(("iks", k))), ("iks", k))
            t = tiles_of("ik")[0]
            got_tile(act, t)
            link(sc.copy(two(ikw[0:HD + NH, :]), acc(t)[0:HD + NH]))
            read_tile(sc.copy(two(ik2[0:HD, :]), acc(t)[0:HD]), t)
            round_weights(n + RING)
            n += 1

            def index_relu(s):
                got_job(act, ("idx", s))
                if s >= 2:
                    act.wait_ge(idx_acc, s - 1)
                w = P * (2 + s // NH)
                read_job(sc.activation(relu[s % 2][:, 0:w], bank(("idx", s))[:, 0:w], ACT.Relu, scale=HD ** -0.5),
                         ("idx", s))

            def key_rows(t):
                rows = P if t < TT else NS
                got_job(act, ("kout", t))
                if t >= 2:
                    act.wait_ge(ktok_out[t % 2], 16 * (t // 2))
                else:
                    job_read(act, ("iks", 3))
                    job_read(act, ("iks", 2))
                read_job(sc.copy(ktok[t % 2][0:rows, :], bank(("kout", t))[0:rows, :]), ("kout", t))

            def value_rows(t):
                rows = P if t < TT else NS
                got_job(act, ("vout", t))
                dst = vtok[:, t, :] if t < TT else vtok_s[:]
                read_job(sc.copy(dst, bank(("vout", t))[0:rows, :]), ("vout", t))

            def past_keys(b):
                for g in range(NPG):
                    got_job(act, ("kts", b, g))
                    if b >= 2 and g == 0:
                        act.wait_ge(slogit_b, b - 1)
                    dst = kts[b % 2][:, :, PG * g:PG * (g + 1)]
                    src = bank(("kts", b, g))[:].rearrange("p (m s) -> p m s", s=PG)
                    read_job(sc.copy(dst, src), ("kts", b, g))

            for kind, dst, scale in (("q", qT, HD ** -0.5), ("k", kT, 1.0), ("v", vT, 1.0)):
                for t in tiles_of(kind):
                    j = TILES[t][1]
                    if kind == "q":
                        for s in range(6 * j, 6 * j + 6):
                            index_relu(s)
                    if kind == "v":
                        if j == 0:
                            act.wait_ge(x_saved, 16)
                            key_rows(0)
                        elif j == 1:
                            key_rows(2)
                        elif j == 2:
                            key_rows(TT)
                            past_keys(0)
                        else:
                            past_keys(2)
                    got_tile(act, t)
                    read_tile(sc.activation(two(dst[:, j, :]), acc(t), ACT.Copy, scale=scale), t)
                    round_weights(n + RING)
                    n += 1
                    if kind == "v" and j <= 1:
                        key_rows(2 * j + 1)
                    elif kind == "v":
                        past_keys(2 * j - 3)
            def sample_exp(g):
                job_read(act, ("smask", g))
                sc.activation(ps_s[:, g, :], ps_s[:, g, :], ACT.Exp, bias=sstat[:, g:g + 1], scale=-1.0,
                              accum_out=sstat[:, 2 + g:3 + g]).then_inc(sexp_ok, 1)

            def sample_turned():
                got_job(act, "spt")
                read_job(sc.copy(pts[:].rearrange("p a g q -> p (a g q)"), bank("spt")), "spt")
                got_job(act, "spn")
                read_job(sc.copy(ptn[:].rearrange("p g q -> p (g q)"), bank("spn")[0:NS, 0:2 * P]), "spn")

            def sample_out_hi():
                got_job(act, "so")
                sc.copy(act_hi[:, 8:FA, SEQ:T], bank("so")[:, 0:HP * NS].rearrange("p (m t) -> p m t", m=HP))\
                    .then_inc(so_hi, 1)

            def conv_line(c, t):
                s = c % 2
                if c >= 2:
                    act.wait_ge(u_ok, c - 1)
                else:
                    act.wait_ge(bd_zero, 2)
                got_tile(act, t)
                ps = acc(t)
                sc.copy(seqs(xe[s][:, S0:EXT])[:, :, 0:CW - 1],
                        prmT[:, c, R_SC:R_SH].rearrange("p (b i) -> p b i", b=NB)).then_inc(xe_ok, 1)
                sc.copy(xe[s][:, CW - 1:CW - 1 + HT], ps[:, 0, :]).then_inc(xe_ok, 1)
                sc.copy(xe[s][:, CW - 1 + HT:S0], ps[:, 1, 0:SEQ - HT]).then_inc(xe_ok, 1)
                read_tile(sc.copy(seqs(xe[s][:, S0:EXT])[:, :, CW - 1:ST],
                                  ps[:, 1, SEQ - HT:HT].rearrange("p (b j) -> p b j", j=NJ)), t)
                act.wait_ge(xe_ok, 3 * (c + 1))
                tile_is_read(act, "xr", c)
                sc.activation(xc[s][:], xe[s][:, 0:EO], ACT.Identity, scale=prmT[:, c, R_CW:R_CW + 1],
                              bias=prmT[:, c, R_CB:R_CB + 1]).then_inc(tap0, 1)

            def gates(c):
                if c >= 1:
                    act.wait_ge(hs_ok, c)
                else:
                    act.wait_ge(lru_v, 1)
                    job_read(act, ("vout", TT))
                for g, dst in ((0, rq), (1, ig)):
                    for k in range(2):
                        job = ("gate", c, g, k)
                        got_job(act, job)
                        read_job(sc.activation(dst[:, EH * k:EH * (k + 1)], bank(job)[:, 0:EH], ACT.Tanh, scale=0.5,
                                               bias=lru[:, 4 + g, c:c + 1]), job)
                    if g == 0:
                        job_read(act, ("gate", c, 0, 0))
                        job_read(act, ("gate", c, 0, 1))
                        sc.activation(rq[:], rq[:], ACT.Tanh, scale=lru[:, 3, c:c + 1],
                                      bias=lru[:, 3, c:c + 1]).then_inc(q_lru, 1)

            def gelu_path(c, t):
                got_tile(act, t)
                if c >= 2:
                    act.wait_ge(yt_ok, c - 1)
                elif c == 0:
                    job_read(act, ("smask", 1))
                read_tile(sc.activation(two(gel[c % 2][:]), acc(t), ACT.Gelu_apprx_tanh), t)

            def lru_root(c):
                act.wait_ge(q_lru, c + 1)
                if c >= 1:
                    act.wait_ge(hs_ok, c)
                root(sq[:], rq[:], sqrt_ok)

            def y_upper(c):
                act.wait_ge(yt_ok, c + 1)
                sc.copy(act_hi[:, c, :], hmul[c % 2][:]).then_inc(y_hi, 1)

            past_keys(4)
            conv_line(0, NTH[("xr", 0, False)])
            round_weights(n + RING)
            n += 1
            past_keys(5)
            past_keys(6)
            for tt in range(TT + 1):
                value_rows(tt)
            past_keys(7)

            sample_exp(0)
            sample_exp(1)
            for c in range(DC):
                gates(c)
                if c == 0:
                    sample_turned()
                if c == SO_CHUNK:
                    sample_out_hi()
                lru_root(c)
                if c + 1 < DC:
                    conv_line(c + 1, NTH[("xr", c + 1, False)])
                    round_weights(n + RING)
                    n += 1
                if c >= 1:
                    y_upper(c - 1)
                gelu_path(c, NTH[("gr", c, False)])
                round_weights(n + RING)
                n += 1
            y_upper(DC - 1)

            def attend_exp(s):
                w = P * (s % TT + 1)
                job_read(act, ("qk", s))
                sc.activation(pr[s % 3][:, 0:w], pr[s % 3][:, 0:w], ACT.Exp, bias=stat[:, 24 + s % 2:25 + s % 2],
                              scale=-1.0, accum_out=stat[:, 26 + s % 2:27 + s % 2]).then_inc(exp_ok, 1)

            def attend_turned(s):
                w = P * (s % TT + 1)
                act.wait_ge(tr_done, s + 1)
                if s >= 2:
                    act.wait_ge(pv_done, s - 1)
                elif s == 0:
                    act.wait_ge(y_lo, DC)
                sc.copy(pT[s % 2][:, 0:s % TT + 1, :].rearrange("p k t -> p (k t)"), psX[2][:, 0:w])\
                    .then_inc(pT_ok, 1)

            def attend_out_hi(m):
                act.wait_ge(pv_done, 2 * TT * (m + 1))
                sc.copy(act_hi[:, 8 + m, 0:SEQ], psX[3][:]).then_inc(o_hi, 1)

            def attend(s):
                if 2 <= s < STEPS + 2:
                    attend_turned(s - 2)
                if s < STEPS:
                    attend_exp(s)
                if s >= 10 and (s - 10) % 8 == 0:
                    attend_out_hi((s - 10) // 8)

            def gate_tanh(k, t):
                got_tile(act, t)
                if k >= 2:
                    tile_is_read(act, *(("rnn", k - 2) if k < DC + 2 else ("att", k - 2 - DC)))
                elif k == 0:
                    act.wait_ge(hs_ok, DC)
                    act.wait_ge(yt_ok, DC)
                read_tile(sc.activation(two(sg[k % 2][:]), acc(t), ACT.Tanh, scale=0.5), t)

            def state_rows():
                for k, job in enumerate(("st_a", "st_b")):
                    got_job(act, job)
                    read_job(sc.copy(orow[:, SEQ * k:SEQ * (k + 1)], bank(job)[0:NC, :]), job)

            for i in range(2 * DC):
                attend(2 * i)
                if i % 2 == 0:
                    gate_tanh(i // 2, FIRST_TILE["ga"] + i)
                round_weights(n + RING)
                n += 1
                attend(2 * i + 1)
                if i == 1:
                    state_rows()
            attend(STEPS)

            def upper(dst, k, hi_ok, scale=1.0):
                sc.activation(dst, hmul[k % 2][:], ACT.Copy, scale=scale).then_inc(hi_ok, 1)

            for j in range(DC):
                gate_tanh(DC + j, FIRST_TILE["gb"] + 2 * j)
                round_weights(n + RING)
                if j == 0:
                    attend(STEPS + 1)
                    attend(STEPS + 2)
                round_weights(n + 1 + RING)
                if j >= 1:
                    act.wait_ge(m_t, j)
                    upper(act_hi[:, j - 1, :], j - 1, m_hi, 0.5)
                if j >= 1 and j - 1 <= TT:
                    t = j - 1
                    c0, c1 = (P * t, P * (t + 1)) if t < TT else (SEQ, T)
                    got_job(act, ("p", t))
                    sc.copy(p_hi[:, :, c0:c1], bank(("p", t))[:, 0:2 * (c1 - c0)].rearrange("p (k t) -> p k t", k=2))\
                        .then_inc(p_hi_ok, 1)
                n += 2
            act.wait_ge(m_t, DC)
            upper(act_hi[:, DC - 1, :], DC - 1, m_hi, 0.5)

            def square(k, c):
                x_is_new(act, k, c)
                i = DC * k + c
                if i >= 2:
                    act.wait_ge(sqacc_ok, i - 1)
                sc.activation(sqt[i % 2][:], x[:, c, :], ACT.Square).then_inc(sq_ok, 1)

            for j in range(DC):
                round_weights(n + RING)
                n += 1
                square(0, j)
            def row_root(k):
                act.wait_ge(fs_v, k)
                root(stat[:, 48:48 + TT + 1], stat[:, 40:40 + TT + 1], fs_a)

            def projection(j0, k):
                nonlocal n
                for i in range(DC // 2):
                    t = NTH[("pp", j0 + i, False)]
                    got_tile(act, t)
                    read_tile(sc.copy(two(pp[:, j0 + i, :]), acc(t)), t)
                    if i == 1:
                        row_root(k)
                    round_weights(n + RING)
                    n += 1

            projection(0, 1)
            for j in range(DC):
                norm_hi(1, j)
            def gate_pair(k, it, f, n, following):
                act.wait_ge(w_used, n + 1 + 4 * it)
                if k >= 2:
                    tile_is_read(act, "up", k - 2, it=it)
                t = NTH[("gate", k, False)]
                read_tile(sc.activation(two(sg[k % 2][:]), acc(t), ACT.Silu), t)
                for m, more in following:
                    round_weights(m, more)
                if not (isinstance(f, int) and f == 0):
                    tile_is_read(act, "up", k - 1, it=it)
                    upper(chunk(act_hi, f - 1), k - 1, f_hi)

            for half, (f0, fn) in enumerate(FFN_HALVES):
                def gates_of_two(it):
                    static = isinstance(it, int)
                    for u in range(2):
                        if static:
                            f = 2 * it + u
                            m = n + 2 * f
                            gate_pair(f0 + f, 0, f, m, [(m + RING, 0), (m + 1 + RING, 0)])
                        else:
                            f, m = 2 + u, n + 2 * (2 + u)
                            gate_pair(f0 + f, it - 1, 2 * it + u, m, [(m + RING, it - 1), (m + 1 + RING, it - 1)])

                ffn_iterations(act, fn, gates_of_two)
                n += 2 * fn
                k = f0 + fn
                tile_is_read(act, "up", k - 1)
                upper(act_hi[:, fn - 1, :], k - 1, f_hi)
                for j in range(DC):
                    round_weights(n + RING)
                    round_weights(n + 1 + RING)
                    n += 2
                    if half:
                        square(1, j)
            projection(DC // 2, 2)
            for j in range(DC):
                norm_hi(2, j)
            for j in range(DC):
                t = FIRST_TILE["pg"] + j
                got_tile(act, t)
                if j >= 2:
                    act.wait_ge(xn_ok, j - 1)
                read_tile(sc.activation(two(sg[j % 2][:]), acc(t), ACT.Tanh, scale=0.5), t)
                round_weights(n + RING)
                n += 1
                if j >= 1:
                    square(2, j - 1)
                    sc.activation(pp[:, j - 1, :], x[:, j - 1, :], ACT.Copy,
                                  scale=prmT[:, j - 1, R_FIN:R_FIN + 1]).then_inc(xf_ok, 1)
            square(2, DC - 1)
            sc.activation(pp[:, DC - 1, :], x[:, DC - 1, :], ACT.Copy,
                          scale=prmT[:, DC - 1, R_FIN:R_FIN + 1]).then_inc(xf_ok, 1)
            row_root(3)
            act.wait_ge(fs_a, 3)
            for t in range(TT + 1):
                rows = P if t < TT else NS
                i = y_order.index((t, 0))
                act.wait_ge(y_turned, i + 1)
                sc.activation(ytok[0:rows, t, 0:512], y_bank[i][0:rows, :], ACT.Copy,
                              scale=stat[0:rows, 48 + t:49 + t]).then_inc(y_half[0], 1)

        @block.vector
        def _(dve):
            v = nc.vector
            steps = [0]

            def link(ins):
                steps[0] += 1
                ins.then_inc(dve_step, 1)
                dve.wait_ge(dve_step, steps[0])

            def inverse_mean(ap, src):
                link(v.tensor_scalar(ap, src, 1.0 / D, EPS, ALU.mult, ALU.add))
                return v.reciprocal(ap, ap)

            def norm_scale(k, c, gain, factor):
                if c >= 4:
                    dve.wait_ge(n_hi, DC * k + c - 3)
                    norm_is_split(dve, k, c - 4)
                v.scalar_tensor_tensor(two(nbuf[c % 4][:]), two(x[:, c, :]), prmT[:, c, gain:gain + 1], factor,
                                       ALU.mult, ALU.mult).then_inc(n_t, 1)

            def norm_lo(k, c):
                dve.wait_ge(n_hi, DC * k + c + 1)
                v.tensor_tensor(h_lo[:, c, :], nbuf[c % 4][:], h_hi[:, c, :].bitcast(F32), ALU.subtract)\
                    .then_inc(n_lo_v, 1)

            def norm(k, gain, factor):
                for c in range(DC):
                    if k == 0:
                        job_read(dve, ("x", c))
                    norm_scale(k, c, gain, factor)
                    if c % 2:
                        norm_lo(k, c - 1)
                    if c == 1:
                        norm_lo(k, c)

            v.memset(ones[:], 1.0).then_inc(ones_ok, 1)
            dve.wait_ge(ident_ok, 2)
            dve.wait_ge(sq_done, TT + 1)
            inverse_mean(stat[:, 8:8 + TT + 1], stat[:, 0:TT + 1]).then_inc(rstd_v, 2)
            dve.wait_ge(rstd_a, 1)
            for t in range(TT):
                ins = v.tensor_scalar(diag[:, t, :], ident[:], stat[:, 16 + t:17 + t], None, ALU.mult)
            ins.then_inc(diag_ok, 1)
            v.tensor_scalar(diag[0:NS, TT, 0:NS], ident[0:NS, 0:NS], stat[0:NS, 16 + TT:17 + TT], None, ALU.mult)\
                .then_inc(diag_ok, 1)
            got_job(dve, ("x", 1))
            read_job(v.tensor_copy(x[:, 1, 0:SEQ], bank(("x", 1))), ("x", 1))
            got_job(dve, "rstd_a")
            read_job(v.tensor_copy(rb0[:, 0:SEQ], bank("rstd_a")), "rstd_a")
            got_job(dve, "rstd_b")
            read_job(v.tensor_copy(rb0[:, SEQ:T], bank("rstd_b")[:, 0:NS]), "rstd_b")
            got_job(dve, ("x", 3))
            read_job(v.tensor_copy(x[:, 3, 0:SEQ], bank(("x", 3))), ("x", 3))
            job_read(dve, "rstd_a")
            job_read(dve, "rstd_b")
            job_read(dve, "prm")
            job_read(dve, "xs")
            norm(0, R_MIX, two(rb0[:]))

            for k, job in enumerate(("lines_a", "lines_b")):
                got_job(dve, job)
                w = LW // 2
                read_job(v.tensor_copy(lines[:, w * k:w * (k + 1)], bank(job)[0:NH, 0:w]), job)
            got_job(dve, "selT")
            read_job(v.tensor_copy(selT[:].rearrange("p g c -> p (g c)"), bank("selT")[:, 0:2 * NS]), "selT")

            dve.wait_ge(lru_a, 1)
            e, z, z2, s, sp_ = (lru[:, i, :] for i in (1, 2, 6, 7, 3))
            link(v.tensor_scalar(z, e, 2.0, None, ALU.add))
            link(v.reciprocal(z, z))
            link(v.tensor_tensor(z, z, e, ALU.mult))
            link(v.tensor_tensor(z2, z, z, ALU.mult))
            link(v.tensor_scalar(s, z2, 1.0 / 17, None, ALU.mult))
            for k in range(15, 1, -2):
                link(v.scalar_tensor_tensor(s, s, 1.0 / k, z2, ALU.add, ALU.mult))
            link(v.scalar_tensor_tensor(s, s, 1.0, z, ALU.add, ALU.mult))
            link(v.tensor_scalar(z, prmT[:, :, R_LAM], -1.0, 0.0, ALU.mult, ALU.max))
            link(v.scalar_tensor_tensor(s, s, 2.0, z, ALU.mult, ALU.add))
            v.tensor_scalar(sp_, s, 2.0, None, ALU.mult)
            v.tensor_scalar(lru[:, 4, :], prmT[:, :, R_BA], 0.5, None, ALU.mult)
            v.tensor_scalar(lru[:, 5, :], prmT[:, :, R_BX], 0.5, None, ALU.mult).then_inc(lru_v, 1)

            def conv_taps(c):
                s = c % 2
                dve.wait_ge(tap0, c + 1)
                for j in range(1, CW):
                    ins = v.scalar_tensor_tensor(xc[s][:], xe[s][:, j:j + EO], prmT[:, c, R_CW + j:R_CW + j + 1],
                                                 xc[s][:], ALU.mult, ALU.add)
                    if j < CW - 1:
                        link(ins)
                    else:
                        ins.then_inc(xc_ok, 1)

            got_job(dve, "ik")
            kw = HD + NH
            src = bank("ik")[:, 0:(TT + 1) * kw].rearrange("p (t c) -> p t c", c=kw)
            link(v.tensor_copy(iktok[:, 0:TT, :], src[:, 0:TT, :]))
            read_job(v.tensor_copy(iktok[0:NS, TT, :], src[0:NS, TT, :]), "ik")
            job_read(dve, "ik")
            link(v.tensor_scalar(iwtok[:, 0:TT, :], iktok[:, 0:TT, HD:kw], NH ** -0.5, None, ALU.mult))
            v.tensor_scalar(iwtok[0:NS, TT, :], iktok[0:NS, TT, HD:kw], NH ** -0.5, None, ALU.mult)\
                .then_inc(iwcol_ok, 1)
            dve.wait_ge(iwcol_ok, 1)

            def to_mask(work):
                return v.tensor_scalar(work, work, TAKEN_BELOW, OFF, ALU.is_gt, ALU.mult)

            def top_round(work, keys, k, rows, r):
                link(v.max(top8[0:rows, :], work[:, 0:keys]))
                left = k - 8 * r
                if left < 8:
                    link(v.memset(top8[0:rows, left:8], PAD))
                link(v.match_replace(work[:], top8[0:rows, :], work[:], TAKEN))

            def top_rounds(i, first, last):
                if first == 0:
                    dve.wait_ge(masked_in, i)
                for r in range(first, last):
                    top_round(score[i], P * (i + 1), TOPK_P, P, r)
                if last == TOPK_P // 8:
                    to_mask(score[i][:]).then_inc(topk_ok, 1)

            done = 0
            for st in range(NH * (TT - 1)):
                i, h = 1 + st // NH, st % NH
                w = P * (i + 1)
                job_read(dve, ("idx", st))
                r, wt = relu[st % 2][:, 0:w], iwtok[:, i, h:h + 1]
                if h == 0:
                    ins = v.tensor_scalar(score[i][:], r, wt, None, ALU.mult)
                else:
                    dve.wait_ge(idx_acc, st)
                    ins = v.scalar_tensor_tensor(score[i][:], r, wt, score[i][:], ALU.mult, ALU.add)
                ins.then_inc(idx_acc, 1)
                if st >= 12:
                    more = 5 if st == 17 else 1
                    top_rounds(1, done, done + more)
                    done += more
            assert done == TOPK_P // 8

            got_job(dve, "iwcol")
            dve.wait_ge(pool_const, 2)
            link(v.tensor_reduce(stat[:, 32:32 + NH], hm[:].rearrange("p b h -> p h b"), mybir.AxisListType.X,
                                 ALU.add))
            for g in range(2):
                src = bank("iwcol")[:, NH * g:NH * (g + 1)].unsqueeze(1).broadcast_to([P, NB // 2, NH])
                ins = v.tensor_tensor(iwsc[:], hm[:], src, ALU.mult)
                if g:
                    read_job(ins, "iwcol")
                    job_read(dve, "iwcol")
                else:
                    link(ins)
                link(v.tensor_reduce(stat[:, 60 + g:61 + g], iwsc[:].rearrange("p b h -> p (b h)"),
                                     mybir.AxisListType.X, ALU.add))
            link(v.tensor_scalar(stat[:, 60:62], stat[:, 60:62], HD ** -0.5, None, ALU.mult))
            top_rounds(2, 0, 4)
            dve.wait_ge(sdots, 1)
            for g in range(2):
                v.tensor_scalar(rs_s[:, g, :], psX[2 + g][:, 0:SK], 0.0, stat[:, 60 + g:61 + g], ALU.max, ALU.mult)\
                    .then_inc(rs_ok, 1)
            v.memset(score_s[:, SK:SK + 8], PAD).then_inc(ss_copied, 1)
            got_job(dve, "sidx")
            read_job(v.tensor_copy(score_s[:, 0:SK], bank("sidx")[0:NS, 0:SK]), "sidx")

            dve.wait_ge(masked_in, TT)
            for r in range(-(-TOPK_S // 8)):
                top_round(score_s, SK, TOPK_S, NS, r)
            to_mask(score_s[:, 0:SK]).then_inc(topk_s_ok, 1)
            top_rounds(2, 4, TOPK_P // 8)
            top_rounds(3, 0, TOPK_P // 8)

            conv_taps(0)
            dve.wait_ge(slogit_b, NB)
            dve.wait_ge(bias_in, 16 * 2 * NB // 2 * NJ)
            new = bias_n[:].unsqueeze(1).broadcast_to([P, NB, NJ])
            link(v.tensor_copy(bias_s[:, PAST:SK].rearrange("p (b j) -> p b j", j=NJ), new))
            for g in range(2):
                ins = v.tensor_tensor(ps_s[:, g, :], psX[2 + g][:, 0:SK], bias_s[:], ALU.add)
                link(ins)
            for g in range(2):
                job = ("smask", g)
                got_job(dve, job)
                read_job(v.tensor_tensor_reduce(ps_s[:, g, :], ps_s[:, g, :], bank(job)[:, 0:SK], -1.0, 3.0e38,
                                                ALU.add, ALU.min, sstat[:, g:g + 1]), job)

            def sample_normal():
                v.tensor_copy(selT2[:], selT[:])
                for g in range(2):
                    dve.wait_ge(sexp_ok, g + 1)
                    link(v.reciprocal(sstat[:, 4 + g:5 + g], sstat[:, 2 + g:3 + g]))
                    v.tensor_scalar(ps_s[:, g, :], ps_s[:, g, :], sstat[:, 4 + g:5 + g], None, ALU.mult)\
                        .then_inc(sp_ok, 1)

            def sample_own():
                dve.wait_ge(spv_b, NB)
                head = stat[:, 32:32 + NH].unsqueeze(2).broadcast_to([P, NH, HD])
                for g in range(2):
                    v.tensor_tensor(own[g][:].rearrange("p (h d) -> p h d", h=NH),
                                    psX[2 + g].rearrange("p (h d) -> p h d", h=NH), head, ALU.mult).then_inc(own_ok, 1)

            def sample_out_lo():
                dve.wait_ge(so_hi, 1)
                read_job(v.tensor_tensor(act_lo[:, 8:FA, SEQ:T],
                                         bank("so")[:, 0:HP * NS].rearrange("p (m t) -> p m t", m=HP),
                                         act_hi[:, 8:FA, SEQ:T].bitcast(F32), ALU.subtract), "so")

            def recurrence(c):
                s = c % 2
                dve.wait_ge(q_lru, c + 1)
                if c:
                    dve.wait_ge(yt_ok, c)
                link(v.tensor_scalar(hs[:], rq[:], 1.0, None, ALU.add))
                link(v.reciprocal(hs[:], hs[:]))
                v.tensor_copy(stO[:, c, C_CP:C_CS], xe[s][:, SEQ:S0])
                v.tensor_copy(stO[:, c, C_CS:C_HP].rearrange("p (b i) -> p b i", b=NB),
                              seqs(xe[s][:, S0:EXT])[:, :, NJ:ST])
                dve.wait_ge(sqrt_ok, c + 1)
                link(v.tensor_tensor(sq[:], sq[:], hs[:], ALU.mult))
                v.tensor_scalar(rq[:], hs[:], 2.0, -1.0, ALU.mult, ALU.add)
                job_read(dve, ("gate", c, 1, 0))
                job_read(dve, ("gate", c, 1, 1))
                link(v.scalar_tensor_tensor(ig[:], ig[:], 1.0, xc[s][:], ALU.add, ALU.mult))
                link(v.tensor_tensor(ig[:], ig[:], sq[:], ALU.mult))
                link(v.memset(seqs(rq[:, SEQ:EO])[:, :, 0:CW - 1], 0.0))
                link(v.memset(seqs(ig[:, SEQ:EO])[:, :, 0:CW - 2], 0.0))
                ins = v.tensor_copy(seqs(ig[:, SEQ:EO])[:, :, CW - 2:CW - 1],
                                    prmT[:, c, R_SH:NR].rearrange("p (b i) -> p b i", i=1))
                ins.then_inc(u_ok, 1)
                dve.wait_ge(u_ok, c + 1)
                v.tensor_tensor_scan(hs[:], rq[:], ig[:], 0.0, ALU.mult, ALU.add).then_inc(hs_ok, 1)
                dve.wait_ge(hs_ok, c + 1)
                v.tensor_copy(stO[:, c, C_HP:C_HS], hs[:, SEQ - 1:SEQ])
                v.tensor_copy(stO[:, c, C_HS:NC].rearrange("p (b i) -> p b i", i=1), seqs(hs[:, SEQ:EO])[:, :, ST - 1:ST])

            def branch(c):
                s = c % 2
                tile_is_read(dve, "gr", c)
                if c >= 2:
                    dve.wait_ge(y_hi, c - 1)
                    dve.wait_ge(y_lo, c - 1)
                link(v.tensor_tensor(hmul[s][:, 0:SEQ], hs[:, 0:SEQ], gel[s][:, 0:SEQ], ALU.mult))
                v.tensor_tensor(hmul[s][:, SEQ:T].rearrange("p (b j) -> p b j", j=NJ),
                                seqs(hs[:, SEQ:EO])[:, :, CW - 1:ST],
                                gel[s][:, SEQ:T].rearrange("p (b j) -> p b j", j=NJ), ALU.mult).then_inc(yt_ok, 1)

            sample_normal()
            for c in range(DC):
                recurrence(c)
                if c == SO_CHUNK:
                    sample_out_lo()
                if c + 1 < DC:
                    conv_taps(c + 1)
                branch(c)
                if c == SO_CHUNK - 1:
                    sample_own()
            dve.wait_ge(y_lo, DC - 1)
            dve.wait_ge(y_hi, DC)
            v.tensor_tensor(act_lo[:, DC - 1, :], hmul[1][:], act_hi[:, DC - 1, :].bitcast(F32), ALU.subtract)\
                .then_inc(y_lo, 1)

            def logits(st):
                i = st % TT
                w = P * (i + 1)
                got_job(dve, ("qk", st))
                dve.wait_ge(tm_ok, st + 1)
                if st >= 3:
                    dve.wait_ge(tr_done, st - 2)
                read_job(v.tensor_tensor_reduce(pr[st % 3][:, 0:w], bank(("qk", st))[:, 0:w], tm[st % 2][:, 0:w],
                                                -1.0, 3.0e38, ALU.add, ALU.min, stat[:, 24 + st % 2:25 + st % 2]),
                         ("qk", st))

            def normal(st):
                w = P * (st % TT + 1)
                dve.wait_ge(exp_ok, st + 1)
                link(v.reciprocal(stat[:, 28 + st % 2:29 + st % 2], stat[:, 26 + st % 2:27 + st % 2]))
                v.tensor_scalar(pr[st % 3][:, 0:w], pr[st % 3][:, 0:w], stat[:, 28 + st % 2:29 + st % 2], None,
                                ALU.mult).then_inc(p_ok, 1)

            def attend_out_lo(m):
                dve.wait_ge(o_hi, m + 1)
                v.tensor_tensor(act_lo[:, 8 + m, 0:SEQ], psX[3][:], act_hi[:, 8 + m, 0:SEQ].bitcast(F32),
                                ALU.subtract).then_inc(o_lo, 1)

            def attend(st):
                if st < STEPS:
                    logits(st)
                if 1 <= st <= STEPS:
                    normal(st - 1)
                if st >= 10 and (st - 10) % 8 == 0:
                    attend_out_lo((st - 10) // 8)

            for i in range(2 * DC):
                attend(2 * i)
                if i % 2:
                    j = i // 2
                    t = FIRST_TILE["rnn"] + 2 * j
                    got_tile(dve, t)
                    tile_is_read(dve, "ga", j)
                    if j == 0:
                        dve.wait_ge(x_saved, 16)
                    if j == OROW_CHUNK:
                        dve.wait_ge(out_done, 16 * (2 + TT + 1 + 4))
                    read_tile(v.scalar_tensor_tensor(two(x[:, j, :]), two(sg[j % 2][:]), 1.0, acc(t),
                                                     ALU.add, ALU.mult), t)
                attend(2 * i + 1)
            for st in range(STEPS, STEPS + 3):
                attend(st)

            def lower(dst, k, hi, hi_ok, lo_ok):
                dve.wait_ge(hi_ok, k + 1)
                v.tensor_tensor(dst, hmul[k % 2][:], hi.bitcast(F32), ALU.subtract).then_inc(lo_ok, 1)

            def merged_lower(k):
                dve.wait_ge(m_hi, k + 1)
                v.scalar_tensor_tensor(act_lo[:, k, :], hmul[k % 2][:], 0.5, act_hi[:, k, :].bitcast(F32),
                                       ALU.mult, ALU.subtract).then_inc(m_lo, 1)

            for j in range(DC):
                t = FIRST_TILE["att"] + 2 * j
                got_tile(dve, t)
                tile_is_read(dve, "gb", j)
                if j == 0:
                    dve.wait_ge(pv_done, STEPS)
                if j >= 2:
                    dve.wait_ge(m_hi, j - 1)
                    dve.wait_ge(m_lo, j - 1)
                read_tile(v.scalar_tensor_tensor(two(hmul[j % 2][:]), two(sg[j % 2][:]), 1.0, acc(t),
                                                 ALU.add, ALU.mult), t)
                tile_is_read(dve, "att", j)
                tile_is_read(dve, "rnn", j)
                v.tensor_tensor(hmul[j % 2][:], hmul[j % 2][:], x[:, j, :], ALU.add).then_inc(m_t, 1)
                if j >= 1:
                    merged_lower(j - 1)
                if j >= 1 and j - 1 <= TT:
                    tt = j - 1
                    c0, c1 = (P * tt, P * (tt + 1)) if tt < TT else (SEQ, T)
                    dve.wait_ge(p_hi_ok, tt + 1)
                    read_job(v.tensor_tensor(p_lo[:, :, c0:c1],
                                             bank(("p", tt))[:, 0:2 * (c1 - c0)].rearrange("p (k t) -> p k t", k=2),
                                             p_hi[:, :, c0:c1].bitcast(F32), ALU.subtract), ("p", tt))
            merged_lower(DC - 1)

            def add_square(k, c):
                i = DC * k + c
                dve.wait_ge(sq_ok, i + 1)
                if c == 0:
                    ins = v.tensor_copy(sqacc[:], sqt[i % 2][:])
                else:
                    dve.wait_ge(sqacc_ok, i)
                    ins = v.tensor_tensor(sqacc[:], sqacc[:], sqt[i % 2][:], ALU.add)
                ins.then_inc(sqacc_ok, 1)

            def row_factor(k):
                job = ("ss", k)
                got_job(dve, job)
                factors = stat[:, 40:40 + TT + 1]
                v.tensor_scalar(factors[:, 0:TT], bank(job)[:, 0:TT], 1.0 / D, EPS, ALU.mult, ALU.add)
                read_job(v.tensor_scalar(factors[0:NS, TT:TT + 1], bank(job)[0:NS, TT:TT + 1], 1.0 / D, EPS,
                                         ALU.mult, ALU.add), job)
                job_read(dve, job)
                v.reciprocal(factors, factors).then_inc(fs_v, 1)
                dve.wait_ge(fs_a, k)

            def norm_by_rows(k, gain):
                row_factor(k)
                v.tensor_tensor(spread[:], ident[:].unsqueeze(1).broadcast_to([P, TT + 1, P]),
                                stat[:, 48:48 + TT + 1].unsqueeze(2).broadcast_to([P, TT + 1, P]), ALU.mult)\
                    .then_inc(spread_ok, 1)
                dve.wait_ge(rb_ok, k)
                norm(k, gain, held[:, :, 0:HT])

            dve.wait_ge(x_back, 16)
            for j in range(DC):
                t = FIRST_TILE["wo"] + j
                got_tile(dve, t)
                read_tile(v.tensor_tensor(two(x[:, j, :]), two(x[:, j, :]), acc(t), ALU.add), t)
                if j >= 1:
                    add_square(0, j - 1)
            add_square(0, DC - 1)
            norm_by_rows(1, R_FFN)

            def gated(k, it, f):
                t = NTH[("up", k, False)]
                tile_is_read(dve, "gate", k, it=it)
                got_tile(dve, t, it)
                if k >= 2:
                    dve.wait_ge(f_hi, k - 1 + 2 * it)
                    dve.wait_ge(f_lo, k - 1 + 2 * it)
                elif k == 1:
                    norm_is_split(dve, 1, 5)
                read_tile(v.tensor_tensor(two(hmul[k % 2][:]), two(sg[k % 2][:]), acc(t), ALU.mult), t)
                if not (isinstance(f, int) and f == 0):
                    dve.wait_ge(f_hi, k + 2 * it)
                    v.tensor_tensor(chunk(act_lo, f - 1), hmul[(k - 1) % 2][:], chunk(act_hi, f - 1).bitcast(F32),
                                    ALU.subtract).then_inc(f_lo, 1)

            for half, (f0, fn) in enumerate(FFN_HALVES):
                def two_products(it):
                    for u in range(2):
                        if isinstance(it, int):
                            gated(f0 + 2 * it + u, 0, 2 * it + u)
                        else:
                            gated(f0 + 2 + u, it - 1, 2 * it + u)

                ffn_iterations(dve, fn, two_products)
                t0 = FIRST_TILE["gate"] + half * (2 * FA + DC)
                k = f0 + fn
                lower(act_lo[:, fn - 1, :], k - 1, act_hi[:, fn - 1, :], f_hi, f_lo)
                for j in range(DC):
                    t = t0 + 2 * fn + j
                    got_tile(dve, t)
                    read_tile(v.tensor_tensor(two(x[:, j, :]), two(x[:, j, :]), acc(t), ALU.add), t)
                    if half and j >= 1:
                        add_square(1, j - 1)
            add_square(1, DC - 1)
            norm_by_rows(2, R_PLE)
            for j in range(DC):
                t = FIRST_TILE["pg"] + j
                got_tile(dve, t)
                tile_is_read(dve, "pg", j)
                tile_is_read(dve, "pp", j)
                if j == 1:
                    norm_is_split(dve, 2, 5)
                elif j >= 2:
                    dve.wait_ge(xn_ok, j - 1)
                link(v.scalar_tensor_tensor(hmul[j % 2][:], sg[j % 2][:], 1.0, pp[:, j, :], ALU.add, ALU.mult))
                v.scalar_tensor_tensor(x[:, j, :], hmul[j % 2][:], 0.5, x[:, j, :], ALU.mult, ALU.add)\
                    .then_inc(xn_ok, 1)
                if j >= 1:
                    add_square(2, j - 1)
            add_square(2, DC - 1)
            row_factor(3)
            for t in range(TT + 1):
                rows = P if t < TT else NS
                i = y_order.index((t, 1))
                dve.wait_ge(y_turned, i + 1)
                v.tensor_scalar(ytok[0:rows, t, 512:D], y_bank[i][0:rows, :], stat[0:rows, 48 + t:49 + t],
                                None, ALU.mult).then_inc(y_half[1], 1)

        @block.gpsimd
        def _(pool):
            g_ = nc.gpsimd
            steps = [0]

            def link(ins):
                steps[0] += 1
                ins.then_inc(pool_step, 1)
                pool.wait_ge(pool_step, steps[0])

            def lower_weights(n, it=0):
                if n >= len(UNITS):
                    return
                _, _, (_, _, rc, _, cc, _, _) = UNITS[n]
                s = n % RING
                pool.wait_ge(w_hi, n + 1 + 4 * it)
                g_.tensor_tensor(wlo[:, s, 0:rc, 0:cc], wraw[:, s, 0:rc, 0:cc], whi[:, s, 0:rc, 0:cc].bitcast(F32),
                                 ALU.subtract).then_inc(w_lo, 1)

            def norm_lo(k, c):
                pool.wait_ge(n_hi, DC * k + c + 1)
                g_.tensor_tensor(h_lo[:, c, :], nbuf[c % 4][:], h_hi[:, c, :].bitcast(F32), ALU.subtract)\
                    .then_inc(n_lo_p, 1)

            def y_lower(c):
                pool.wait_ge(y_hi, c + 1)
                if c == 0:
                    pool.wait_ge(ktok_out[0], 16 * 3)
                    pool.wait_ge(ktok_out[1], 16 * 2)
                if c == 5:
                    pool.wait_ge(spv_b, NB)
                g_.tensor_tensor(act_lo[:, c, :], hmul[c % 2][:], act_hi[:, c, :].bitcast(F32), ALU.subtract)\
                    .then_inc(y_lo, 1)

            def causal(ap, fill):
                return g_.affine_select(out=ap, in_=ap, compare_op=ALU.is_ge, fill=fill, base=0,
                                        pattern=[[-1, P]], channel_multiplier=1)

            def own_new_keys(ap, fill):
                v = ap.rearrange("p (b j) -> p b j", j=NJ)
                link(g_.affine_select(out=v, in_=v, compare_op=ALU.is_ge, fill=fill, base=0,
                                      pattern=[[-NJ, NB], [-1, NJ]], channel_multiplier=1))
                return g_.affine_select(out=v, in_=v, compare_op=ALU.is_ge, fill=fill, base=NJ - 1,
                                        pattern=[[NJ, NB], [0, NJ]], channel_multiplier=-1)

            link(g_.memset(ident[:], 0.0))
            g_.affine_select(out=ident[:], in_=ident[:], compare_op=ALU.not_equal, fill=1.0, base=0,
                             pattern=[[-1, P]], channel_multiplier=1).then_inc(ident_ok, 1)
            g_.memset(stat[:], 1.0).then_inc(pool_const, 1)
            g_.memset(iwtok[:], 0.0).then_inc(ident_ok, 1)
            link(g_.memset(mask0[:], 0.0))
            link(causal(mask0[:], OFF))
            lower_weights(0)
            lower_weights(1)
            for i, c in enumerate(pool_lowers):
                norm_lo(0, c)
                if i != 1:
                    lower_weights(2 + i // 2)
            job_read(pool, ("x", DC - 2))
            job_read(pool, ("x", DC - 1))
            link(g_.memset(sel[:], 0.0))
            v = sel[:].rearrange("p g (b h j) -> p (g b) h j", b=NB // 2, h=NH)
            link(g_.affine_select(out=v, in_=v, compare_op=ALU.not_equal, fill=1.0, base=0,
                                  pattern=[[-NJ, NB], [0, NH], [-1, NJ]], channel_multiplier=1))
            link(g_.memset(hm[:], 1.0))
            link(g_.affine_select(out=hm[:], in_=hm[:], compare_op=ALU.is_ge, fill=0.0, base=0,
                                  pattern=[[-NS, NB // 2], [-NJ, NH]], channel_multiplier=1))
            g_.affine_select(out=hm[:], in_=hm[:], compare_op=ALU.is_ge, fill=0.0, base=NJ - 1,
                             pattern=[[NS, NB // 2], [NJ, NH]], channel_multiplier=-1).then_inc(pool_const, 1)
            def at_unit(n):
                if n == U["q"] + 1:
                    all_read(pool, "iq", HP)
                    pool.wait_ge(n_t, DC)
                    link(g_.memset(iqbd[:], 0.0))
                    for h in range(2):
                        rows = slice(HD * h, HD * (h + 1))
                        dst = iqbd[rows].rearrange("p b (m h j) -> p b m h j", h=2, j=NJ)[:, :, :, h, :]
                        src = iqT[rows, :, SEQ:T].rearrange("p m (b j) -> p b m j", j=NJ)
                        for m in range(HP):
                            g_.tensor_copy(dst[:, :, m, :], src[:, :, m, :]).then_inc(iqbd_ok, 1)
                        pool.wait_ge(iqbd_ok, HP * (h + 1))
                if n - U["q"] in range(2, 2 + TT - 1):
                    i = n - U["q"] - 1
                    pool.wait_ge(idx_acc, NH * i)
                    causal(score[i][:, P * i:P * (i + 1)], MASKED).then_inc(masked_in, 1)
                if n == U["xr"] - 1:
                    pool.wait_ge(x_saved, 16)
                    for s in range(2):
                        ins = g_.memset(xe[s][:, 0:CW - 1], 0.0)
                        if s:
                            ins.then_inc(bd_zero, 1)
                        else:
                            link(ins)
                if n == FIRST[("gate", 0)] - 1:
                    for c in pool_lowers:
                        norm_lo(1, c)
                if U["ga"] <= n < U["gb"]:
                    for s in (2 * (n - U["ga"]), 2 * (n - U["ga"]) + 1):
                        h, i = s // TT, s % TT
                        w = P * (i + 1)
                        if i == 0:
                            pool.wait_ge(th_in[h % 2], 16 * (h // 2 + 1))
                        if s == 0:
                            pool.wait_ge(mask_ok, TT)
                        if s >= 2:
                            job_read(pool, ("qk", s - 2))
                        m = mask0 if i == 0 else score[i]
                        g_.tensor_tensor(tm[s % 2][:, 0:w], th[h % 2][:, SEQ - w:SEQ], m[:], ALU.add).then_inc(tm_ok, 1)
                if TILES[UNITS[n][0]][0] == "gr" and TILES[UNITS[n][0]][1] >= 1:
                    y_lower(TILES[UNITS[n][0]][1] - 1)
                lower_weights(n + RING)
                if n == U["q"] + HP:
                    pool.wait_ge(ss_copied, 1)
                    job_read(pool, "sidx")
                    own_new_keys(score_s[:, PAST:SK], MASKED).then_inc(masked_in, 1)
                    pool.wait_ge(masked_in, TT)
                if n == U["q"] + HP + 1:
                    all_read(pool, "q", HP)
                    job_read(pool, ("iks", 3))
                    pool.wait_ge(sdots, 1)
                    link(g_.memset(qbd[:], 0.0))
                    for h in range(2):
                        rows = slice(HD * h, HD * (h + 1))
                        for m in range(HP):
                            c0 = NJ * (2 * m + h)
                            g_.tensor_copy(qbd[rows, m, :, c0:c0 + NJ],
                                           qT[rows, m, SEQ:T].rearrange("p (b j) -> p b j", j=NJ)).then_inc(qbd_ok, 1)
                        pool.wait_ge(qbd_ok, HP * (h + 1))
                    job_read(pool, ("idx", NH * (TT - 1) - 1))
                    g_.memset(bd[:], 0.0).then_inc(bd_zero, 1)
                if n == U["k"] + HP - 1:
                    pool.wait_ge(topk_s_ok, 1)
                    own_new_keys(score_s[:, PAST:SK], OFF).then_inc(mask_ok, 1)
                    pool.wait_ge(mask_ok, 1)
                if n == U["ga"] - 3:
                    for i in range(1, TT):
                        pool.wait_ge(topk_ok, i)
                        causal(score[i][:, P * i:P * (i + 1)], OFF).then_inc(mask_ok, 1)
                if n == U["pg"] - 1:
                    for c in pool_lowers:
                        norm_lo(2, c)

            n = 0
            for f0, fn in FFN_HALVES:
                while n < FIRST[("gate", f0)]:
                    at_unit(n)
                    n += 1

                def four_units(it):
                    for u in range(4):
                        if isinstance(it, int):
                            at_unit(n + 4 * it + u)
                        else:
                            lower_weights(n + 4 + u + RING, it - 1)

                ffn_iterations(pool, fn, four_units)
                n += 2 * fn
            while n < len(UNITS):
                at_unit(n)
                n += 1

        @block.tensor
        def _(pe):
            te = nc.tensor

            def start_job(job):
                n = AUX[job]
                if n >= 2:
                    pe.wait_ge(aux_read[n % 2], n // 2)
                return bank(job)

            def end_job(ins):
                return ins.then_inc(aux_done, 1)

            def turn(out, src):
                rows = src.shape[0]
                return te.transpose(out, src, ident[0:rows, 0:rows])

            operands = {"h": (h_hi, h_lo), "y": (act_hi, act_lo), "m": (act_hi, act_lo), "f": (act_hi, act_lo),
                        "p": (p_hi, p_lo)}

            def wait_operand(n, c):
                kind = TILES[UNITS[n][0]][0]
                firsts = (0, FIRST[("gate", 0)], U["pg"])
                if n in firsts:
                    k = firsts.index(n)
                    norm_is_split(pe, k, c)
                elif n == U["ga"] + 1:
                    pe.wait_ge(y_lo, c + 1)
                elif n == U["gb"] + 1:
                    pe.wait_ge(o_lo, c + 1)
                    job_read(pe, "so")
                elif n == U["wo"]:
                    pe.wait_ge(m_lo, c + 1)
                elif n == U["pp"]:
                    job_read(pe, ("p", TT - 1))
                    job_read(pe, ("p", TT))
                elif n in (FIRST[("down", 0, False)], FIRST[("down", 0, False)] + 1):
                    pe.wait_ge(f_lo, c + 1)
                elif n in (FIRST[("down", 0, True)], FIRST[("down", 0, True)] + 1):
                    pe.wait_ge(f_lo, FA + c + 1)

            def run(n, first=True, last=True, it=0):
                t, part, (_, _, rc, _, cc, operand, k0) = UNITS[n]
                parts = len(TILES[t][2])
                s = n % RING
                if first:
                    if part == 0 and t >= 2:
                        pe.wait_ge(tile_read[t % 2], t // 2 + 2 * it)
                    pe.wait_ge(w_lo, n + 1 + 4 * it)
                b0 = 2 * (t % 2)
                if operand == "o":
                    hi, lo = act_hi[:, 8:FA, :], act_lo[:, 8:FA, :]
                else:
                    hi, lo = operands[operand][0][:], operands[operand][1][:]
                for c in range(0 if first else rc // 2, rc if last else rc // 2):
                    wait_operand(n, k0 + c)
                    for w, m in ((whi, hi), (whi, lo), (wlo, hi)):
                        for half in range(2):
                            ins = te.matmul(psD[0:cc, b0 + half, 0:HT], w[:, s, c, 0:cc],
                                            m[:, k0 + c, HT * half:HT * (half + 1)],
                                            start=(part == 0 and c == 0 and w is whi and m is hi),
                                            stop=(part == parts - 1 and c == rc - 1 and w is wlo))
                if last:
                    ins.then_inc(w_used, 1)

            def run_around(n, work):
                run(n, last=False)
                work()
                run(n, first=False)

            def x_chunk(c):
                x_bank = start_job(("x", c))
                if c == 0:
                    for t in range(TT):
                        pe.wait_ge(x_in[t], 16)
                for t in range(TT):
                    ins = turn(x_bank[:, P * t:P * (t + 1)], xtok[:, t, P * c:P * (c + 1)])
                end_job(ins)

            pe.wait_ge(ident_ok, 1)
            pe.wait_ge(prm_in, 16 * 11)
            b = start_job("prm")
            for c in range(DC):
                ins = turn(b[:, NR * c:NR * (c + 1)], prm[:, P * c:P * (c + 1)])
            end_job(ins)
            b = start_job("xs")
            pe.wait_ge(x_in[TT], 16)
            for c in range(DC):
                ins = turn(b[:, NS * c:NS * (c + 1)], xtok[0:NS, TT, P * c:P * (c + 1)])
            end_job(ins)
            for c in range(2):
                x_chunk(c)
            b = start_job("rstd_a")
            pe.wait_ge(ones_ok, 1)
            pe.wait_ge(diag_ok, 2)
            for t in range(TT):
                ins = te.matmul(b[:, P * t:P * (t + 1)], ones[:], diag[:, t, :], start=True, stop=True)
            end_job(ins)
            b = start_job("rstd_b")
            end_job(te.matmul(b[:, 0:NS], ones[0:NS, :], diag[0:NS, TT, 0:NS], start=True, stop=True))
            for c in range(2, DC):
                x_chunk(c)
            run(0)
            for n in range(1, U["ik"]):
                run(n)
            pe.wait_ge(idxp_in, 16 * NB * NPG)
            for n in range(4):
                b = start_job(("iks", n))
                for k in range(4):
                    ins = turn(b[:, P * k:P * (k + 1)], idxp[:, 4 * n + k].rearrange("p r d -> p (r d)"))
                end_job(ins)
            pe.wait_ge(small_in, 32)
            w = LW // 2
            for k, job in enumerate(("lines_a", "lines_b")):
                b = start_job(job)
                end_job(te.matmul(b[0:NH, 0:w], relb[:], onehot[:, w * k:w * (k + 1)], start=True, stop=True))
            b = start_job("selT")
            pe.wait_ge(pool_const, 2)
            for g in range(2):
                ins = turn(b[:, NS * g:NS * (g + 1)], sel[:, g, :])
            end_job(ins)
            run(U["ik"])
            run(U["q"], last=False)
            b = start_job("ik")
            tile_is_read(pe, "ik", 0)
            kw = HD + NH
            for t in range(TT + 1):
                c0, c1 = (P * t, P * (t + 1)) if t < TT else (SEQ, T)
                ins = turn(b[0:c1 - c0, kw * t:kw * (t + 1)], ikw[0:kw, c0:c1])
            end_job(ins)

            def head_rows(h):
                return slice(HD * (h % 2), HD * (h % 2) + HD)

            def index_dots(s):
                i, h = 1 + s // NH, s % NH
                job = ("idx", s)
                b = start_job(job)
                end_job(te.matmul(b[:, 0:P * (i + 1)], iqT[head_rows(h), h // 2, P * i:P * (i + 1)],
                                  ik2[head_rows(h), 0:P * (i + 1)], start=True, stop=True))

            pe.wait_ge(ik_dup, 16)
            for j in range(HP):
                run(U["q"] + j, first=j > 0)
                for s in range(6 * j, 6 * j + 6):
                    index_dots(s)

            pe.wait_ge(iwcol_ok, 1)
            job_read(pe, "selT")
            b = start_job("iwcol")
            for g in range(2):
                ins = te.matmul(b[:, NH * g:NH * (g + 1)], sel[:, g, :], iwtok[0:NS, TT, :], start=True, stop=True)
            end_job(ins)
            pe.wait_ge(iqbd_ok, 2 * HP)
            job_read(pe, ("iks", 2))
            job_read(pe, ("iks", 3))
            for q in range(NB):
                rows = slice(NS * (q % 4), NS * (q % 4) + NS)
                out = psX[2 + q // 4]
                te.matmul(out[rows, 0:PAST], iqbd[:, q, :], iks[:, q, :], start=True, stop=True,
                          tile_position=(0, NS * (q % 4)))
            for g in range(2):
                ins = te.matmul(psX[2 + g][:, PAST:SK], iqbd[:, 4 * g:4 * g + 4, :], ik2[:, SEQ:T],
                                start=True, stop=True)
            ins.then_inc(sdots, 1)
            run(U["k"])
            b = start_job("sidx")
            pe.wait_ge(rs_ok, 2)
            for g in range(2):
                ins = te.matmul(b[0:NS, 0:SK], selT[:, g, :], rs_s[:, g, :], start=(g == 0), stop=(g == 1))
            end_job(ins)
            for n in range(U["k"] + 1, U["v"]):
                run(n)

            def rows_out(kind, src, t):
                c0, c1 = (P * t, P * (t + 1)) if t < TT else (SEQ, T)
                b = start_job((kind, t))
                for m in range(HP):
                    ins = turn(b[0:c1 - c0, P * m:P * (m + 1)], src[:, m, c0:c1])
                end_job(ins)

            def past_turn(q):
                pe.wait_ge(kpg_in[q % 2], 16 * NPG * (q // 2 + 1))
                for g in range(NPG):
                    b = start_job(("kts", q, g))
                    for m in range(HP):
                        ins = turn(b[:, PG * m:PG * (m + 1)], kpg[q % 2][:, g, P * m:P * (m + 1)])
                    end_job(ins)

            def past_logits(q):
                if q == 0:
                    pe.wait_ge(qbd_ok, 2 * HP)
                    for g in range(2):
                        for m in range(HP):
                            te.matmul(psX[2 + g][:, PAST:SK], qbd[:, m, 4 * g:4 * g + 4, :], kT[:, m, SEQ:T],
                                      start=(m == 0), stop=(m == HP - 1))
                job_read(pe, ("kts", q, 0))
                job_read(pe, ("kts", q, 1))
                rows = slice(NS * (q % 4), NS * (q % 4) + NS)
                out = psX[2 + q // 4]
                for m in range(HP):
                    ins = te.matmul(out[rows, 0:PAST], qbd[:, m, q, :], kts[q % 2][:, m, :], start=(m == 0),
                              stop=(m == HP - 1), tile_position=(0, NS * (q % 4)))
                ins.then_inc(slogit_b, 1)

            def k_rows_first():
                all_read(pe, "k", HP)
                rows_out("kout", kT, 0)

            run_around(U["v"], k_rows_first)
            rows_out("kout", kT, 1)
            run_around(U["v"] + 1, lambda: rows_out("kout", kT, 2))
            rows_out("kout", kT, 3)

            def k_rows_last():
                rows_out("kout", kT, TT)
                past_turn(0)

            def past_step(q):
                past_turn(q)
                past_logits(q - 1)

            run_around(U["v"] + 2, k_rows_last)
            past_step(1)
            run_around(U["v"] + 3, lambda: past_step(2))
            past_step(3)
            run_around(U["xr"], lambda: past_step(4))
            past_step(5)
            past_step(6)
            all_read(pe, "v", HP)
            for t in range(TT + 1):
                rows_out("vout", vT, t)
            past_step(7)
            past_logits(7)

            def gate_sums(c, g):
                for k in range(2):
                    b = start_job(("gate", c, g, k))
                    if g == 0 and k == 0:
                        pe.wait_ge(xc_ok, c + 1)
                        if c == 0:
                            pe.wait_ge(bd_in, 64)
                    end_job(te.matmul(b[:, 0:EH], bd[:, c, g, :], xc[c % 2][:, EH * k:EH * (k + 1)],
                                      start=True, stop=True))

            def new_values(g):
                te.matmul(psX[2 + g][:], ptn[:, g, :], vtok_s[:], start=True, stop=False)

            def past_values(q):
                pe.wait_ge(kpg_in[q % 2], 16 * NPG * (NB // 2 + q // 2 + 1))
                g, r = q // 4, q % 4
                rows = slice(NS * r, NS * (r + 1))
                for k in range(NPG):
                    ins = te.matmul(psX[2 + g][rows, :], pts[:, k, g, rows], kpg[q % 2][:, k, :], start=False,
                                    stop=(k == NPG - 1), tile_position=(0, NS * r))
                ins.then_inc(spv_b, 1)

            def sample_gather():
                b = start_job("so")
                pe.wait_ge(own_ok, 2)
                for m in range(HP):
                    for g in range(2):
                        ins = te.matmul(b[:, NS * m:NS * (m + 1)], own[g][:, P * m:P * (m + 1)], selT2[:, g, :],
                                        start=(g == 0), stop=(g == 1))
                end_job(ins)

            pe.wait_ge(mask_ok, 1)
            for g in range(2):
                b = start_job(("smask", g))
                end_job(te.matmul(b[:, 0:SK], sel[:, g, :], score_s[:, 0:SK], start=True, stop=True))
            run(U["xr"] + 1)
            gate_sums(0, 0)
            gate_sums(0, 1)
            b = start_job("spt")
            pe.wait_ge(sp_ok, 2)
            for kk in range(NPG):
                for g in range(2):
                    ins = turn(b[:, P * (2 * kk + g):P * (2 * kk + g + 1)], ps_s[:, g, PG * kk:PG * (kk + 1)])
            end_job(ins)
            b = start_job("spn")
            for g in range(2):
                ins = turn(b[0:NS, P * g:P * (g + 1)], ps_s[:, g, PAST:SK])
            end_job(ins)
            run(U["xr"] + 2)
            job_read(pe, "spt")
            job_read(pe, "spn")
            job_read(pe, ("vout", TT))
            new_values(0)
            new_values(1)
            past_values(0)
            for c in range(1, DC):
                n = U["xr"] + 1 + 2 * c
                run_around(n, lambda: gate_sums(c, 0))
                gate_sums(c, 1)
                if c == SO_CHUNK:
                    sample_gather()
                if 2 * c - 1 < NB:
                    past_values(2 * c - 1)
                if c + 1 < DC:
                    run(n + 1)
                if 2 * c < NB:
                    past_values(2 * c)

            def attend_products(s):
                h, i = s // TT, s % TT
                w = P * (i + 1)
                b = start_job(("qk", s))
                end_job(te.matmul(b[:, 0:w], qT[head_rows(h), h // 2, P * i:w], kT[head_rows(h), h // 2, 0:w],
                                  start=True, stop=True))

            def attend_turn(s):
                i = s % TT
                pe.wait_ge(p_ok, s + 1)
                if s == 0:
                    job_read(pe, "so")
                else:
                    pe.wait_ge(pT_ok, s)
                for k in range(i + 1):
                    ins = turn(psX[2][:, P * k:P * (k + 1)], pr[s % 3][:, P * k:P * (k + 1)])
                ins.then_inc(tr_done, 1)

            def attend_values(s):
                h, i = s // TT, s % TT
                pe.wait_ge(pT_ok, s + 1)
                if s == 0:
                    job_read(pe, ("smask", 1))
                elif s % (2 * TT) == 0:
                    pe.wait_ge(o_lo, s // (2 * TT))
                for k in range(i + 1):
                    ins = te.matmul(psX[3][head_rows(h), P * i:P * (i + 1)], vtok[:, k, HD * h:HD * (h + 1)],
                                    pT[s % 2][:, k, :], start=(k == 0), stop=(k == i),
                                    tile_position=(0, HD * (h % 2)))
                ins.then_inc(pv_done, 1)

            def attend(s):
                if s < STEPS:
                    attend_products(s)
                if 2 <= s < STEPS + 2:
                    attend_turn(s - 2)
                if 3 <= s:
                    attend_values(s - 3)

            for n in range(U["ga"], U["gb"]):
                s = 2 * (n - U["ga"])
                run_around(n, lambda: attend(s))
                attend(s + 1)
                if n == U["ga"] + 1:
                    for k, job in enumerate(("st_a", "st_b")):
                        b = start_job(job)
                        for c in range(4):
                            ins = turn(b[0:NC, P * c:P * (c + 1)], stO[:, 4 * k + c, :])
                        end_job(ins)
            run_around(U["gb"], lambda: attend(STEPS))
            attend(STEPS + 1)
            attend(STEPS + 2)

            for n in range(U["gb"] + 1, U["wo"]):
                run(n)
                k = n - U["gb"]
                if k >= 2 and k % 2 == 0 and k // 2 - 1 <= TT:
                    t = k // 2 - 1
                    c0, c1 = (P * t, P * (t + 1)) if t < TT else (SEQ, T)
                    w = c1 - c0
                    b = start_job(("p", t))
                    pe.wait_ge(p_in, 32)
                    for kk in range(2):
                        ins = turn(b[:, w * kk:w * (kk + 1)], ptok[0:w, t, P * kk:P * (kk + 1)])
                    end_job(ins)

            def sum_squares(k):
                b = start_job(("ss", k))
                pe.wait_ge(sqacc_ok, DC * k)
                for t in range(TT + 1):
                    c0, c1 = (P * t, P * (t + 1)) if t < TT else (SEQ, T)
                    ins = te.matmul(b[0:c1 - c0, t:t + 1], sqacc[:, c0:c1], ones[:, 0:1], start=True, stop=True)
                end_job(ins)

            def spread_factors(k):
                pe.wait_ge(spread_ok, k)
                for t in range(TT + 1):
                    rows = P if t < TT else NS
                    for half in range(2):
                        c0, c1 = max(P * t, HT * half), min(P * t + rows, HT * (half + 1))
                        if c0 < c1:
                            ins = te.matmul(held[:, half, c0 - HT * half:c1 - HT * half], ones[0:rows, :],
                                            spread[0:rows, t, c0 - P * t:c1 - P * t], start=True, stop=True)
                ins.then_inc(rb_ok, 1)

            for n in range(U["wo"], U["pp"] + 2):
                run(n)
            sum_squares(1)
            run(U["pp"] + 2)
            run(U["pp"] + 3)
            spread_factors(1)
            n = U["pp"] + 4
            for f0, fn in FFN_HALVES:
                while n < FIRST[("gate", f0)]:
                    run(n)
                    n += 1

                def gate_and_up(it):
                    for u in range(4):
                        if isinstance(it, int):
                            run(n + 4 * it + u)
                        else:
                            run(n + 4 + u, it=it - 1)

                ffn_iterations(pe, fn, gate_and_up)
                n += 2 * fn
            while n < U["pp2"] + 2:
                run(n)
                n += 1
            sum_squares(2)
            for n in range(U["pp2"] + 2, U["pg"]):
                run(n)
            spread_factors(2)

            def turn_back(i):
                t, half = y_order[i]
                c0, c1 = (P * t, P * (t + 1)) if t < TT else (SEQ, T)
                for c in range(4):
                    ins = turn(y_bank[i][0:c1 - c0, P * c:P * (c + 1)], pp[:, 4 * half + c, c0:c1])
                ins.then_inc(y_turned, 1)

            for n in range(U["pg"], len(UNITS)):
                run(n)
            pe.wait_ge(xf_ok, DC // 2)
            for i in range(TT):
                if i == 2:
                    t = len(TILES) - 2
                    pe.wait_ge(tile_read[t % 2], t // 2 + 1)
                turn_back(i)
            sum_squares(3)
            pe.wait_ge(xf_ok, DC)
            for i in range(TT, len(y_order)):
                if i == 4:
                    t = len(TILES) - 1
                    pe.wait_ge(tile_read[t % 2], t // 2 + 1)
                elif i == 7:
                    job_read(pe, ("ss", 3))
                elif i >= 8:
                    pe.wait_ge(y_half[0], i - 7)
                turn_back(i)


_INS = ["x_prompt", "x_sample", "p_prompt", "p_sample", "cache_k", "cache_v", "cache_idx_k", "state_rglru_h",
        "state_conv", "page_table", "rel_bias", "norm_mix", "w_in", "conv_w", "conv_b", "w_rg_a", "b_rg_a",
        "w_rg_x", "b_rg_x", "lru_lambda", "w_rnn_out", "w_att_out", "w_o", "norm_ffn", "w_ffn_gate", "w_ffn_up",
        "w_ffn_down", "norm_ple", "w_ple_gate", "w_ple_proj", "norm_final"]
_OUTS = [("y_prompt", (1, SEQ, D)), ("y_sample", (NB, NJ, D)), ("k_prompt", (1, 1, SEQ, NH, HD)),
         ("v_prompt", (1, 1, SEQ, NH, HD)), ("idx_k_prompt", (1, 1, SEQ, HD)), ("h_prompt", (1, 1, D)),
         ("conv_prompt", (1, 1, CW - 1, D)), ("k_sample", (1, NB, NJ, NH, HD)), ("v_sample", (1, NB, NJ, NH, HD)),
         ("idx_k_sample", (1, NB, NJ, HD)), ("h_sample", (1, NB, D)), ("conv_sample", (1, NB, CW - 1, D))]


def kernel(**inputs):
    import numpy as _np
    import concourse.bacc as _bacc
    from concourse import mybir as _mybir
    from concourse.bass_utils import run_bass_kernel_spmd as _run

    nc = _bacc.Bacc("TRN2", target_bir_lowering=False, num_devices=1)
    arrays, ins, outs = {}, {}, {}
    held = {name: _np.ascontiguousarray(inputs[name]) for name in _INS}
    held["bias_onehot"] = bias_onehot()
    for name, array in held.items():
        arrays[f"in_{name}"] = array
        ins[name] = nc.dram_tensor(f"in_{name}", array.shape, _mybir.dt.from_np(array.dtype),
                                   kind="ExternalInput").ap()
    for name, shape in _OUTS:
        outs[name] = nc.dram_tensor(f"out_{name}", shape, _mybir.dt.float32, kind="ExternalOutput").ap()
    hybrid_decoder_step(nc, ins, outs)
    r = _run(nc, [arrays], core_ids=[0])
    return tuple(r.results[0][f"out_{name}"] for name, _ in _OUTS)
```
